# Optimizing a Trainium2 kernel written in Bass

```python
import numpy as np
import jax
import jax.numpy as jnp
from jax import lax
import math
import jax, jax.numpy as jnp

D_MODEL = 1024
BATCH = 1
SEQ = 512
DEPTH = 1

POOL_WINDOWS = (2, 4, 8, 16)
POOL_GROUPS = len(POOL_WINDOWS)
POOL_GROUP_W = 128
POOL_W = POOL_GROUPS * POOL_GROUP_W
N_HEADS = 8
HEAD_DIM = 64
N_KV_GROUPS = 2
HEADS_PER_GROUP = N_HEADS // N_KV_GROUPS
ATTN_W = N_HEADS * HEAD_DIM
KV_W = N_KV_GROUPS * HEAD_DIM
N_KV_SLOTS = 6
N_NSA_BRANCHES = 3
CMP_BLOCK = 32
CMP_STRIDE = 16
CMP_HIDDEN = 128
SEL_BLOCK = 64
N_SELECT = 16
WINDOW = 512
QUERY_CHUNK = 16
ROPE_THETA = 500000.0
ROT_DIM = HEAD_DIM // 4
N_MERGE = 2
D_FF = 2816
CONV_WIDTH = 3
IN_W = POOL_W + ATTN_W + N_KV_SLOTS * KV_W + N_HEADS * N_NSA_BRANCHES + N_MERGE * D_MODEL
RMS_EPS = 1e-6
NEG_INF = -1e30
SEL_FORCE = 1e9


def rms_norm(x, g):
    xf = x.astype(jnp.float32)
    y = xf * lax.rsqrt(jnp.mean(xf * xf, axis=-1, keepdims=True) + RMS_EPS)
    return (y * g.astype(jnp.float32)).astype(x.dtype)

def partial_rope(x, pos):
    half = ROT_DIM // 2
    inv = ROPE_THETA ** (-(jnp.arange(half, dtype=jnp.float32) * 2.0 / ROT_DIM))
    ang = pos.astype(jnp.float32)[:, :, None, None] * inv
    cos, sin = jnp.cos(ang), jnp.sin(ang)
    xf = x.astype(jnp.float32)
    x1, x2 = xf[..., :half], xf[..., half:ROT_DIM]
    rot = jnp.concatenate([x1 * cos - x2 * sin, x2 * cos + x1 * sin], axis=-1).astype(x.dtype)
    return jnp.concatenate([rot, x[..., ROT_DIM:]], axis=-1)

def masked_softmax(s, mask, axis):
    s = jnp.where(mask, s.astype(jnp.float32), NEG_INF)
    p = jax.nn.softmax(s, axis=axis)
    return jnp.where(mask, p, 0.0)

def pooling_mixer(u, pool_w, pool_scale):
    S = u.shape[1]
    uf = u.astype(jnp.float32)
    cs = jnp.cumsum(uf, axis=1)
    count = jnp.arange(S, dtype=jnp.float32) + 1.0
    outs = []
    for gi, w in enumerate(POOL_WINDOWS):
        sl = slice(gi * POOL_GROUP_W, (gi + 1) * POOL_GROUP_W)
        c = cs[..., sl]
        lag = jnp.pad(c[:, :S - w], ((0, 0), (w, 0), (0, 0)))
        mean = (c - lag) / jnp.minimum(count, float(w))[None, :, None]
        pooled = (mean - uf[..., sl]).astype(u.dtype)
        outs.append(pooled @ pool_w[gi])
    return jnp.concatenate(outs, axis=-1) * pool_scale

def compress_blocks(kv, pe, w1, w2, idx):
    blk = kv[:, idx] + pe[None, None, :, None, :]
    hid = jax.nn.silu(jnp.einsum('bnlgd,ldh->bngh', blk, w1))
    return jnp.einsum('bngh,hd->bngd', hid, w2)

def nsa_mixer(q, k_cmp, v_cmp, k_sel, v_sel, k_win, v_win, gates, positions,
              q_norm_g, k_norm_g, cmp_pe, cmp_w1, cmp_w2):
    B, S = q.shape[0], q.shape[1]
    G, R, dh = N_KV_GROUPS, HEADS_PER_GROUP, HEAD_DIM
    scale = HEAD_DIM ** -0.5
    q = partial_rope(rms_norm(q, q_norm_g), positions)

    n_cmp = (S - CMP_BLOCK) // CMP_STRIDE + 1
    cmp_idx = np.arange(n_cmp)[:, None] * CMP_STRIDE + np.arange(CMP_BLOCK)[None, :]
    cmp_end = jnp.asarray(cmp_idx[:, -1], dtype=jnp.int32)
    kc = compress_blocks(k_cmp, cmp_pe[0], cmp_w1[0], cmp_w2[0], cmp_idx)
    vc = compress_blocks(v_cmp, cmp_pe[1], cmp_w1[1], cmp_w2[1], cmp_idx)
    kc = partial_rope(rms_norm(kc, k_norm_g[0]), positions[:, cmp_idx[:, -1]])

    n_sel = S // SEL_BLOCK
    k_top = min(N_SELECT, n_sel)
    ks = partial_rope(rms_norm(k_sel, k_norm_g[1]), positions)
    ks_blocks = ks.reshape(B, n_sel, SEL_BLOCK, G, dh).transpose(0, 3, 1, 2, 4)
    vs_blocks = v_sel.reshape(B, n_sel, SEL_BLOCK, G, dh).transpose(0, 3, 1, 2, 4)
    sel_start = np.arange(n_sel)[:, None] * SEL_BLOCK
    cmp_start = np.arange(n_cmp)[None, :] * CMP_STRIDE
    ov = np.clip(np.minimum(sel_start + SEL_BLOCK, cmp_start + CMP_BLOCK)
                 - np.maximum(sel_start, cmp_start), 0, None) / CMP_BLOCK
    overlap = jnp.asarray(ov, dtype=jnp.float32)
    gather_blocks = jax.vmap(jax.vmap(lambda blocks, i: blocks[i]))

    kw = partial_rope(rms_norm(k_win, k_norm_g[2]), positions)
    kw_pad = jnp.pad(kw, ((0, 0), (WINDOW, 0), (0, 0), (0, 0)))
    vw_pad = jnp.pad(v_win, ((0, 0), (WINDOW, 0), (0, 0), (0, 0)))

    n_chunks = S // QUERY_CHUNK
    q_ch = q.reshape(B, n_chunks, QUERY_CHUNK, G, R, dh).swapaxes(0, 1)
    g_ch = gates.reshape(B, n_chunks, QUERY_CHUNK, G, R, N_NSA_BRANCHES).swapaxes(0, 1)
    j_blk = jnp.arange(n_sel)
    tok_off = jnp.arange(SEL_BLOCK)
    win_off = jnp.arange(WINDOW + QUERY_CHUNK)

    def chunk(args):
        c, qc, gc = args
        t = c * QUERY_CHUNK + jnp.arange(QUERY_CHUNK)
        s = jnp.einsum('bqgrd,bngd->bgrqn', qc, kc) * scale
        p_cmp = masked_softmax(s, cmp_end[None, :] <= t[:, None], -1)
        o_cmp = jnp.einsum('bgrqn,bngd->bqgrd', p_cmp.astype(vc.dtype), vc)
        imp = jnp.einsum('bgrqn,jn->bgqj', p_cmp, overlap)
        cur = t // SEL_BLOCK
        forced = (j_blk[None, :] == 0) | (j_blk[None, :] == cur[:, None]) | (j_blk[None, :] == cur[:, None] - 1)
        future = j_blk[None, :] * SEL_BLOCK > t[:, None]
        imp = jnp.where(forced, SEL_FORCE, jnp.where(future, NEG_INF, imp))
        _, top = lax.top_k(imp, k_top)
        ksel = gather_blocks(ks_blocks, top)
        vsel = gather_blocks(vs_blocks, top)
        tok = top[..., None] * SEL_BLOCK + tok_off
        m_sel = (tok <= t[None, None, :, None, None])[:, :, None]
        s = jnp.einsum('bqgrd,bgqkld->bgrqkl', qc, ksel) * scale
        p = masked_softmax(s, m_sel, (-2, -1))
        o_sel = jnp.einsum('bgrqkl,bgqkld->bqgrd', p.astype(vsel.dtype), vsel)
        kwc = lax.dynamic_slice_in_dim(kw_pad, c * QUERY_CHUNK, WINDOW + QUERY_CHUNK, axis=1)
        vwc = lax.dynamic_slice_in_dim(vw_pad, c * QUERY_CHUNK, WINDOW + QUERY_CHUNK, axis=1)
        kpos = c * QUERY_CHUNK - WINDOW + win_off
        m_win = (kpos[None, :] >= 0) & (kpos[None, :] <= t[:, None]) & (t[:, None] - kpos[None, :] < WINDOW)
        s = jnp.einsum('bqgrd,bkgd->bgrqk', qc, kwc) * scale
        p = masked_softmax(s, m_win, -1)
        o_win = jnp.einsum('bgrqk,bkgd->bqgrd', p.astype(vwc.dtype), vwc)
        return gc[..., 0:1] * o_cmp + gc[..., 1:2] * o_sel + gc[..., 2:3] * o_win

    out = lax.map(chunk, (jnp.arange(n_chunks), q_ch, g_ch))
    return out.swapaxes(0, 1).reshape(B, S, ATTN_W)

def causal_dwconv(x, w, b):
    C = x.shape[-1]
    y = lax.conv_general_dilated(x, w[:, None, :].astype(x.dtype), window_strides=(1,),
                                 padding=[(CONV_WIDTH - 1, 0)],
                                 dimension_numbers=('NWC', 'WIO', 'NWC'),
                                 feature_group_count=C)
    return y + b

def first_inputs(seed: int = 0) -> dict:
    key = jax.random.key(seed)
    ks = jax.random.split(key, 20)
    f32 = jnp.float32

    def nrm(k, shape, s):
        return jax.random.normal(k, shape, f32) * s

    x = jax.random.normal(ks[0], (BATCH, SEQ, D_MODEL), f32)
    offsets = jax.random.randint(ks[1], (BATCH, 1), 0, 4096, dtype=jnp.int32)
    positions = (jnp.arange(SEQ, dtype=jnp.int32)[None, :] + offsets).astype(jnp.int32)
    return {
        "x": x,
        "positions": positions,
        "mix_norm_g": 1.0 + nrm(ks[2], (DEPTH, D_MODEL), 0.05),
        "w_in": nrm(ks[3], (DEPTH, D_MODEL, IN_W), D_MODEL ** -0.5),
        "q_norm_g": 1.0 + nrm(ks[4], (DEPTH, HEAD_DIM), 0.05),
        "k_norm_g": 1.0 + nrm(ks[5], (DEPTH, 3, HEAD_DIM), 0.05),
        "cmp_pe": nrm(ks[6], (DEPTH, 2, CMP_BLOCK, HEAD_DIM), 0.1),
        "cmp_w1": nrm(ks[7], (DEPTH, 2, CMP_BLOCK, HEAD_DIM, CMP_HIDDEN), (CMP_BLOCK * HEAD_DIM) ** -0.5),
        "cmp_w2": nrm(ks[8], (DEPTH, 2, CMP_HIDDEN, HEAD_DIM), CMP_HIDDEN ** -0.5),
        "pool_w": nrm(ks[9], (DEPTH, POOL_GROUPS, POOL_GROUP_W, POOL_GROUP_W), POOL_GROUP_W ** -0.5),
        "pool_scale": 1.0 + nrm(ks[10], (DEPTH, POOL_W), 0.1),
        "w_pool_out": nrm(ks[11], (DEPTH, POOL_W, D_MODEL), POOL_W ** -0.5),
        "w_nsa_out": nrm(ks[12], (DEPTH, ATTN_W, D_MODEL), ATTN_W ** -0.5),
        "w_out": nrm(ks[13], (DEPTH, D_MODEL, D_MODEL), D_MODEL ** -0.5),
        "ffn_norm_g": 1.0 + nrm(ks[14], (DEPTH, D_MODEL), 0.05),
        "w_up": nrm(ks[15], (DEPTH, D_MODEL, 2 * D_FF), D_MODEL ** -0.5),
        "conv_w": nrm(ks[16], (DEPTH, CONV_WIDTH, D_FF), CONV_WIDTH ** -0.5),
        "conv_b": nrm(ks[17], (DEPTH, D_FF), 0.01),
        "w_down": nrm(ks[18], (DEPTH, D_FF, D_MODEL), D_FF ** -0.5),
    }

def first_block(x, positions, mix_norm_g, w_in, q_norm_g, k_norm_g, cmp_pe, cmp_w1, cmp_w2,
              pool_w, pool_scale, w_pool_out, w_nsa_out, w_out, ffn_norm_g, w_up, conv_w,
              conv_b, w_down):
    B, S = x.shape[0], x.shape[1]
    split_at = [POOL_W, POOL_W + ATTN_W, POOL_W + ATTN_W + N_KV_SLOTS * KV_W,
                POOL_W + ATTN_W + N_KV_SLOTS * KV_W + N_HEADS * N_NSA_BRANCHES]
    for l in range(DEPTH):
        h = rms_norm(x, mix_norm_g[l])
        proj = h @ w_in[l]
        u, q, kv, nsa_g, merge_g = jnp.split(proj, split_at, axis=-1)
        q = q.reshape(B, S, N_HEADS, HEAD_DIM)
        kv = kv.reshape(B, S, N_KV_SLOTS, N_KV_GROUPS, HEAD_DIM)
        nsa_gates = jax.nn.sigmoid(nsa_g.reshape(B, S, N_HEADS, N_NSA_BRANCHES))
        gate_pool, gate_nsa = jnp.split(jax.nn.sigmoid(merge_g), N_MERGE, axis=-1)
        y_pool = pooling_mixer(u, pool_w[l], pool_scale[l]) @ w_pool_out[l]
        y_nsa = nsa_mixer(q, kv[:, :, 0], kv[:, :, 1], kv[:, :, 2], kv[:, :, 3], kv[:, :, 4], kv[:, :, 5],
                          nsa_gates, positions, q_norm_g[l], k_norm_g[l], cmp_pe[l], cmp_w1[l],
                          cmp_w2[l]) @ w_nsa_out[l]
        x = x + (gate_pool * y_pool + gate_nsa * y_nsa) @ w_out[l]
        h = rms_norm(x, ffn_norm_g[l])
        gate_pre, val = jnp.split(h @ w_up[l], 2, axis=-1)
        gate_c = causal_dwconv(gate_pre, conv_w[l], conv_b[l])
        x = x + (jax.nn.silu(gate_c) * val) @ w_down[l]
    return x


DEPTH_2 = 2

MIX_WIDTH = D_MODEL
CONV_A_WIDTH = MIX_WIDTH // 4
DIFF_WIDTH = MIX_WIDTH // 2
CONF_WIDTH = MIX_WIDTH - CONV_A_WIDTH - DIFF_WIDTH
N_DIFF_HEADS = 4
DIFF_HEAD_DIM = DIFF_WIDTH // (2 * N_DIFF_HEADS)
DIFF_V_DIM = 2 * DIFF_HEAD_DIM
SHORT_CONV_K = 3
CONF_CONV_K = 31
ROPE_THETA_2 = 10000.0
Q_BLOCK = 128
FFN_HIDDEN = -(-8 * D_MODEL // (3 * 256)) * 256
LN_EPS = 1e-5
IN_SPLITS = [CONV_A_WIDTH, CONV_A_WIDTH, CONV_A_WIDTH,
             DIFF_WIDTH, DIFF_WIDTH, DIFF_WIDTH,
             2 * CONF_WIDTH]
IN_WIDTH = sum(IN_SPLITS)


def rmsnorm(x, g):
    xf = x.astype(jnp.float32)
    y = xf * lax.rsqrt(jnp.mean(xf * xf, axis=-1, keepdims=True) + RMS_EPS)
    return (y * g.astype(jnp.float32)).astype(x.dtype)

def layernorm(x, g, b):
    xf = x.astype(jnp.float32)
    mu = jnp.mean(xf, axis=-1, keepdims=True)
    xc = xf - mu
    y = xc * lax.rsqrt(jnp.mean(xc * xc, axis=-1, keepdims=True) + LN_EPS)
    return (y * g.astype(jnp.float32) + b.astype(jnp.float32)).astype(x.dtype)

def causal_depthwise_conv(x, w):
    k, c = w.shape
    return lax.conv_general_dilated(
        x, w.astype(x.dtype)[:, None, :], window_strides=(1,), padding=((k - 1, 0),),
        dimension_numbers=("NWC", "WIO", "NWC"), feature_group_count=c)

def rope_tables(positions):
    inv_freq = 1.0 / (ROPE_THETA_2 ** (jnp.arange(0, DIFF_HEAD_DIM, 2, dtype=jnp.float32) / DIFF_HEAD_DIM))
    ang = positions.astype(jnp.float32)[..., None] * inv_freq
    return jnp.cos(ang)[:, :, None, None, :], jnp.sin(ang)[:, :, None, None, :]

def apply_rope(x, cos, sin):
    xf = x.astype(jnp.float32)
    x1, x2 = jnp.split(xf, 2, axis=-1)
    out = jnp.concatenate([x1 * cos - x2 * sin, x2 * cos + x1 * sin], axis=-1)
    return out.astype(x.dtype)

def diff_attention(q, k, v, lam):
    b, s, _, h, d = q.shape
    nb = s // Q_BLOCK
    qb = q.reshape(b, nb, Q_BLOCK, 2, h, d).transpose(1, 0, 2, 3, 4, 5)
    key_idx = jnp.arange(s)
    scale = d ** -0.5

    def block(args):
        i, qi = args
        sc = jnp.einsum("bqmhd,bkmhd->bmhqk", qi, k,
                        preferred_element_type=jnp.float32) * scale
        q_idx = i * Q_BLOCK + jnp.arange(Q_BLOCK)
        mask = key_idx[None, :] <= q_idx[:, None]
        p = jax.nn.softmax(jnp.where(mask, sc, -jnp.inf), axis=-1)
        a = p[:, 0] - lam * p[:, 1]
        return jnp.einsum("bhqk,bkhe->bqhe", a.astype(v.dtype), v)

    out = lax.map(block, (jnp.arange(nb), qb))
    return out.transpose(1, 0, 2, 3, 4).reshape(b, s, h, DIFF_V_DIM)

def mixing_layer(h, cos, sin, w_in, short_conv_w, glu_b, conf_dw_w, conf_dw_b,
                 conf_ln_g, conf_ln_b, lam_q1, lam_k1, lam_q2, lam_k2, diff_subln_g,
                 w_out, lam_init):
    b, s, _ = h.shape
    u = jnp.einsum("bsd,de->bse", h, w_in)
    offs = np.cumsum(IN_SPLITS)[:-1].tolist()
    a_b, a_c, a_x, q, k, v, c_in = jnp.split(u, offs, axis=-1)

    y_a = a_b * causal_depthwise_conv(a_c * a_x, short_conv_w)

    q = apply_rope(q.reshape(b, s, 2, N_DIFF_HEADS, DIFF_HEAD_DIM), cos, sin)
    k = apply_rope(k.reshape(b, s, 2, N_DIFF_HEADS, DIFF_HEAD_DIM), cos, sin)
    v = v.reshape(b, s, N_DIFF_HEADS, DIFF_V_DIM)
    lam = (jnp.exp(jnp.sum(lam_q1.astype(jnp.float32) * lam_k1.astype(jnp.float32)))
           - jnp.exp(jnp.sum(lam_q2.astype(jnp.float32) * lam_k2.astype(jnp.float32)))
           + lam_init)
    o = diff_attention(q, k, v, lam)
    o = rmsnorm(o, diff_subln_g) * (1.0 - lam_init)
    y_b = o.reshape(b, s, DIFF_WIDTH)

    c = c_in + glu_b
    c = c[..., :CONF_WIDTH] * jax.nn.sigmoid(c[..., CONF_WIDTH:])
    c = causal_depthwise_conv(c, conf_dw_w) + conf_dw_b
    y_c = jax.nn.silu(layernorm(c, conf_ln_g, conf_ln_b))

    y = jnp.concatenate([y_a, y_b, y_c], axis=-1)
    return jnp.einsum("bse,ed->bsd", y, w_out)

def swiglu(h, w_gate, w_up, w_down):
    g = jnp.einsum("bsd,df->bsf", h, w_gate)
    u = jnp.einsum("bsd,df->bsf", h, w_up)
    return jnp.einsum("bsf,fd->bsd", jax.nn.silu(g) * u, w_down)

def second_inputs(seed: int = 0) -> dict:
    key = jax.random.key(seed)
    ks = iter(jax.random.split(key, 32))
    f32 = jnp.float32

    def nrm(shape, scale):
        return jax.random.normal(next(ks), shape, f32) * scale

    x = jax.random.normal(next(ks), (BATCH, SEQ, D_MODEL), f32)
    offsets = jax.random.randint(next(ks), (BATCH, 1), 0, 1024, dtype=jnp.int32)
    positions = offsets + jnp.arange(SEQ, dtype=jnp.int32)[None, :]
    return {
        "x": x,
        "positions": positions,
        "mix_norm_g": 1.0 + nrm((DEPTH_2, D_MODEL), 0.02),
        "w_in": nrm((DEPTH_2, D_MODEL, IN_WIDTH), D_MODEL ** -0.5),
        "short_conv_w": nrm((DEPTH_2, SHORT_CONV_K, CONV_A_WIDTH), SHORT_CONV_K ** -0.5),
        "glu_b": nrm((DEPTH_2, 2 * CONF_WIDTH), 0.02),
        "conf_dw_w": nrm((DEPTH_2, CONF_CONV_K, CONF_WIDTH), CONF_CONV_K ** -0.5),
        "conf_dw_b": nrm((DEPTH_2, CONF_WIDTH), 0.02),
        "conf_ln_g": 1.0 + nrm((DEPTH_2, CONF_WIDTH), 0.02),
        "conf_ln_b": nrm((DEPTH_2, CONF_WIDTH), 0.02),
        "lam_q1": nrm((DEPTH_2, DIFF_HEAD_DIM), 0.1),
        "lam_k1": nrm((DEPTH_2, DIFF_HEAD_DIM), 0.1),
        "lam_q2": nrm((DEPTH_2, DIFF_HEAD_DIM), 0.1),
        "lam_k2": nrm((DEPTH_2, DIFF_HEAD_DIM), 0.1),
        "diff_subln_g": 1.0 + nrm((DEPTH_2, DIFF_V_DIM), 0.02),
        "w_out": nrm((DEPTH_2, MIX_WIDTH, D_MODEL), MIX_WIDTH ** -0.5),
        "ffn_norm_g": 1.0 + nrm((DEPTH_2, D_MODEL), 0.02),
        "w_gate": nrm((DEPTH_2, D_MODEL, FFN_HIDDEN), D_MODEL ** -0.5),
        "w_up": nrm((DEPTH_2, D_MODEL, FFN_HIDDEN), D_MODEL ** -0.5),
        "w_down": nrm((DEPTH_2, FFN_HIDDEN, D_MODEL), FFN_HIDDEN ** -0.5),
        "final_norm_g": 1.0 + nrm((D_MODEL,), 0.02),
    }

def second_block(x, positions, mix_norm_g, w_in, short_conv_w, glu_b, conf_dw_w, conf_dw_b,
              conf_ln_g, conf_ln_b, lam_q1, lam_k1, lam_q2, lam_k2, diff_subln_g, w_out,
              ffn_norm_g, w_gate, w_up, w_down, final_norm_g):
    cos, sin = rope_tables(positions)
    for l in range(DEPTH_2):
        lam_init = 0.8 - 0.6 * math.exp(-0.3 * l)
        h = rmsnorm(x, mix_norm_g[l])
        x = x + mixing_layer(h, cos, sin, w_in[l], short_conv_w[l], glu_b[l], conf_dw_w[l],
                             conf_dw_b[l], conf_ln_g[l], conf_ln_b[l], lam_q1[l], lam_k1[l],
                             lam_q2[l], lam_k2[l], diff_subln_g[l], w_out[l], lam_init)
        h = rmsnorm(x, ffn_norm_g[l])
        x = x + swiglu(h, w_gate[l], w_up[l], w_down[l])
    return rmsnorm(x, final_norm_g)


def setup_inputs(seed=0):
    out = dict(first_inputs(seed))
    for name, value in second_inputs(seed + 1).items():
        if name != "x":
            out[name + "_2"] = value
    return out


def reference(
    x, positions, mix_norm_g, w_in, q_norm_g, k_norm_g, cmp_pe, cmp_w1, cmp_w2, pool_w,
    pool_scale, w_pool_out, w_nsa_out, w_out, ffn_norm_g, w_up, conv_w, conv_b, w_down,
    positions_2, mix_norm_g_2, w_in_2, short_conv_w_2, glu_b_2, conf_dw_w_2, conf_dw_b_2,
    conf_ln_g_2, conf_ln_b_2, lam_q1_2, lam_k1_2, lam_q2_2, lam_k2_2, diff_subln_g_2, w_out_2,
    ffn_norm_g_2, w_gate_2, w_up_2, w_down_2, final_norm_g_2,
):
    x = first_block(
        x, positions, mix_norm_g, w_in, q_norm_g, k_norm_g, cmp_pe, cmp_w1, cmp_w2, pool_w,
        pool_scale, w_pool_out, w_nsa_out, w_out, ffn_norm_g, w_up, conv_w, conv_b, w_down,
    )
    return second_block(
        x, positions_2, mix_norm_g_2, w_in_2, short_conv_w_2, glu_b_2, conf_dw_w_2, conf_dw_b_2,
        conf_ln_g_2, conf_ln_b_2, lam_q1_2, lam_k1_2, lam_q2_2, lam_k2_2, diff_subln_g_2,
        w_out_2, ffn_norm_g_2, w_gate_2, w_up_2, w_down_2, final_norm_g_2,
    )


_drawn_inputs = setup_inputs


def setup_inputs(seed=0):
    import zlib

    import numpy as np

    out = dict(_drawn_inputs(seed))
    spreads = {}
    factors = {'q_norm_g': 8.0,
     'k_norm_g': 8.0,
     'conv_b': 7.972,
     'glu_b_2': 8.0,
     'conf_dw_b_2': 4.279,
     'conf_ln_g_2': 21.213,
     'conf_ln_b_2': 22.175,
     'lam_k1_2': 5.535,
     'lam_k2_2': 8.0,
     'diff_subln_g_2': 5.237,
     'ffn_norm_g_2': 3.651,
     'final_norm_g_2': 7.992}
    for name, (base, spread) in spreads.items():
        noise = np.random.default_rng([zlib.crc32(name.encode()), seed]).standard_normal(out[name].shape)
        drawn = base * np.exp(spread * noise) if base else spread * noise
        out[name] = jnp.asarray(drawn.astype(out[name].dtype))
    for name, factor in factors.items():
        out[name] = (out[name] * factor).astype(out[name].dtype)
    return out
```

```python
from contextlib import ExitStack

import numpy as np

import concourse.bass as bass
from concourse import mybir

ALU = mybir.AluOpType
ACT = mybir.ActivationFunctionType
AX = mybir.AxisListType
F32 = mybir.dt.float32
F32R = mybir.dt.float32r
BF16 = mybir.dt.bfloat16
I32 = mybir.dt.int32

P = 128
S = 512
NT = S // P
D = 1024
KD = D // P
FF = 2816
KF = FF // P
CB = 8
DOWN_CHUNKS = -(-KF // CB)
N_CMP = (S - 32) // 16 + 1
LAYERS = 2
EPS = 1e-6
LN_EPS = 1e-5
TAPS = 31
MASKED = -1e30

P1 = {}
_at = 0
for _name, _n in (("mix_g", KD), ("q_g", 1), ("cmp_g", 1), ("sel_g", 1), ("win_g", 1), ("pool_scale", 4),
                  ("ffn_g", KD), ("conv_w", 3 * KF), ("conv_b", KF), ("next_g", KD), ("pe_k", 32), ("pe_v", 32)):
    P1[_name] = _at
    _at += _n
NP1 = _at
P2 = {}
_at = 0
for _name, _n in (("short_w", 6), ("glu_b", 4), ("dw_w", 2 * TAPS), ("dw_b", 2), ("ln_g", 2), ("ln_b", 2),
                  ("sub_g", 1), ("ffn_g", KD), ("next_g", KD), ("lam", 4), ("lam_init", 2)):
    P2[_name] = _at
    _at += _n
NP2 = _at
C = {}
_at = 0
for _name, _n in (("ident", P), ("rot1", P), ("rot2", P), ("ones", P), ("halves", 2), ("inv1", 1), ("inv2", 1),
                  ("rcount", 64)):
    C[_name] = _at
    _at += _n
NC = _at

T_IN, N_IN = 15, 15
T_MIX, N_MIX = 3 * KD, 4 * KD
T_OUT = KD
T_UP = 2 * KF
T_DOWN = DOWN_CHUNKS * KD
T_BLOCK1 = T_IN + T_MIX + T_OUT + T_UP + T_DOWN
N_BLOCK1 = N_IN + N_MIX + T_OUT + T_UP + KD
T_LIN = 22
T_LAYER = T_LIN + T_OUT + T_UP + T_DOWN
N_LAYER = T_LIN + T_OUT + T_UP + KD
T_ALL = T_BLOCK1 + LAYERS * T_LAYER
assert T_LAYER % 2 == 0 and N_LAYER % 2 == 0
U_BLOCK1, U_LAYER = 9, 8
NU = 16


class Count:

    def __init__(self, const, terms=()):
        self.const, self.terms = const, tuple(terms)

    def __add__(self, n):
        return Count(self.const + n, self.terms)

    def loop(self, reg, step):
        return Count(self.const, self.terms + ((reg, step),))

    def half(self):
        assert all(s % 2 == 0 for _, s in self.terms)
        return Count(self.const // 2, [(r, s // 2) for r, s in self.terms])

    def even(self):
        assert all(s % 2 == 0 for _, s in self.terms)
        return self.const % 2

    def value(self, times=1):
        v = self.const * times
        for r, s in self.terms:
            v = r * (s * times) + v
        return v

    def low(self):
        return self.const


def wait(eng, sem, count, times=1):
    if count.low() > 0:
        eng.wait_ge(sem, count.value(times))


def build(nc, x, positions, positions2, weights, par1, par2, consts, masks, w1, w2, pool_w, out):
    ctx = ExitStack()
    with ctx:
        base = -(-nc.sbuf_base // 64) * 64
        top = [base]

        def at(name, shape, dt, offset):
            return nc.alloc_sbuf_tensor_at(name, list(shape), dt, offset=offset)

        def sb(name, shape, dt=F32):
            size = int(np.prod(shape[1:])) * (2 if dt == BF16 else 4)
            t = at(name, shape, dt, top[0])
            top[0] += -(-size // 64) * 64
            return t

        def sem(name):
            return ctx.enter_context(nc.semaphore(name))

        xs = sb("xs", [P, KD, S])
        xh = sb("xh", [P, KD, S], F32R)
        xl = sb("xl", [P, KD, S], F32R)
        raw = sb("raw", [P, 4 * CB * P])
        wh = sb("wh", [P, 2, CB * P], F32R)
        wl = sb("wl", [P, 2, CB * P], F32R)
        cst = sb("cst", [P, NC])
        msk = sb("msk", [P, 2 * P + 256], BF16)
        pr1 = sb("pr1", [P, NP1])
        pr2 = sb("pr2", [P, LAYERS * NP2])
        par = sb("par", [P, NP2])
        cos = sb("cos", [P, S])
        sin = sb("sin", [P, S])
        cos2 = sb("cos2", [P, S])
        sin2 = sb("sin2", [P, S])
        rstd = sb("rstd", [P, S])
        sqacc = sb("sqacc", [P, S])
        small = sb("small", [P, 192])
        ybuf = sb("ybuf", [P, 2, S])
        BIG = top[0]
        UNIT = 4 * S

        def big(name, unit, shape, dt=F32):
            size = int(np.prod(shape[1:])) * 4
            assert unit * UNIT + size <= 44 * UNIT, name
            return at(name, shape, dt, BIG + unit * UNIT)

        top[0] = BIG + 44 * UNIT
        sq = sb("sq", [P, 2, S])
        tmp = sb("tmp", [P, 2, S])
        tmp2 = sb("tmp2", [P, 528])
        tmp3 = sb("tmp3", [P, 528])
        small2 = sb("small2", [P, 512])
        pairs = sb("pairs", [P, S])
        assert top[0] <= nc.sbuf_usable_end, (top[0], nc.sbuf_usable_end)

        ident = cst[:, C["ident"]:C["ident"] + P]
        rot1 = cst[:, C["rot1"]:C["rot1"] + P]
        rot2 = cst[:, C["rot2"]:C["rot2"] + P]
        ones = cst[:, C["ones"]:C["ones"] + P]
        one = cst[:, C["ones"]:C["ones"] + 1]
        halves = cst[:, C["halves"]:C["halves"] + 2]
        identb = msk[:, 0:P]
        causal = msk[:, P:2 * P]
        cmp_mask = msk[:, 2 * P:2 * P + 256]

        def c1(name, i=0):
            return pr1[:, P1[name] + i:P1[name] + i + 1]

        def c2(name, i=0):
            return par[:, P2[name] + i:P2[name] + i + 1]

        s_root = small[:, 0:8]
        s_recip = small[:, 8:16]
        q_g8 = small[:, 16:17]
        mx8 = small[:, 24:32]
        sum8 = small[:, 32:40]
        fac8 = small[:, 40:48]
        negmx = small[:, 48:64]
        rows = small[:, 64:80]
        rinv = small[:, 80:96]
        lamp = small[:, 96:98]
        lame = small[:, 98:100]
        neglam = small[:, 100:101]
        negmx2 = small[:, 104:112]
        rows2 = small[:, 112:120]
        rinv2 = small[:, 120:128]
        sub_gain = small[:, 128:129]
        gates_t = small2[:, 0:96].rearrange("p (i c) -> p i c", i=NT)
        vct = small2[0:32, 96:224]
        kcf = small2[:, 224:256]
        vcf = small2[:, 256:288]
        kct = small2[:, 288:320]
        csq = small2[:, 320:352]
        cyn = small2[:, 352:384]
        ctm = small2[:, 384:416]
        hid = small2[:, 416:480].rearrange("p (g n) -> p g n", g=2)

        kvraw = big("kvraw", 0, [P, 2, S])
        kk = big("kk", 2, [P, 2, S])
        vt = big("vt", 4, [P, 2, NT, P])
        qall = big("qall", 6, [P, 4, S])
        qcur = big("qcur", 10, [P, S])
        cmp_p = big("cmp_p", 11, [P, 8, 32])
        cmp_pt = big("cmp_pt", 12, [32, 2, S])
        w2t = big("w2t", 14, [P, 2, P])
        poolw = big("poolw", 15, [P, 4, P])
        w1t = big("w1t", 16, [P, 32, P])
        blk = big("blk", 24, [P, 32, 31])
        probs = big("probs", 16, [P, 4, S])
        pt = big("pt", 20, [P, 2, NT, S])
        poh = big("poh", 28, [P, 4, S], F32R)
        pol = big("pol", 32, [P, 4, S], F32R)
        nh = big("nh", 36, [P, 4, S], F32R)
        nl = big("nl", 40, [P, 4, S], F32R)
        mh = big("mh", 0, [P, KD, S], F32R)
        ml = big("ml", 8, [P, KD, S], F32R)
        hh = big("hh", 0, [P, KF, S], F32R)
        hl = big("hl", KF, [P, KF, S], F32R)
        cpad = big("cpad", 0, [P, 2, TAPS - 1 + S])
        conv = big("conv", 3, [P, 2, S])
        ya = big("ya", 5, [P, 2, S])
        acp = big("acp", 7, [P, 2 + S])
        lv = big("lv", 9, [P, NT, S])
        lq = big("lq", 13, [P, 4, S])
        lk = big("lk", 17, [P, 4, S])
        lqc = big("lqc", 21, [P, S])
        lkc = big("lkc", 22, [P, S])
        lvc = big("lvc", 23, [P, NT, P])
        lp = big("lp", 24, [P, 2, 2, S])
        lpt = big("lpt", 28, [P, NT, S])
        lo_ = big("lo_", 32, [P, 4, S])
        ca = big("ca", 36, [P, 2, S])
        cg = big("cg", 38, [P, 2, S])
        yh = big("yh", 13, [P, KD, S], F32R)
        yl = big("yl", 21, [P, KD, S], F32R)
        posi = big("posi", 0, [P, S], I32)
        posf = big("posf", 1, [P, S])
        ang = big("ang", 2, [P, S])
        turns = big("turns", 3, [P, S])
        red = big("red", 4, [P, S])
        posi2 = big("posi2", 8, [P, S], I32)
        posf2 = big("posf2", 9, [P, S])
        ang2 = big("ang2", 10, [P, S])
        turns2 = big("turns2", 11, [P, S])
        red2 = big("red2", 12, [P, S])

        bank = [ctx.enter_context(nc.psum_tensor(f"bank{i}", [P, S], F32)) for i in range(8)]
        G = bank[0:2]
        ROT, POOLB, TR, STAT, BC, OUT = bank[2], bank[3], bank[4], bank[5], bank[6], bank[7]

        stored = [sem(f"stored{i}") for i in range(2)]
        raw_landed = [sem(f"raw_landed{i}") for i in range(2)]
        x_landed = sem("x_landed")
        par_landed = sem("par_landed")
        pos_landed = sem("pos_landed")
        w1_landed = sem("w1_landed")
        hi_ready = sem("hi_ready")
        lo_ready = sem("lo_ready")
        chunk_done = sem("chunk_done")
        tile_out = sem("tile_out")
        xh_ready = sem("xh_ready")
        xl_ready = sem("xl_ready")
        stat_ready = sem("stat_ready")
        root_ready = sem("root_ready")
        recip_ready = sem("recip_ready")
        bc_ready = sem("bc_ready")
        bc_read = sem("bc_read")
        sq_ready = sem("sq_ready")
        rot_in = sem("rot_in")
        rot_ready = sem("rot_ready")
        rot_read = sem("rot_read")
        tr_ready = sem("tr_ready")
        tr_read = sem("tr_read")
        sine_done = sem("sine_done")
        ready = {n: sem(n) for n in (
            "tables", "blk_ready", "hid_psum", "hid_ready", "cmp_psum", "cmp_copied", "vct_psum", "vct_ready",
            "pool_in", "pool_psum", "pool_hi", "pool_lo",
            "q_cur", "s_psum", "max_ready", "exp_ready", "p_ready", "pt_psum", "pt_ready", "pv_done", "o_psum",
            "o_hi", "o_lo", "c_psum", "c_sub", "c_exp", "c_probs", "c_tpsum", "c_tready",
            "mix_sig", "mix_sum", "mix_hi", "mix_lo",
            "conv_ready", "silu_ready", "prod_ready", "h_hi", "h_lo",
            "lam_in", "lam_psum", "lam_exp", "lam_ready", "glu_sig", "conv_done", "kv_cur",
            "head_ready", "ln_sq", "yc_ready", "y_hi", "y_lo",
            "zeroed", "out_ready", "par_ready")}
        R = ready
        block = ctx.enter_context(nc.Block())

        def cols(start, n):
            return slice(start, start + n) if isinstance(start, int) else bass.ds(start, n)

        def raw_slot(t):
            v = t.value()
            return raw[:, cols((v % 4) * (CB * P), CB * P)]

        t0 = Count(0)

        @block.sync
        def _(sp):
            sp.dma_start(cst[:, :], consts).then_inc(par_landed, 16)
            sp.dma_start(pr1[:, :], par1).then_inc(par_landed, 16)
            sp.dma_start(xs[:, :, :], x).then_inc(x_landed, 16)
            for t in range(2):
                sp.dma_start(raw[:, t * CB * P:(t + 1) * CB * P], weights[t]).then_inc(raw_landed[t], 16)
            sp.dma_start(posi[:, :], positions.partition_broadcast(P)).then_inc(pos_landed, 16)
            sp.dma_start(posi2[:, :], positions2.partition_broadcast(P)).then_inc(pos_landed, 16)
            sp.dma_start(pr2[:, :], par2).then_inc(par_landed, 16)
            sp.dma_start(msk[:, :], masks).then_inc(par_landed, 16)
            sp.dma_start(w2t[:, :, :], w2).then_inc(par_landed, 16)
            sp.dma_start(poolw[:, :, :], pool_w).then_inc(par_landed, 16)
            sp.dma_start(w1t[:, :, :], w1[0]).then_inc(w1_landed, 16)

            def load(t, source):
                sp.wait_ge(raw_landed[t % 2], 16 * (t // 2))
                if t >= 4:
                    sp.wait_ge(lo_ready, t - 3)
                sp.dma_start(raw[:, (t % 4) * CB * P:(t % 4 + 1) * CB * P], weights[source])\
                    .then_inc(raw_landed[t % 2], 16)

            load(2, 2)
            load(3, 3)
            for t in range(4, 20):
                load(t, t)
            sp.wait_ge(R["hid_psum"], 1)
            sp.dma_start(w1t[:, :, :], w1[1]).then_inc(w1_landed, 16)
            trips = (T_ALL - 20) // 4
            with sp.Fori(0, trips) as r:
                for c in range(4):
                    t = Count(20 + c).loop(r, 4)
                    chunk, landed, split = t.value(), t.half().value(16), (t + -3).value()
                    for v in (landed, split, chunk * (P * CB * P) * 4):
                        sp.compute_val(v)
                    src = weights[bass.ds(chunk, 1), :, :].rearrange("o p c -> (o p) c")
                    sp.wait_ge(raw_landed[c % 2], landed)
                    sp.wait_ge(lo_ready, split)
                    sp.dma_start(raw[:, c * CB * P:(c + 1) * CB * P], src).then_inc(raw_landed[c % 2], 16)
            for t in range(20 + 4 * trips, T_ALL + 2):
                load(t, t if t < T_ALL else t - T_ALL)
            for m in range(KD):
                sp.wait_ge(R["out_ready"], m + 1)
                sp.dma_start(out[m], ybuf[:, m % 2, :]).then_inc(stored[m % 2], 16)
            for i in range(2):
                sp.wait_ge(stored[i], 16 * (KD // 2))

        @block.gpsimd
        def _(pool):
            def rest(t):
                v = t.value()
                two = cols((v % 2) * (CB * P), CB * P)
                pool.wait_ge(hi_ready, (t + 1).value())
                pool.tensor_tensor(wl[:, :, :].rearrange("p s n -> p (s n)")[:, two], raw_slot(t),
                                   wh[:, :, :].rearrange("p s n -> p (s n)")[:, two].bitcast(F32),
                                   ALU.subtract).then_inc(lo_ready, 1)

            with pool.Fori(0, T_ALL + 2) as t:
                rest(Count(0).loop(t, 1))

        @block.tensor
        def _(pe):
            mm = pe.matmul

            def tile(t, n, kh, kl, blocks=CB, blk0=0, first=True, last=True, count=True, feed=None, mid=None):
                s, b = t.even(), G[n.even()]
                if first:
                    wait(pe, tile_out, n + -1)
                if blk0 == 0:
                    pe.wait_ge(hi_ready, (t + 1).value())
                for k in range(blocks):
                    if feed is not None:
                        pe.wait_ge(xl_ready, (feed + (k + 1)).value())
                    w = wh[:, s, (blk0 + k) * P:(blk0 + k + 1) * P]
                    mm(b[:, :], w, kh(k), start=first and k == 0, stop=False)
                    mm(b[:, :], w, kl(k), start=False, stop=False)
                if mid is not None:
                    mid()
                if blk0 == 0:
                    pe.wait_ge(lo_ready, (t + 1).value())
                for k in range(blocks):
                    i = mm(b[:, :], wl[:, s, (blk0 + k) * P:(blk0 + k + 1) * P], kh(k),
                           start=False, stop=last and k == blocks - 1)
                if count:
                    i.then_inc(chunk_done, 1)

            def xk(t, n, feed=None, mid=None):
                tile(t, n, lambda k: xh[:, k, :], lambda k: xl[:, k, :], feed=feed, mid=mid)

            def stats(u, src, cols_, n=P, per=1, tiles=NT, start=lambda i: True):
                for i in range(tiles):
                    lists = src(i)
                    for a, s_ in enumerate(lists):
                        x_ = mm(STAT[0:n, per * i:per * (i + 1)], s_, cols_, start=a == 0, stop=a == len(lists) - 1)
                x_.then_inc(stat_ready, 1)

            def spread(u, src, n=P, tiles=NT, width=S):
                pe.wait_ge(recip_ready, (u + 1).value())
                wait(pe, bc_read, u)
                for i in range(tiles):
                    x_ = pe.transpose(BC[:, i * P:i * P + n], src(i), ident[0:n, 0:n])
                x_.then_inc(bc_ready, 1)

            def x_norm(u, feed):
                pe.wait_ge(xl_ready, (feed + KD).value())
                stats(u, lambda i: [sqacc[:, i * P:(i + 1) * P]], one)
                spread(u, lambda i: s_recip[:, i:i + 1].to_broadcast([P, P]))

            pe.wait_ge(par_landed, 16 * 6)
            norm_of = {2: 1, 3: 2, 4: 3, 5: 4, 6: 5, 7: 6}
            rot_of = {n: i for i, n in enumerate((2, 3, 4, 5, 6, 7))}
            tr_of = {8: 0, 9: 1, 10: 2}
            pool_of = {11: 0, 12: 1, 13: 2, 14: 3}

            def head_stats(n):
                u = Count(norm_of[n])
                pe.wait_ge(sq_ready, norm_of[n])
                wait(pe, root_ready, u)
                stats(u, lambda i: [sq[:, 0, i * P:(i + 1) * P]], halves, per=2)

            def head_spread(n):
                spread(Count(norm_of[n]), lambda i: pairs[:, i * P:(i + 1) * P])

            def rotate(n):
                pe.wait_ge(rot_in, rot_of[n] + 1)
                if rot_of[n]:
                    pe.wait_ge(rot_read, rot_of[n])
                mm(ROT[:, :], rot1, tmp[:, rot_of[n] % 2, :], start=True, stop=True).then_inc(rot_ready, 1)

            def turn(n):
                pe.wait_ge(tile_out, n + 1)
                if tr_of[n]:
                    pe.wait_ge(tr_read, tr_of[n])
                for i in range(NT):
                    x_ = pe.transpose(TR[:, i * P:(i + 1) * P], ybuf[:, n % 2, i * P:(i + 1) * P], ident)
                x_.then_inc(tr_ready, 1)

            def pool_mix(g):
                pe.wait_ge(R["pool_in"], g + 1)
                if g:
                    pe.wait_ge(R["pool_lo"], g)
                mm(POOLB[:, :], poolw[:, g, :], tmp[:, g % 2, :], start=True, stop=True).then_inc(R["pool_psum"], 1)

            def after(n):
                if n - 1 in norm_of:
                    head_stats(n - 1)
                if n - 2 in rot_of:
                    rotate(n - 2)
                if n - 1 in tr_of:
                    turn(n - 1)
                if n - 2 in pool_of:
                    pool_mix(pool_of[n - 2])

            for n in range(N_IN):
                xk(Count(n), Count(n), feed=Count(0) if n == 0 else None, mid=lambda: after(n))
                if n == 0:
                    x_norm(Count(0), Count(0))
                if n - 1 in norm_of:
                    head_spread(n - 1)
            pool_mix(2)

            def compress(c):
                pe.wait_ge(w1_landed, 16 * (c + 1))
                pe.wait_ge(R["blk_ready"], c + 1)
                if c:
                    pe.wait_ge(R["hid_ready"], c)
                for g in range(2):
                    for l in range(32):
                        x_ = mm((ROT, BC)[g][:, 0:31], w1t[g * 64:(g + 1) * 64, l, :],
                                blk[g * 64:(g + 1) * 64, l, :], start=l == 0, stop=l == 31)
                x_.then_inc(R["hid_psum"], 1)

            def compress_out(c):
                pe.wait_ge(R["hid_ready"], c + 1)
                if c:
                    pe.wait_ge(R["cmp_copied"], c)
                mm(TR[:, 0:62].rearrange("p (g n) -> p g n", g=2), w2t[:, c, :], hid[:, :, 0:31],
                   start=True, stop=True).then_inc(R["cmp_psum"], 1)

            pe.wait_ge(rot_read, 6)
            pe.wait_ge(tr_read, 3)
            pe.wait_ge(bc_read, 7)
            compress(0)
            pool_mix(3)
            compress_out(0)
            compress(1)
            compress_out(1)
            pe.wait_ge(sq_ready, 7)
            mm(STAT[0:32, 0:2], csq, halves, start=True, stop=True).then_inc(stat_ready, 1)
            pe.wait_ge(recip_ready, 8)
            pe.transpose(BC[:, 0:32], pairs[0:32, 0:P],
                         ident[0:32, 0:32]).then_inc(bc_ready, 1)
            pe.wait_ge(R["cmp_copied"], 2)
            pe.transpose(TR[0:32, 0:P], vcf, ident).then_inc(R["vct_psum"], 1)
            pe.wait_ge(rot_in, 7)
            mm(ROT[:, 0:32], rot1, cyn, start=True, stop=True).then_inc(rot_ready, 1)
            pe.wait_ge(R["vct_ready"], 1)
            pe.wait_ge(rot_read, 7)

            SB = [G[0], G[1], ROT, POOLB]
            TB = [STAT, BC]
            pe.wait_ge(tile_out, N_IN)
            pe.wait_ge(R["pool_lo"], 4)
            with pe.Fori(0, 4) as j:
                U = Count(0).loop(j, NU)
                J = Count(0).loop(j, 1)
                B4 = Count(0).loop(j, 4)
                pe.wait_ge(R["q_cur"], (J + 1).value())
                for g in range(2):
                    s = (TR, OUT)[g]
                    mm(s[:, 0:P], identb, cmp_mask[:, g * P:(g + 1) * P], start=True, stop=False)
                    for i in range(NT):
                        x_ = mm(s[:, i * 32:(i + 1) * 32], qcur[g * 64:(g + 1) * 64, i * P:(i + 1) * P],
                                kct[g * 64:(g + 1) * 64, :], start=False, stop=i == 3)
                x_.then_inc(R["c_psum"], 1)

                def score(u):
                    g, b, i = u // 8, u // 4 % 2, u % 4
                    pe.wait_ge(R["exp_ready"], (U + (u - 3)).value()) if u >= 4 else None
                    s = SB[u % 4]
                    n = (i + 1) * P
                    mm(s[:, 0:n], qcur[g * 64:(g + 1) * 64, i * P:(i + 1) * P], kk[g * 64:(g + 1) * 64, b, 0:n],
                       start=True, stop=False)
                    mm(s[:, i * P:n], identb, causal, start=False, stop=True).then_inc(R["s_psum"], 1)

                def turn_probs(u):
                    i = u % 4
                    pe.wait_ge(R["p_ready"], (U + (u + 1)).value())
                    if u >= 2:
                        pe.wait_ge(R["pt_ready"], (U + (u - 1)).value())
                    for c in range(i + 1):
                        x_ = pe.transpose(TB[u % 2][:, c * P:(c + 1) * P], probs[:, u % 4, c * P:(c + 1) * P], ident)
                    x_.then_inc(R["pt_psum"], 1)

                def values(w):
                    g, b = w // 2, w % 2
                    pe.wait_ge(R["pt_ready"], (U + (4 * w + 4)).value())
                    for c in range(NT):
                        x_ = mm(OUT[g * 64:(g + 1) * 64, c * P:S], vt[:, b, c, g * 64:(g + 1) * 64],
                                pt[:, w % 2, c, c * P:S], start=b == 0 and c == 0, stop=False)
                    x_.then_inc(R["pv_done"], 1)

                score(0)
                score(1)
                score(2)
                for u in range(NU):
                    if u + 3 < NU:
                        score(u + 3)
                    turn_probs(u)
                    if u == 3:
                        pe.wait_ge(R["c_probs"], (J + 1).value())
                        for g in range(2):
                            for i in range(NT):
                                x_ = pe.transpose(TR[0:32, i * P:(i + 1) * P], cmp_p[:, g * NT + i, :], ident)
                            x_.then_inc(R["c_tpsum"], 1)
                            if g == 0:
                                pe.wait_ge(R["c_tready"], Count(1).loop(j, 2).value())
                    if u % 4 == 0 and u:
                        values(u // 4 - 1)
                        if u == 8:
                            pe.wait_ge(R["c_tready"], Count(2).loop(j, 2).value())
                            mm(OUT[0:64, :], vct[:, 0:64], cmp_pt[:, 0, :], start=False, stop=True)
                values(3)
                mm(OUT[64:P, :], vct[:, 64:P], cmp_pt[:, 1, :], start=False, stop=True).then_inc(R["o_psum"], 1)
                pe.wait_ge(R["o_lo"], (J + 1).value())

            tb, nb = Count(T_IN), Count(N_IN)
            with pe.Fori(0, KD // 2) as r:
                for m in range(2):
                    t, n = (tb + 3 * m).loop(r, 6), (nb + 4 * m).loop(r, 8)
                    xk(t, n)
                    xk(t + 1, n + 1)
                    tile(t + 2, n + 2, lambda k: poh[:, k, :], lambda k: pol[:, k, :], blocks=4, count=False)
                    tile(t + 2, n + 3, lambda k: nh[:, k, :], lambda k: nl[:, k, :], blocks=4, blk0=4)

            def out_and_ffn(tb, nb, ysrc, y_ready, u, feed):
                with pe.Fori(0, KD // 2) as r:
                    pe.wait_ge(y_ready[0], y_ready[1].value())
                    for m in range(2):
                        tile((tb + m).loop(r, 2), (nb + m).loop(r, 2), lambda k: ysrc[0][:, k, :],
                             lambda k: ysrc[1][:, k, :])
                tb, nb = tb + T_OUT, nb + KD
                xk(tb, nb, feed=feed)
                x_norm(u, feed)
                xk(tb + 1, nb + 1)
                with pe.Fori(0, KF - 1) as r:
                    xk((tb + 2).loop(r, 2), (nb + 2).loop(r, 2))
                    xk((tb + 3).loop(r, 2), (nb + 3).loop(r, 2))
                tb, nb = tb + T_UP, nb + T_UP
                return tb, nb

            def down(tb, nb, h_lo):
                with pe.Fori(0, KD // 2) as r:
                    pe.wait_ge(R["h_lo"], h_lo.value())
                    for m in range(2):
                        for c in range(DOWN_CHUNKS):
                            k0 = CB * c
                            tile((tb + (DOWN_CHUNKS * m + c)).loop(r, 2 * DOWN_CHUNKS), (nb + m).loop(r, 2),
                                 lambda k: hh[:, k0 + k, :], lambda k: hl[:, k0 + k, :],
                                 blocks=min(CB, KF - k0), first=c == 0, last=c == DOWN_CHUNKS - 1)

            tb, nb = out_and_ffn(Count(T_IN + T_MIX), Count(N_IN + N_MIX), (mh, ml), (R["mix_lo"], Count(KD)),
                                 Count(8), Count(KD))
            down(tb, nb, Count(KF))

            with pe.Fori(0, LAYERS) as l:
                T = Count(T_BLOCK1).loop(l, T_LAYER)
                N = Count(N_BLOCK1).loop(l, N_LAYER)
                U0 = Count(U_BLOCK1).loop(l, U_LAYER)
                feed = Count(2 * KD).loop(l, 2 * KD)
                L1 = Count(1).loop(l, 1)

                def lam_sum():
                    pe.wait_ge(R["lam_in"], L1.value())
                    mm(POOLB[:, 0:2], ones, lamp, start=True, stop=True).then_inc(R["lam_psum"], 1)

                TRL = Count(3).loop(l, 4)

                def turn_v(i):
                    pe.wait_ge(tile_out, (N + (10 + i + 1)).value())
                    pe.wait_ge(tr_read, (TRL + i).value())
                    for c in range(NT):
                        x_ = pe.transpose(TR[:, c * P:(c + 1) * P], ybuf[:, (10 + i) % 2, c * P:(c + 1) * P], ident)
                    x_.then_inc(tr_ready, 1)

                RO = Count(7).loop(l, 8)

                def rotate_l(i):
                    pe.wait_ge(tile_out, (N + (14 + i + 1)).value())
                    pe.wait_ge(rot_read, (RO + i).value())
                    mm(ROT[:, :], rot2, ybuf[:, (14 + i) % 2, :], start=True, stop=True).then_inc(rot_ready, 1)

                def after_l(n):
                    if 10 <= n - 1 < 14:
                        turn_v(n - 1 - 10)
                    if 14 <= n - 1 < 22:
                        rotate_l(n - 1 - 14)

                for n in range(T_LIN):
                    xk(T + n, N + n, feed=feed if n == 0 else None, mid=lambda: after_l(n))
                    if n == 0:
                        x_norm(U0, feed)
                        lam_sum()
                rotate_l(7)

                SL = [G[0], G[1], ROT, POOLB]
                with pe.Fori(0, 4) as h:
                    pe.wait_ge(tile_out, (N + T_LIN).value())
                    pe.wait_ge(rot_read, (RO + 8).value())
                    pe.wait_ge(R["lam_exp"], L1.value())
                    H = Count(0).loop(l, 4).loop(h, 1)
                    SS = Count(4 * NU).loop(l, 32).loop(h, 8)
                    TT = Count(4 * NU).loop(l, 16).loop(h, 4)
                    pe.wait_ge(R["kv_cur"], Count(2).loop(l, 8).loop(h, 2).value())

                    def score_l(i):
                        n = (i + 1) * P
                        for m in range(2):
                            s = SL[(2 * i + m) % 4]
                            if i >= 2:
                                pe.wait_ge(R["exp_ready"], (SS + (2 * i + m - 3)).value())
                            mm(s[:, 0:n], lqc[m * 64:(m + 1) * 64, i * P:n], lkc[m * 64:(m + 1) * 64, 0:n],
                               start=True, stop=False)
                            mm(s[:, i * P:n], identb, causal, start=False, stop=True).then_inc(R["s_psum"], 1)

                    def turn_l(i):
                        pe.wait_ge(R["p_ready"], (TT + (i + 1)).value())
                        if i >= 2:
                            pe.wait_ge(R["pt_ready"], (TT + (i - 1)).value())
                        for c in range(i + 1):
                            x_ = pe.transpose(TB[i % 2][:, c * P:(c + 1) * P], lp[:, i % 2, 0, c * P:(c + 1) * P], ident)
                        x_.then_inc(R["pt_psum"], 1)

                    score_l(0)
                    score_l(1)
                    for i in range(NT):
                        turn_l(i)
                        if i + 2 < NT:
                            score_l(i + 2)
                    pe.wait_ge(R["pt_ready"], (TT + 4).value())
                    for c in range(NT):
                        x_ = mm(OUT[:, c * P:S], lvc[:, c, :], lpt[:, c, c * P:S], start=c == 0, stop=c == 3)
                    x_.then_inc(R["o_psum"], 1)
                    pe.wait_ge(R["head_ready"], (H + 1).value())

                def ln_stats(u, src):
                    stats(u, lambda i: [src[:, c, i * P:(i + 1) * P] for c in range(2)], one)

                pe.wait_ge(R["conv_done"], L1.value())
                ln_stats(U0 + 1, conv)
                spread(U0 + 1, lambda i: s_recip[:, i:i + 1].to_broadcast([P, P]))
                pe.wait_ge(R["ln_sq"], L1.value())
                ln_stats(U0 + 2, sq)
                spread(U0 + 2, lambda i: s_recip[:, i:i + 1].to_broadcast([P, P]))
                with pe.Fori(0, 4) as h:
                    u = (U0 + 3).loop(h, 1)
                    pe.wait_ge(sq_ready, Count(8).loop(l, 4).loop(h, 1).value())
                    stats(u, lambda i: [sq[:, 0, i * P:(i + 1) * P]], one)
                    spread(u, lambda i: s_recip[:, i:i + 1].to_broadcast([P, P]))

                tb, nb = out_and_ffn(T + T_LIN, N + T_LIN, (yh, yl), (R["y_lo"], Count(KD).loop(l, KD)), U0 + 7,
                                     Count(3 * KD).loop(l, 2 * KD))
                down(tb, nb, Count(2 * KF).loop(l, KF))

            x_norm(Count(U_BLOCK1 + LAYERS * U_LAYER), Count((2 + 2 * LAYERS) * KD))

        @block.scalar
        def _(act):
            def copy(o, i, scale=1.0):
                return act.activation(o, i, ACT.Copy, scale=scale)

            def head(t):
                s = t.even()
                act.wait_ge(raw_landed[s], (t.half() + 1).value(16))
                wait(act, chunk_done, t + -1)
                copy(wh[:, s, :], raw_slot(t)).then_inc(hi_ready, 1)

            def root(u, n, parts=P, scale=1.0, eps=EPS, plain=False):
                act.wait_ge(stat_ready, (u + 1).value())
                wait(act, recip_ready, u)
                o, i = s_root[0:parts, 0:n], STAT[0:parts, 0:n]
                if plain:
                    copy(o, i, scale=scale).then_inc(root_ready, 1)
                else:
                    act.activation(o, i, ACT.Sqrt, scale=scale, bias=eps_ap(eps)[0:parts, :]).then_inc(root_ready, 1)

            def eps_ap(e):
                return small[:, 188:189] if e == EPS else small[:, 189:190]

            def flat(a):
                return a[:, :, :].rearrange("p k n -> p (k n)")

            def feed(m, k, g, n):
                if n is not None:
                    act.wait_ge(tile_out, (n + 1).value())
                wait(act, xl_ready, k + -1)
                copy(flat(xh)[:, cols(m * S, S)], flat(xs)[:, cols(m * S, S)], scale=g)
                act.activation(sq[:, k.even(), :], flat(xs)[:, cols(m * S, S)], ACT.Square).then_inc(xh_ready, 1)

            act.wait_ge(R["zeroed"], 1)
            act.wait_ge(par_landed, 16 * 6)
            act.wait_ge(x_landed, 16)
            head(Count(0))
            head(Count(1))
            for m in range(KD):
                feed(m, Count(m), c1("mix_g", m), None)
            for n, (o, i) in enumerate(((sin, red), (cos, red), (sin2, red2), (cos2, red2))):
                act.wait_ge(R["tables"], n + 1)
                act.activation(o[:, :], i[:, :], ACT.Sin).then_inc(sine_done, 1)
            root(Count(0), NT, scale=1.0 / D)
            for n in range(N_IN):
                act.wait_ge(chunk_done, n + 1)
                head(Count(n + 2))
                act.wait_ge(tile_out, n + 1)
                if 2 <= n < 8:
                    act.activation(sq[:, 0, :], ybuf[:, n % 2, :], ACT.Square).then_inc(sq_ready, 1)
                    root(Count(n - 1), 8, scale=1.0 / 64)
                if 8 <= n < 10:
                    act.wait_ge(tr_ready, n - 7)
                    copy(vt[:, n - 8, :, :].rearrange("p i d -> p (i d)"), TR[:, :]).then_inc(tr_read, 1)
                if n == 10:
                    act.wait_ge(tr_ready, 3)
                    act.activation(gates_t, TR[:, :].rearrange("p (i c) -> p i c", i=NT)[:, :, 0:24],
                                   ACT.Sigmoid).then_inc(tr_read, 1)
                if n >= 13:
                    g = n - 13
                    act.wait_ge(R["pool_psum"], g + 1)
                    copy(poh[:, g, :], POOLB[:, :], scale=c1("pool_scale", g)).then_inc(R["pool_hi"], 1)
            act.wait_ge(R["pool_psum"], 3)
            copy(poh[:, 2, :], POOLB[:, :], scale=c1("pool_scale", 2)).then_inc(R["pool_hi"], 1)
            act.wait_ge(R["hid_psum"], 1)
            act.activation(hid[:, 0, 0:31], ROT[:, 0:31], ACT.Silu)
            act.activation(hid[:, 1, 0:31], BC[:, 0:31], ACT.Silu).then_inc(R["hid_ready"], 1)
            act.wait_ge(R["pool_psum"], 4)
            copy(poh[:, 3, :], POOLB[:, :], scale=c1("pool_scale", 3)).then_inc(R["pool_hi"], 1)
            act.wait_ge(R["hid_psum"], 2)
            act.wait_ge(R["cmp_psum"], 1)
            act.activation(hid[:, 0, 0:31], ROT[:, 0:31], ACT.Silu)
            act.activation(hid[:, 1, 0:31], BC[:, 0:31], ACT.Silu).then_inc(R["hid_ready"], 1)
            act.wait_ge(R["cmp_copied"], 1)
            act.activation(csq, kcf, ACT.Square).then_inc(sq_ready, 1)
            root(Count(7), 2, parts=32, scale=1.0 / 64)
            act.wait_ge(R["vct_psum"], 1)
            copy(vct, TR[0:32, 0:P]).then_inc(R["vct_ready"], 1)

            TB = [STAT, BC]
            SB = [G[0], G[1], ROT, POOLB]
            with act.Fori(0, 4) as j:
                U = Count(0).loop(j, NU)
                J = Count(0).loop(j, 1)

                def exps(u):
                    n = (u % 4 + 1) * P
                    act.wait_ge(R["max_ready"], (U + (u + 1)).value())
                    if u >= 4:
                        act.wait_ge(R["pt_psum"], (U + (u - 3)).value())
                    act.activation(probs[:, u % 4, 0:n], SB[u % 4][:, 0:n], ACT.Exp, bias=negmx[:, u:u + 1],
                                   accum_out=rows[:, u:u + 1]).then_inc(R["exp_ready"], 1)

                def put(u):
                    i, w = u % 4, u // 4
                    act.wait_ge(R["pt_psum"], (U + (u + 1)).value())
                    if w >= 2 and i == 0:
                        act.wait_ge(R["pv_done"], Count(w - 1).loop(j, 4).value())
                    copy(pt[:, w % 2, 0:i + 1, i * P:(i + 1) * P],
                         TB[u % 2][:, 0:(i + 1) * P].rearrange("p (c q) -> p c q", q=P)).then_inc(R["pt_ready"], 1)

                for u in range(NU + 2):
                    if u < NU:
                        exps(u)
                    if u == 1:
                        act.wait_ge(R["c_sub"], (J + 1).value())
                        act.activation(cmp_p[:, :, :], cmp_p[:, :, :], ACT.Exp).then_inc(R["c_exp"], 1)
                    if u >= 2:
                        put(u - 2)
                    if u == 5:
                        for g in range(2):
                            act.wait_ge(R["c_tpsum"], Count(g + 1).loop(j, 2).value())
                            copy(cmp_pt[:, g, :], TR[0:32, :]).then_inc(R["c_tready"], 1)
                act.wait_ge(R["o_psum"], (J + 1).value())
                copy(nh[:, :, :].rearrange("p k n -> p (k n)")[:, bass.ds(j * S, S)], OUT[:, :])\
                    .then_inc(R["o_hi"], 1)

            with act.Fori(0, KD // 2) as r:
                for m in range(2):
                    t = Count(T_IN + 3 * m).loop(r, 6)
                    K = Count(m).loop(r, 2)
                    for c in range(3):
                        act.wait_ge(chunk_done, (t + (c + 1)).value())
                        head(t + (c + 2))
                        if c < 2:
                            act.wait_ge(tile_out, Count(N_IN + 4 * m + c + 1).loop(r, 8).value())
                            act.activation(ybuf[:, c, :], ybuf[:, c, :], ACT.Sigmoid).then_inc(R["mix_sig"], 1)
                    act.wait_ge(R["mix_sum"], (K + 1).value())
                    copy(mh[:, :, :].rearrange("p k n -> p (k n)")[:, bass.ds(K.value() * S, S)], tmp2[:, 0:S])\
                        .then_inc(R["mix_hi"], 1)

            def out_and_ffn(t, n, u, feed0, gain, h0, first_block):
                with act.Fori(0, KD // 2) as r:
                    for m in range(2):
                        tt = (t + m).loop(r, 2)
                        act.wait_ge(chunk_done, (tt + 1).value())
                        head(tt + 2)
                    for m in range(2):
                        feed(r * 2 + m, (feed0 + m).loop(r, 2), gain("ffn_g", r, m), (n + m).loop(r, 2))
                t, n = t + T_OUT, n + KD
                act.wait_ge(chunk_done, (t + 1).value())
                head(t + 2)
                root(u, NT, scale=1.0 / D)
                act.wait_ge(chunk_done, (t + 2).value())
                head(t + 3)

                hidden(n, h0, 0, first_block)
                with act.Fori(1, KF) as r:
                    for c in range(2):
                        act.wait_ge(chunk_done, (t + (c + 1)).loop(r, 2).value())
                        head((t + (c + 2)).loop(r, 2))
                    hidden(n.loop(r, 2), h0.loop(r, 1), r, first_block)
                return t + T_UP, n + T_UP

            def hidden(n, k, j, first_block):
                if first_block:
                    act.wait_ge(R["conv_ready"], (k + 1).value())
                else:
                    act.wait_ge(tile_out, (n + 1).value())
                act.activation(tmp[:, 0, :], tmp[:, 0, :], ACT.Silu).then_inc(R["silu_ready"], 1)
                act.wait_ge(R["prod_ready"], (k + 1).value())
                copy(flat(hh)[:, cols(j * S, S)], tmp[:, 1, :]).then_inc(R["h_hi"], 1)

            def down(t, n, feed0, gain):
                with act.Fori(0, KD // 2) as r:
                    for c in range(2 * DOWN_CHUNKS):
                        tt = (t + c).loop(r, 2 * DOWN_CHUNKS)
                        act.wait_ge(chunk_done, (tt + 1).value())
                        head(tt + 2)
                        if c == DOWN_CHUNKS:
                            feed(r * 2, feed0.loop(r, 2), gain("next_g", r, 0), n.loop(r, 2))
                    feed(r * 2 + 1, (feed0 + 1).loop(r, 2), gain("next_g", r, 1), (n + 1).loop(r, 2))

            def gain1(name, r, m):
                return pr1[:, bass.ds(r * 2 + (P1[name] + m), 1)]

            def gain2(name, r, m):
                return par[:, bass.ds(r * 2 + (P2[name] + m), 1)]

            t, n = out_and_ffn(Count(T_IN + T_MIX), Count(N_IN + N_MIX), Count(8), Count(KD), gain1, Count(0), True)
            down(t, n, Count(2 * KD), gain1)

            with act.Fori(0, LAYERS) as l:
                T = Count(T_BLOCK1).loop(l, T_LAYER)
                N = Count(N_BLOCK1).loop(l, N_LAYER)
                U0 = Count(U_BLOCK1).loop(l, U_LAYER)
                L1 = Count(1).loop(l, 1)
                act.wait_ge(R["par_ready"], L1.value())
                for n in range(T_LIN):
                    act.wait_ge(chunk_done, (T + (n + 1)).value())
                    head(T + (n + 2))
                    if n == 0:
                        root(U0, NT, scale=1.0 / D)
                        act.wait_ge(R["lam_psum"], L1.value())
                        act.activation(lame, POOLB[:, 0:2], ACT.Exp).then_inc(R["lam_exp"], 1)
                    if n in (2, 3):
                        act.wait_ge(tile_out, (N + (n + 1)).value())
                        act.activation(cg[:, n - 2, :], cg[:, n - 2, :], ACT.Sigmoid, bias=c2("glu_b", n))\
                            .then_inc(R["glu_sig"], 1)
                    if 10 <= n < 14:
                        act.wait_ge(tr_ready, Count(3 + n - 10 + 1).loop(l, 4).value())
                        copy(lv[:, :, (n - 10) * P:(n - 9) * P], TR[:, :].rearrange("p (c d) -> p c d", c=NT))\
                            .then_inc(tr_read, 1)
                with act.Fori(0, 4) as h:
                    SS = Count(4 * NU).loop(l, 32).loop(h, 8)
                    TT = Count(4 * NU).loop(l, 16).loop(h, 4)
                    H = Count(0).loop(l, 4).loop(h, 1)
                    act.wait_ge(R["o_psum"], (Count(4).loop(l, 4).loop(h, 1)).value())
                    copy(lvc[:, :, :], lv[:, :, bass.ds(h * P, P)]).then_inc(R["kv_cur"], 1)

                    def exps(i):
                        n = (i + 1) * P
                        for m in range(2):
                            u = 2 * i + m
                            act.wait_ge(R["max_ready"], (SS + (u + 1)).value())
                            if i >= 2 and m == 0:
                                act.wait_ge(R["pt_psum"], (TT + (i - 1)).value())
                            act.activation(lp[:, i % 2, m, 0:n], SB[u % 4][:, 0:n], ACT.Exp, bias=negmx2[:, u:u + 1],
                                           accum_out=rows2[:, u:u + 1]).then_inc(R["exp_ready"], 1)

                    def put(i):
                        act.wait_ge(R["pt_psum"], (TT + (i + 1)).value())
                        copy(lpt[:, 0:i + 1, i * P:(i + 1) * P],
                             TB[i % 2][:, 0:(i + 1) * P].rearrange("p (c q) -> p c q", q=P)).then_inc(R["pt_ready"], 1)

                    exps(0)
                    exps(1)
                    for i in range(NT):
                        put(i)
                        if i + 2 < NT:
                            exps(i + 2)
                    act.wait_ge(R["o_psum"], (Count(5).loop(l, 4).loop(h, 1)).value())
                    copy(lo_[:, :, :].rearrange("p k n -> p (k n)")[:, bass.ds(h * S, S)], OUT[:, :])\
                        .then_inc(R["head_ready"], 1)
                root(U0 + 1, NT, scale=1.0 / 256, plain=True)
                act.wait_ge(bc_read, (U0 + 2).value())
                act.activation(sq[:, :, :], conv[:, :, :], ACT.Square).then_inc(R["ln_sq"], 1)
                root(U0 + 2, NT, scale=1.0 / 256, eps=LN_EPS)
                for h in range(4):
                    act.wait_ge(stat_ready, (U0 + (3 + h)).value())
                    act.activation(sq[:, 0, :], lo_[:, h, :], ACT.Square).then_inc(sq_ready, 1)
                    root(U0 + (3 + h), NT, scale=1.0 / P)
                for c in range(2):
                    act.wait_ge(bc_read, (U0 + 3).value())
                    act.activation(conv[:, c, :], conv[:, c, :], ACT.Silu, bias=c2("ln_b", c)).then_inc(R["yc_ready"], 1)
                act.wait_ge(bc_read, (U0 + 7).value())
                for k in range(KD):
                    src = ya[:, k, :] if k < 2 else lo_[:, k - 2, :] if k < 6 else conv[:, k - 6, :]
                    if k == 6:
                        act.wait_ge(R["yc_ready"], Count(2).loop(l, 2).value())
                    copy(yh[:, k, :], src).then_inc(R["y_hi"], 1)
                t, n = out_and_ffn(T + T_LIN, N + T_LIN, U0 + 7, Count(3 * KD).loop(l, 2 * KD), gain2,
                                   Count(KF).loop(l, KF), False)
                down(t, n, Count(4 * KD).loop(l, 2 * KD), gain2)
            root(Count(U_BLOCK1 + LAYERS * U_LAYER), NT, scale=1.0 / D)

        @block.vector
        def _(dve):
            tt, ts, stt = dve.tensor_tensor, dve.tensor_scalar, dve.scalar_tensor_tensor

            def fma(o, a, s, b):
                return stt(out=o, in0=a, scalar=s, in1=b, op0=ALU.mult, op1=ALU.add)

            def mul3(o, a, s, b):
                return stt(out=o, in0=a, scalar=s, in1=b, op0=ALU.mult, op1=ALU.mult)

            flat = lambda a: a[:, :, :].rearrange("p k n -> p (k n)")

            def tile_of(a, m):
                return a[:, m, :] if isinstance(m, int) else flat(a)[:, bass.ds(m * S, S)]

            def feed(m, k, g):
                dve.wait_ge(xh_ready, (k + 1).value())
                stt(out=tile_of(xl, m), in0=tile_of(xs, m), scalar=g, in1=tile_of(xh, m).bitcast(F32),
                    op0=ALU.mult, op1=ALU.subtract)
                tt(sqacc[:, :], sqacc[:, :], sq[:, k.even(), :], ALU.add).then_inc(xl_ready, 1)

            def recips(u, n, parts=P, plain=False):
                dve.wait_ge(root_ready, (u + 1).value())
                o, i = s_recip[0:parts, 0:n], s_root[0:parts, 0:n]
                (dve.tensor_copy(o, i) if plain else dve.reciprocal(o, i)).then_inc(recip_ready, 1)

            def pair_recips(u, n, parts=P):
                dve.wait_ge(root_ready, (u + 1).value())
                dve.reciprocal(s_recip[0:parts, 0:n], s_root[0:parts, 0:n])
                dve.drain()
                dve.tensor_copy(pairs[0:parts, 0:64 * n].rearrange("p (u d) -> p u d", d=64),
                                s_recip[0:parts, 0:n].unsqueeze(2).to_broadcast([parts, n, 64])).then_inc(recip_ready, 1)

            def x_norm(u):
                recips(u, NT)
                dve.wait_ge(bc_ready, (u + 1).value())
                dve.tensor_copy(rstd[:, :], BC[:, :]).then_inc(bc_read, 1)
                dve.memset(sqacc[:, :], 0.0)
                dve.drain()

            def take(t, n, o, scale=None):
                dve.wait_ge(chunk_done, (t + 1).value())
                b = G[n.even()]
                if scale is None:
                    return tt(o, b[:, :], rstd[:, :], ALU.mult).then_inc(tile_out, 1)
                return mul3(o, b[:, :], scale, rstd[:, :]).then_inc(tile_out, 1)

            def tables(src, pf, an, tu, rd, inv, first):
                two_pi = 2.0 * np.pi
                c1_ = 6.28125
                c2_ = float(np.float32(np.round((two_pi - c1_) * 2 ** 18) / 2 ** 18))
                c3_ = float(two_pi - c1_ - c2_)
                magic = 1.5 * 2 ** 23
                lim = 3.1415925
                dve.tensor_copy(pf[:, :], src[:, :])
                dve.drain()
                ts(an[:, :], pf[:, :], inv, None, ALU.mult)
                dve.drain()
                for c in range(2):
                    ts(tu[:, :], an[:, :], 1.0 / two_pi, 0.25 * c, ALU.mult, ALU.add)
                    dve.drain()
                    ts(tu[:, :], tu[:, :], magic, magic, ALU.add, ALU.subtract)
                    if c:
                        dve.wait_ge(sine_done, first + 1)
                    dve.drain()
                    fma(rd[:, :], tu[:, :], -c1_, an[:, :])
                    dve.drain()
                    fma(rd[:, :], tu[:, :], -c2_, rd[:, :])
                    dve.drain()
                    fma(rd[:, :], tu[:, :], -c3_, rd[:, :])
                    dve.drain()
                    ts(rd[:, :], rd[:, :], float(np.pi / 2) * c, lim, ALU.add, ALU.min)
                    dve.drain()
                    ts(rd[:, :], rd[:, :], -lim, None, ALU.max).then_inc(R["tables"], 1)

            dve.memset(small[:, :], 0.0)
            dve.memset(small2[:, :], 0.0)
            dve.memset(sqacc[:, :], 0.0)
            dve.drain()
            dve.memset(small[:, 188:189], EPS)
            dve.memset(small[:, 189:190], LN_EPS)
            dve.drain()
            dve.memset(tmp2[:, :], 0.0).then_inc(R["zeroed"], 1)
            dve.wait_ge(par_landed, 16 * 6)
            dve.wait_ge(x_landed, 16)
            for m in range(KD):
                dve.drain()
                feed(m, Count(m), c1("mix_g", m))
            ts(q_g8, c1("q_g"), 0.125, None, ALU.mult)
            dve.wait_ge(pos_landed, 32)
            tables(posi, posf, ang, turns, red, cst[:, C["inv1"]:C["inv1"] + 1], 0)
            tables(posi2, posf2, ang2, turns2, red2, cst[:, C["inv2"]:C["inv2"] + 1], 2)
            x_norm(Count(0))
            dve.wait_ge(sine_done, 4)

            def normed(n, gain):
                i = n - 2
                dve.wait_ge(bc_ready, n)
                mul3(tmp[:, i % 2, :], ybuf[:, n % 2, :], gain, BC[:, :]).then_inc(bc_read, 1)
                dve.drain()
                tt(tmp3[:, 0:S], tmp[:, i % 2, :], cos[:, :], ALU.mult).then_inc(rot_in, 1)

            def rotated(i, dst):
                dve.wait_ge(rot_ready, i + 1)
                tt(tmp2[:, 0:S], ROT[:, :], sin[:, :], ALU.mult).then_inc(rot_read, 1)
                dve.drain()
                tt(dst, tmp2[:, 0:S], tmp3[:, 0:S], ALU.add)

            dsts = [kk[:, 0, :], kk[:, 1, :]] + [qall[:, c, :] for c in range(4)]
            gains = [c1("sel_g"), c1("win_g")] + [q_g8] * 4

            def pooled(g):
                w = 2 << g
                y = ybuf[:, (11 + g) % 2, :]
                dve.memset(tmp2[:, 0:16], 0.0)
                dve.memset(tmp3[:, 0:16], 0.0)
                dve.tensor_copy(tmp2[:, 16:528], y)
                a, b, w_ = tmp2, tmp3, 1
                while w_ < w:
                    dve.drain()
                    tt(b[:, 16:528], a[:, 16:528], a[:, 16 - w_:528 - w_], ALU.add)
                    a, b, w_ = b, a, 2 * w_
                dve.drain()
                if g >= 2:
                    dve.wait_ge(R["pool_psum"], g - 1)
                stt(out=tmp[:, g % 2, :], in0=a[:, 16:528], scalar=1.0 / w, in1=y, op0=ALU.mult, op1=ALU.subtract)
                tt(small2[:, 480:496], a[:, 16:32], cst[:, C["rcount"] + 16 * g:C["rcount"] + 16 * g + 16], ALU.mult)
                dve.drain()
                tt(tmp[:, g % 2, 0:16], small2[:, 480:496], y[:, 0:16], ALU.subtract).then_inc(R["pool_in"], 1)

            def pool_rest(g):
                dve.wait_ge(R["pool_hi"], g + 1)
                stt(out=pol[:, g, :], in0=POOLB[:, :], scalar=c1("pool_scale", g), in1=poh[:, g, :].bitcast(F32),
                    op0=ALU.mult, op1=ALU.subtract).then_inc(R["pool_lo"], 1)

            def blocks(c, pe_name):
                for half in range(2):
                    v = kvraw[:, c, 16 * half:16 * half + 16 * N_CMP].rearrange("p (b l) -> p l b", l=16)
                    e = pr1[:, P1[pe_name] + 16 * half:P1[pe_name] + 16 * half + 16].unsqueeze(2)\
                        .to_broadcast([P, 16, N_CMP])
                    x_ = tt(blk[:, 16 * half:16 * half + 16, :], v, e, ALU.add)
                x_.then_inc(R["blk_ready"], 1)

            for n in range(N_IN):
                if 2 <= n - 1 < 8:
                    pair_recips(Count(n - 2), 8)
                take(Count(n), Count(n), kvraw[:, n, :] if n < 2 else ybuf[:, n % 2, :])
                if 2 <= n - 2 < 8:
                    rotated(n - 4, dsts[n - 4])
                if 2 <= n - 1 < 8:
                    normed(n - 1, gains[n - 3])
                if n == 10:
                    blocks(0, "pe_k")
                if n >= 11:
                    dve.drain()
                    pooled(n - 11)
                if n >= 13:
                    pool_rest(n - 13)
            pool_rest(2)
            dve.wait_ge(R["hid_psum"], 1)
            blocks(1, "pe_v")
            pool_rest(3)
            for c, dst in enumerate((kcf, vcf)):
                dve.wait_ge(R["cmp_psum"], c + 1)
                for g in range(2):
                    x_ = dve.tensor_copy(dst[g * 64:(g + 1) * 64, 0:31], TR[g * 64:(g + 1) * 64, g * 31:g * 31 + 31])
                x_.then_inc(R["cmp_copied"], 1)
            pair_recips(Count(7), 2, parts=32)
            dve.wait_ge(bc_ready, 8)
            mul3(cyn[:, 0:32], kcf, c1("cmp_g"), BC[:, 0:32]).then_inc(bc_read, 1)
            dve.drain()
            ends = lambda a: a[:, 16:S].rearrange("p (b l) -> p b l", l=16)[:, :, 15]
            tt(ctm[:, 0:31], cyn[:, 0:31], ends(cos), ALU.mult).then_inc(rot_in, 1)
            dve.wait_ge(rot_ready, 7)
            tt(csq[:, 0:31], ROT[:, 0:31], ends(sin), ALU.mult)
            dve.drain()
            tt(kct[:, 0:31], csq[:, 0:31], ctm[:, 0:31], ALU.add).then_inc(rot_read, 1)
            dve.drain()

            SB = [G[0], G[1], ROT, POOLB]
            with dve.Fori(0, 4) as j:
                U = Count(0).loop(j, NU)
                J = Count(0).loop(j, 1)
                dve.tensor_copy(qcur[:, :], flat(qall)[:, bass.ds(j * S, S)]).then_inc(R["q_cur"], 1)
                dve.wait_ge(R["c_psum"], (J + 1).value())
                sc = [b[:, 0:P].rearrange("p (u n) -> p u n", n=32) for b in (TR, OUT)]
                for g in range(2):
                    dve.tensor_reduce(mx8[:, 4 * g:4 * g + 4], sc[g], AX.X, ALU.max)
                dve.drain()
                ts(mx8, mx8, MASKED / 1e5, None, ALU.max)
                dve.drain()
                for g in range(2):
                    x_ = tt(cmp_p[:, 4 * g:4 * g + 4, :], sc[g],
                            mx8[:, 4 * g:4 * g + 4].unsqueeze(2).to_broadcast([P, 4, 32]), ALU.subtract)
                x_.then_inc(R["c_sub"], 1)

                def top(u):
                    dve.wait_ge(R["s_psum"], (U + (u + 1)).value())
                    dve.tensor_reduce(negmx[:, u:u + 1], SB[u % 4][:, 0:(u % 4 + 1) * P], AX.X, ALU.max, negate=True)\
                        .then_inc(R["max_ready"], 1)

                def scale(u):
                    g, b, i = u // 8, u // 4 % 2, u % 4
                    n = (i + 1) * P
                    dve.wait_ge(R["exp_ready"], (U + (u + 1)).value())
                    dve.reciprocal(rinv[:, u:u + 1], rows[:, u:u + 1])
                    dve.drain()
                    ts(probs[:, u % 4, 0:n], probs[:, u % 4, 0:n], rinv[:, u:u + 1],
                       small2[:, bass.ds(j * 6 + (24 * i + 3 * g + 1 + b), 1)], ALU.mult, ALU.mult)\
                        .then_inc(R["p_ready"], 1)

                for u in range(NU + 2):
                    if u < NU:
                        top(u)
                    if u >= 2:
                        scale(u - 2)
                    if u == 2:
                        dve.wait_ge(R["c_exp"], (J + 1).value())
                        dve.tensor_reduce(sum8, cmp_p[:, :, :], AX.X, ALU.add)
                        dve.drain()
                        ts(sum8, sum8, 1e-30, None, ALU.max)
                        dve.drain()
                        dve.reciprocal(fac8, sum8)
                        dve.drain()
                        for g in range(2):
                            for i in range(NT):
                                x_ = ts(cmp_p[:, g * NT + i, :], cmp_p[:, g * NT + i, :],
                                   fac8[:, g * NT + i:g * NT + i + 1],
                                   small2[:, bass.ds(j * 6 + (24 * i + 3 * g), 1)], ALU.mult, ALU.mult)
                        x_.then_inc(R["c_probs"], 1)
                dve.wait_ge(R["o_hi"], (J + 1).value())
                tt(flat(nl)[:, bass.ds(j * S, S)], OUT[:, :], flat(nh)[:, bass.ds(j * S, S)].bitcast(F32),
                   ALU.subtract).then_inc(R["o_lo"], 1)

            with dve.Fori(0, KD // 2) as r:
                for m in range(2):
                    t, n = Count(T_IN + 3 * m).loop(r, 6), Count(N_IN + 4 * m).loop(r, 8)
                    K = Count(m).loop(r, 2)
                    for c in range(2):
                        take(t + c, n + c, ybuf[:, c, :])
                    for c in range(2):
                        dve.wait_ge(R["mix_sig"], Count(2 * m + c + 1).loop(r, 4).value())
                        dve.wait_ge(chunk_done, (t + 3).value())
                        tt(tmp[:, c, :], ybuf[:, c, :], G[(n + (2 + c)).even()][:, :], ALU.mult).then_inc(tile_out, 1)
                    dve.drain()
                    tt(tmp2[:, 0:S], tmp[:, 0, :], tmp[:, 1, :], ALU.add).then_inc(R["mix_sum"], 1)
                    dve.wait_ge(R["mix_hi"], (K + 1).value())
                    tt(flat(ml)[:, bass.ds(K.value() * S, S)], tmp2[:, 0:S],
                       flat(mh)[:, bass.ds(K.value() * S, S)].bitcast(F32), ALU.subtract).then_inc(R["mix_lo"], 1)

            def add_to_x(t, n, m):
                dve.wait_ge(chunk_done, (t + 1).value())
                tt(tile_of(xs, m), tile_of(xs, m), G[n.even()][:, :], ALU.add).then_inc(tile_out, 1)

            def out_and_ffn(t, n, u, feed0, gain, h0, first_block):
                with dve.Fori(0, KD // 2) as r:
                    for m in range(2):
                        add_to_x((t + m).loop(r, 2), (n + m).loop(r, 2), r * 2 + m)
                    for m in range(2):
                        dve.drain()
                        feed(r * 2 + m, (feed0 + m).loop(r, 2), gain("ffn_g", r, m))
                t, n = t + T_OUT, n + KD
                x_norm(u)
                hidden(t, n, h0, 0, first_block)
                with dve.Fori(1, KF) as r:
                    hidden(t.loop(r, 2), n.loop(r, 2), h0.loop(r, 1), r, first_block)
                return t + T_UP, n + T_UP

            def hidden(t, n, k, j, first_block):
                if first_block:
                    take(t, n, tmp2[:, 2:2 + S])
                    w = (lambda c: pr1[:, P1["conv_w"] + c:P1["conv_w"] + c + 1]) if isinstance(j, int) else \
                        (lambda c: pr1[:, bass.ds(j * 3 + (P1["conv_w"] + c), 1)])
                    b = c1("conv_b") if isinstance(j, int) else pr1[:, bass.ds(j + P1["conv_b"], 1)]
                    if isinstance(j, int):
                        dve.memset(tmp2[:, 0:2], 0.0)
                    dve.drain()
                    ts(tmp3[:, 0:S], tmp2[:, 2:2 + S], w(2), b, ALU.mult, ALU.add)
                    dve.drain()
                    fma(tmp3[:, 0:S], tmp2[:, 1:1 + S], w(1), tmp3[:, 0:S])
                    dve.drain()
                    fma(tmp[:, 0, :], tmp2[:, 0:S], w(0), tmp3[:, 0:S]).then_inc(R["conv_ready"], 1)
                else:
                    take(t, n, tmp[:, 0, :])
                take(t + 1, n + 1, ybuf[:, 0, :])
                dve.drain()
                dve.wait_ge(R["silu_ready"], (k + 1).value())
                tt(tmp[:, 1, :], tmp[:, 0, :], ybuf[:, 0, :], ALU.mult).then_inc(R["prod_ready"], 1)
                dve.wait_ge(R["h_hi"], (k + 1).value())
                tt(flat(hl)[:, cols(j * S, S)], tmp[:, 1, :], flat(hh)[:, cols(j * S, S)].bitcast(F32),
                   ALU.subtract).then_inc(R["h_lo"], 1)

            def down(t, n, feed0, gain):
                with dve.Fori(0, KD // 2) as r:
                    for m in range(2):
                        add_to_x((t + (DOWN_CHUNKS * (m + 1) - 1)).loop(r, 2 * DOWN_CHUNKS), (n + m).loop(r, 2), r * 2 + m)
                        dve.drain()
                        feed(r * 2 + m, (feed0 + m).loop(r, 2), gain("next_g", r, m))
                dve.drain()

            def gain1(name, r, m):
                return pr1[:, bass.ds(r * 2 + (P1[name] + m), 1)]

            def gain2(name, r, m):
                return par[:, bass.ds(r * 2 + (P2[name] + m), 1)]

            t, n = out_and_ffn(Count(T_IN + T_MIX), Count(N_IN + N_MIX), Count(8), Count(KD), gain1, Count(0), True)
            down(t, n, Count(2 * KD), gain1)

            with dve.Fori(0, LAYERS) as l:
                T = Count(T_BLOCK1).loop(l, T_LAYER)
                N = Count(N_BLOCK1).loop(l, N_LAYER)
                U0 = Count(U_BLOCK1).loop(l, U_LAYER)
                L1 = Count(1).loop(l, 1)
                dve.tensor_copy(par[:, :], pr2[:, bass.ds(l * NP2, NP2)]).then_inc(R["par_ready"], 1)
                dve.memset(cpad[:, :, 0:TAPS - 1], 0.0)
                dve.memset(acp[:, 0:2], 0.0)
                dve.drain()
                for c in range(2):
                    x_ = tt(lamp[:, c:c + 1], c2("lam", 2 * c), c2("lam", 2 * c + 1), ALU.mult)
                x_.then_inc(R["lam_in"], 1)
                ts(sub_gain, c2("sub_g"), c2("lam_init", 1), None, ALU.mult)
                x_norm(U0)
                dve.wait_ge(R["lam_exp"], L1.value())
                tt(neglam, lame[:, 1:2], lame[:, 0:1], ALU.subtract)
                dve.drain()
                tt(neglam, neglam, c2("lam_init", 0), ALU.subtract)

                def rot_end(i):
                    dve.wait_ge(rot_ready, Count(8 + i).loop(l, 8).value())
                    tt(tmp2[:, 0:S], ROT[:, :], sin2[:, :], ALU.mult).then_inc(rot_read, 1)
                    dve.drain()
                    tt((lq, lk)[i % 2][:, i // 2, :], tmp2[:, 0:S], tmp3[:, 0:S], ALU.add)

                tap = [0]

                def taps(n):
                    for k in range(tap[0], tap[0] + n):
                        dve.drain()
                        for c in range(2):
                            w = c2("dw_w", c * TAPS + k)
                            if k == 0:
                                ts(conv[:, c, :], cpad[:, c, 0:S], w, c2("dw_b", c), ALU.mult, ALU.add)
                            else:
                                x_ = fma(conv[:, c, :], cpad[:, c, k:k + S], w, conv[:, c, :])
                        if k == TAPS - 1:
                            x_.then_inc(R["conv_done"], 1)
                    tap[0] += n

                def glu(c):
                    dve.wait_ge(R["glu_sig"], Count(c + 1).loop(l, 2).value())
                    stt(out=cpad[:, c, TAPS - 1:TAPS - 1 + S], in0=ca[:, c, :], scalar=c2("glu_b", c),
                        in1=cg[:, c, :], op0=ALU.add, op1=ALU.mult)

                for n in range(T_LIN):
                    tl, nl_ = T + n, N + n
                    if n < 2:
                        take(tl, nl_, ca[:, n, :])
                    elif n < 4:
                        take(tl, nl_, cg[:, n - 2, :])
                        if n == 3:
                            glu(0)
                    elif n < 10:
                        c, what = (n - 4) // 3, (n - 4) % 3
                        if n == 4:
                            glu(1)
                        if what == 0:
                            take(tl, nl_, tmp3[:, 0:S])
                        elif what == 1:
                            take(tl, nl_, tmp2[:, 0:S])
                            dve.drain()
                            tt(acp[:, 2:2 + S], tmp3[:, 0:S], tmp2[:, 0:S], ALU.mult)
                            dve.drain()
                            ts(ya[:, c, :], acp[:, 2:2 + S], c2("short_w", 3 * c + 2), None, ALU.mult)
                            dve.drain()
                            fma(ya[:, c, :], acp[:, 1:1 + S], c2("short_w", 3 * c + 1), ya[:, c, :])
                            dve.drain()
                            fma(ya[:, c, :], acp[:, 0:S], c2("short_w", 3 * c), ya[:, c, :])
                        else:
                            take(tl, nl_, tmp3[:, 0:S])
                            dve.drain()
                            tt(ya[:, c, :], ya[:, c, :], tmp3[:, 0:S], ALU.mult)
                        taps((2, 0, 2)[what])
                    elif n < 14:
                        take(tl, nl_, ybuf[:, n % 2, :])
                        taps(3)
                    else:
                        i = n - 14
                        if i:
                            rot_end(i - 1)
                        take(tl, nl_, ybuf[:, n % 2, :], scale=0.125 if i % 2 == 0 else None)
                        dve.drain()
                        tt(tmp3[:, 0:S], ybuf[:, n % 2, :], cos2[:, :], ALU.mult)
                        taps(1 if i < 3 else 2 if i < 7 else 0)
                rot_end(7)
                assert tap[0] == TAPS
                dve.drain()

                with dve.Fori(0, 4) as h:
                    SS = Count(4 * NU).loop(l, 32).loop(h, 8)
                    TT = Count(4 * NU).loop(l, 16).loop(h, 4)
                    dve.wait_ge(R["o_psum"], (Count(4).loop(l, 4).loop(h, 1)).value())
                    dve.tensor_copy(lqc[:, :], flat(lq)[:, bass.ds(h * S, S)])
                    dve.tensor_copy(lkc[:, :], flat(lk)[:, bass.ds(h * S, S)]).then_inc(R["kv_cur"], 1)

                    def top(i):
                        for m in range(2):
                            u = 2 * i + m
                            dve.wait_ge(R["s_psum"], (SS + (u + 1)).value())
                            dve.tensor_reduce(negmx2[:, u:u + 1], SB[u % 4][:, 0:(i + 1) * P], AX.X, ALU.max,
                                              negate=True).then_inc(R["max_ready"], 1)

                    def combine(i):
                        n = (i + 1) * P
                        dve.wait_ge(R["exp_ready"], (SS + (2 * i + 2)).value())
                        dve.reciprocal(rinv2[:, 2 * i:2 * i + 2], rows2[:, 2 * i:2 * i + 2])
                        dve.drain()
                        ts(lp[:, i % 2, 1, 0:n], lp[:, i % 2, 1, 0:n], rinv2[:, 2 * i + 1:2 * i + 2], neglam,
                           ALU.mult, ALU.mult)
                        dve.drain()
                        fma(lp[:, i % 2, 0, 0:n], lp[:, i % 2, 0, 0:n], rinv2[:, 2 * i:2 * i + 1],
                            lp[:, i % 2, 1, 0:n]).then_inc(R["p_ready"], 1)

                    top(0)
                    top(1)
                    for i in range(NT):
                        combine(i)
                        if i + 2 < NT:
                            top(i + 2)

                recips(U0 + 1, NT, plain=True)
                dve.wait_ge(bc_ready, (U0 + 2).value())
                for c in range(2):
                    x_ = tt(conv[:, c, :], conv[:, c, :], BC[:, :], ALU.subtract)
                x_.then_inc(bc_read, 1)
                recips(U0 + 2, NT)
                dve.wait_ge(bc_ready, (U0 + 3).value())
                for c in range(2):
                    x_ = mul3(conv[:, c, :], conv[:, c, :], c2("ln_g", c), BC[:, :])
                x_.then_inc(bc_read, 1)
                for h in range(4):
                    recips(U0 + (3 + h), NT)
                    dve.wait_ge(bc_ready, (U0 + (4 + h)).value())
                    mul3(lo_[:, h, :], lo_[:, h, :], sub_gain, BC[:, :]).then_inc(bc_read, 1)
                for k in range(KD):
                    src = ya[:, k, :] if k < 2 else lo_[:, k - 2, :] if k < 6 else conv[:, k - 6, :]
                    dve.wait_ge(R["y_hi"], Count(k + 1).loop(l, KD).value())
                    tt(yl[:, k, :], src, yh[:, k, :].bitcast(F32), ALU.subtract).then_inc(R["y_lo"], 1)
                t, n = out_and_ffn(T + T_LIN, N + T_LIN, U0 + 7, Count(3 * KD).loop(l, 2 * KD), gain2,
                                   Count(KF).loop(l, KF), False)
                down(t, n, Count(4 * KD).loop(l, 2 * KD), gain2)

            x_norm(Count(U_BLOCK1 + LAYERS * U_LAYER))
            for m in range(KD):
                if m >= 2:
                    dve.wait_ge(stored[m % 2], 16 * (m // 2))
                mul3(ybuf[:, m % 2, :], xs[:, m, :], c2("next_g", m), rstd[:, :]).then_inc(R["out_ready"], 1)


def kernel(**inputs):
    import ml_dtypes
    import concourse.bacc as bacc
    from concourse.bass_utils import run_bass_kernel_spmd

    g = {k: np.ascontiguousarray(v) for k, v in inputs.items()}

    def blocks(w):
        k, m = w.shape
        return w.reshape(k // P, P, m // P, P).transpose(2, 0, 1, 3)

    def chunks(b):
        m, k = b.shape[:2]
        n = -(-k // CB)
        full = np.zeros((m, n * CB, P, P), np.float32)
        full[:, :k] = b
        return full.reshape(m * n, CB, P, P).transpose(0, 2, 1, 3).reshape(m * n, P, CB * P)

    def columns(v):
        return v.reshape(-1, P).T

    def pair(v):
        return np.concatenate([v, v])[:, None]

    w_in = g["w_in"][0]
    kv = w_in[:, 1024:1792].reshape(D, 6, P)
    q = w_in[:, 512:1024].reshape(D, 2, 4, 64).transpose(0, 2, 1, 3).reshape(D, 4, P)
    gates = np.zeros((D, P), np.float32)
    gates[:, :24] = w_in[:, 1792:1816].reshape(D, 2, 4, 3).transpose(0, 2, 1, 3).reshape(D, 24)
    tiles = [kv[:, i] for i in (0, 1, 2, 4)] + [q[:, j] for j in range(4)] + [kv[:, 3], kv[:, 5], gates]
    stream = [chunks(blocks(np.concatenate(tiles + [w_in[:, 0:512]], 1)))]
    merge = blocks(w_in[:, 1816:])
    nsa_rows = g["w_nsa_out"][0].reshape(2, 4, 64, D).transpose(1, 0, 2, 3).reshape(512, D)
    both = np.concatenate([blocks(g["w_pool_out"][0]), blocks(nsa_rows)], 1)
    mix = np.stack([merge[:KD], merge[KD:], both], 1).reshape(3 * KD, CB, P, P)
    stream.append(chunks(mix))

    def ffn(gate, value, down):
        up = np.stack([blocks(gate), blocks(value)], 1).reshape(2 * KF, KD, P, P)
        return [chunks(up), chunks(blocks(down))]

    stream.append(chunks(blocks(g["w_out"][0])))
    stream += ffn(g["w_up"][0][:, :FF], g["w_up"][0][:, FF:], g["w_down"][0])
    for l in range(LAYERS):
        w = g["w_in_2"][l]
        a_b, a_c, a_x = w[:, 0:256], w[:, 256:512], w[:, 512:768]
        ql, kl = (w[:, o:o + 512].reshape(D, 2, 4, 64).transpose(0, 2, 1, 3).reshape(D, 4, P) for o in (768, 1280))
        parts = [w[:, 2304:2816]]
        for c in range(2):
            parts += [a[:, c * P:(c + 1) * P] for a in (a_c, a_x, a_b)]
        parts.append(w[:, 1792:2304])
        for h in range(4):
            parts += [ql[:, h], kl[:, h]]
        stream.append(chunks(blocks(np.concatenate(parts, 1))))
        stream.append(chunks(blocks(g["w_out_2"][l])))
        stream += ffn(g["w_gate_2"][l], g["w_up_2"][l], g["w_down_2"][l])
    weights = np.concatenate(stream)
    assert len(weights) == T_ALL

    par1 = np.zeros((P, NP1), np.float32)

    def put1(name, v):
        par1[:, P1[name]:P1[name] + v.shape[1]] = v

    put1("mix_g", columns(g["mix_norm_g"][0]))
    put1("q_g", pair(g["q_norm_g"][0]))
    for i, name in enumerate(("cmp_g", "sel_g", "win_g")):
        put1(name, pair(g["k_norm_g"][0, i]))
    put1("pool_scale", columns(g["pool_scale"][0]))
    put1("ffn_g", columns(g["ffn_norm_g"][0]))
    put1("conv_w", g["conv_w"][0].reshape(3, KF, P).transpose(2, 1, 0).reshape(P, 3 * KF))
    put1("conv_b", columns(g["conv_b"][0]))
    put1("next_g", columns(g["mix_norm_g_2"][0]))
    for i, name in enumerate(("pe_k", "pe_v")):
        put1(name, np.concatenate([g["cmp_pe"][0, i].T] * 2))

    par2 = np.zeros((P, LAYERS * NP2), np.float32)
    for l in range(LAYERS):
        def put2(name, v, at=0):
            o = l * NP2 + P2[name] + at
            par2[:v.shape[0], o:o + v.shape[1]] = v

        put2("short_w", g["short_conv_w_2"][l].reshape(3, 2, P).transpose(2, 1, 0).reshape(P, 6))
        put2("glu_b", columns(g["glu_b_2"][l]))
        put2("dw_w", g["conf_dw_w_2"][l].reshape(TAPS, 2, P).transpose(2, 1, 0).reshape(P, 2 * TAPS))
        put2("dw_b", columns(g["conf_dw_b_2"][l]))
        put2("ln_g", columns(g["conf_ln_g_2"][l]))
        put2("ln_b", columns(g["conf_ln_b_2"][l]))
        put2("sub_g", columns(g["diff_subln_g_2"][l]))
        put2("ffn_g", columns(g["ffn_norm_g_2"][l]))
        put2("next_g", columns(g["mix_norm_g_2"][l + 1] if l + 1 < LAYERS else g["final_norm_g_2"]))
        for i, name in enumerate(("lam_q1_2", "lam_k1_2", "lam_q2_2", "lam_k2_2")):
            put2("lam", g[name][l][:, None], i)
        init = 0.8 - 0.6 * np.exp(-0.3 * l)
        put2("lam_init", np.tile(np.float32([[init, 1.0 - init]]), (P, 1)))

    consts = np.zeros((P, NC), np.float32)
    consts[:, C["ident"]:C["ident"] + P] = np.eye(P)
    for name, dim, half in (("rot1", 16, 8), ("rot2", 64, 32)):
        for h in (0, 64):
            for i in range(half):
                consts[h + half + i, C[name] + h + i] = -1.0
                consts[h + i, C[name] + h + half + i] = 1.0
    consts[:, C["ones"]:C["ones"] + P] = 1.0
    consts[:64, C["halves"]] = 1.0
    consts[64:, C["halves"] + 1] = 1.0
    p = np.arange(P) % 64
    inv1 = (500000.0 ** (-(np.arange(8) * 2.0 / 16))).astype(np.float32)
    consts[:, C["inv1"]] = np.where(p < 16, inv1[p % 8], 0.0)
    inv2 = np.float32(1) / (np.float32(10000) ** (np.arange(0, 64, 2, dtype=np.float32) / np.float32(64)))
    consts[:, C["inv2"]] = inv2[p % 32]
    for i in range(4):
        consts[:, C["rcount"] + 16 * i:C["rcount"] + 16 * i + 16] = 1.0 / np.minimum(np.arange(16) + 1, 2 << i)
    masks = np.zeros((P, 2 * P + 256), np.float32)
    masks[:, 0:P] = np.eye(P)
    t = np.arange(P)
    masks[:, P:2 * P] = np.where(t[None, :] <= t[:, None], 0.0, MASKED)
    for i in range(NT):
        seen = (16 * np.arange(32) + 31)[None, :] <= (i * P + t)[:, None]
        for u in (i, NT + i):
            masks[:, 2 * P + 32 * u:2 * P + 32 * u + 32] = np.where(seen & (np.arange(32) < N_CMP), 0.0, MASKED)
    masks = masks.astype(ml_dtypes.bfloat16)

    w1 = np.stack([np.concatenate([w.transpose(1, 0, 2)] * 2) for w in g["cmp_w1"][0]])
    w2 = np.stack([np.concatenate([w, w], 1) for w in g["cmp_w2"][0]], 1)
    pool_w = g["pool_w"][0].transpose(1, 0, 2)
    xt = g["x"][0].T.reshape(KD, P, S).transpose(1, 0, 2)
    arrays = {
        "x": xt, "positions": g["positions"][0], "positions2": g["positions_2"][0], "weights": weights, "par1": par1,
        "par2": par2, "consts": consts, "masks": masks, "w1": w1, "w2": w2, "pool_w": pool_w,
    }
    arrays = {k: np.ascontiguousarray(v) for k, v in arrays.items()}
    nc = bacc.Bacc("TRN2", target_bir_lowering=False, num_devices=1)
    args = [nc.dram_tensor(f"in_{k}", v.shape, mybir.dt.from_np(v.dtype), kind="ExternalInput").ap()
            for k, v in arrays.items()]
    out = nc.dram_tensor("out_t", (KD, P, S), F32, kind="ExternalOutput").ap()
    build(nc, *args, out)
    r = run_bass_kernel_spmd(nc, [{f"in_{k}": v for k, v in arrays.items()}], core_ids=[0])
    return r.results[0]["out_t"].reshape(D, S).T.reshape(1, S, D)
```

```python
from contextlib import ExitStack

import numpy as np

import concourse.bass as bass
from concourse import mybir

ALU = mybir.AluOpType
ACT = mybir.ActivationFunctionType
AX = mybir.AxisListType
F32 = mybir.dt.float32
F32R = mybir.dt.float32r
BF16 = mybir.dt.bfloat16
I32 = mybir.dt.int32

P = 128
S = 512
NT = S // P
D = 1024
KD = D // P
FF = 2816
KF = FF // P
CB = 8
DOWN_CHUNKS = -(-KF // CB)
N_CMP = (S - 32) // 16 + 1
LAYERS = 2
EPS = 1e-6
LN_EPS = 1e-5
TAPS = 31
MASKED = -1e30

P1 = {}
_at = 0
for _name, _n in (("mix_g", KD), ("q_g", 1), ("cmp_g", 1), ("sel_g", 1), ("win_g", 1), ("pool_scale", 4),
                  ("ffn_g", KD), ("conv_w", 3 * KF), ("conv_b", KF), ("next_g", KD), ("pe_k", 16), ("pe_v", 16)):
    P1[_name] = _at
    _at += _n
NP1 = _at
P2 = {}
_at = 0
for _name, _n in (("short_w", 6), ("glu_b", 4), ("dw_w", 2 * TAPS), ("dw_b", 2), ("ln_g", 2), ("ln_b", 2),
                  ("sub_g", 1), ("ffn_g", KD), ("next_g", KD), ("lam", 4), ("lam_init", 2)):
    P2[_name] = _at
    _at += _n
NP2 = _at
C = {}
_at = 0
for _name, _n in (("ident", P), ("rot1", P), ("rot2", P), ("ones", P), ("halves", 2), ("inv1", 1), ("inv2", 1),
                  ("rcount", 64)):
    C[_name] = _at
    _at += _n
NC = _at

T_IN, N_IN = 15, 15
T_MIX, N_MIX = 3 * KD, 4 * KD
T_OUT = KD
T_UP = 2 * KF
T_DOWN = DOWN_CHUNKS * KD
T_BLOCK1 = T_IN + T_MIX + T_OUT + T_UP + T_DOWN
N_BLOCK1 = N_IN + N_MIX + T_OUT + T_UP + KD
T_LIN = 22
T_LAYER = T_LIN + T_OUT + T_UP + T_DOWN
N_LAYER = T_LIN + T_OUT + T_UP + KD
T_ALL = T_BLOCK1 + LAYERS * T_LAYER
assert T_LAYER % 2 == 0 and N_LAYER % 2 == 0
U_BLOCK1, U_LAYER = 9, 8
HEAD0 = 7
Y_ORDER = ("head0", "head1", "head2", "ya0", "head3", "ya1", "conv0", "conv1")
NU = 16


class Count:

    def __init__(self, const, terms=()):
        self.const, self.terms = const, tuple(terms)

    def __add__(self, n):
        return Count(self.const + n, self.terms)

    def loop(self, reg, step):
        return Count(self.const, self.terms + ((reg, step),))

    def half(self):
        assert all(s % 2 == 0 for _, s in self.terms)
        return Count(self.const // 2, [(r, s // 2) for r, s in self.terms])

    def even(self):
        assert all(s % 2 == 0 for _, s in self.terms)
        return self.const % 2

    def value(self, times=1):
        v = self.const * times
        for r, s in self.terms:
            v = r * (s * times) + v
        return v

    def low(self):
        return self.const


def layer_slots(n):
    for half in range(2):
        s = 2 * (n - HEAD0) + half
        yield s, [(h, s - 6 * h) for h in (3, 2, 1, 0) if 0 <= s - 6 * h <= 10]


def wait(eng, sem, count, times=1):
    if count.low() > 0:
        eng.wait_ge(sem, count.value(times))


def build(nc, x, positions, positions2, weights, par1, par2, consts, masks, w1, w2, pool_w, out):
    ctx = ExitStack()
    with ctx:
        base = -(-nc.sbuf_base // 64) * 64
        top = [base]

        def at(name, shape, dt, offset):
            return nc.alloc_sbuf_tensor_at(name, list(shape), dt, offset=offset)

        def sb(name, shape, dt=F32):
            size = int(np.prod(shape[1:])) * (2 if dt == BF16 else 4)
            t = at(name, shape, dt, top[0])
            top[0] += -(-size // 64) * 64
            return t

        def sem(name):
            return ctx.enter_context(nc.semaphore(name))

        xs = sb("xs", [P, KD, S])
        xh = sb("xh", [P, KD, S], F32R)
        xl = sb("xl", [P, KD, S], F32R)
        raw = sb("raw", [P, 4 * CB * P])
        wh = sb("wh", [P, 2, CB * P], F32R)
        wl = sb("wl", [P, 2, CB * P], F32R)
        cst = sb("cst", [P, NC])
        msk = sb("msk", [P, 2 * P + 256], BF16)
        pr1 = sb("pr1", [P, NP1])
        pr2 = sb("pr2", [P, LAYERS * NP2])
        par = sb("par", [P, NP2])
        cos = sb("cos", [P, S])
        sin = sb("sin", [P, S])
        cos2 = sb("cos2", [P, S])
        sin2 = sb("sin2", [P, S])
        rstd = sb("rstd", [P, S])
        sqacc = sb("sqacc", [P, S])
        small = sb("small", [P, 192])
        ybuf = sb("ybuf", [P, 2, S])
        BIG = top[0]
        UNIT = 4 * S

        def big(name, unit, shape, dt=F32):
            size = int(np.prod(shape[1:])) * 4
            assert unit * UNIT + size <= 44 * UNIT, name
            return at(name, shape, dt, BIG + unit * UNIT)

        top[0] = BIG + 44 * UNIT
        sq = sb("sq", [P, 2, S])
        tmp = sb("tmp", [P, 2, S])
        tmp2 = sb("tmp2", [P, 528])
        tmp3 = sb("tmp3", [P, 528])
        small2 = sb("small2", [P, 512])
        pairs = sb("pairs", [P, S])
        assert top[0] <= nc.sbuf_usable_end, (top[0], nc.sbuf_usable_end)

        ident = cst[:, C["ident"]:C["ident"] + P]
        rot1 = cst[:, C["rot1"]:C["rot1"] + P]
        rot2 = cst[:, C["rot2"]:C["rot2"] + P]
        ones = cst[:, C["ones"]:C["ones"] + P]
        one = cst[:, C["ones"]:C["ones"] + 1]
        halves = cst[:, C["halves"]:C["halves"] + 2]
        identb = msk[:, 0:P]
        causal = msk[:, P:2 * P]
        cmp_mask = msk[:, 2 * P:2 * P + 256]

        def c1(name, i=0):
            return pr1[:, P1[name] + i:P1[name] + i + 1]

        def c2(name, i=0):
            return par[:, P2[name] + i:P2[name] + i + 1]

        s_root = small[:, 0:8]
        s_recip = small[:, 8:16]
        q_g8 = small[:, 16:17]
        mx8 = small[:, 24:32]
        sum8 = small[:, 32:40]
        fac8 = small[:, 40:48]
        negmx = small[:, 48:64]
        rows = small[:, 64:80]
        rinv = small[:, 80:96]
        lamp = small[:, 96:98]
        lame = small[:, 98:100]
        neglam = small[:, 100:101]
        negmx2 = small[:, 104:112]
        rows2 = small[:, 112:120]
        rinv2 = small[:, 120:128]
        sub_gain = small[:, 128:129]
        gates_t = small2[:, 0:96].rearrange("p (i c) -> p i c", i=NT)
        vct = small2[0:32, 96:224]
        kcf = small2[:, 224:256]
        vcf = small2[:, 256:288]
        kct = small2[:, 288:320]
        csq = small2[:, 320:352]
        cyn = small2[:, 352:384]
        ctm = small2[:, 384:416]
        hid = small2[:, 416:478]

        kvraw = big("kvraw", 0, [P, 2, S])
        kk = big("kk", 2, [P, 2, S])
        vt = big("vt", 4, [P, 2, NT, P])
        qall = big("qall", 6, [P, 4, S])
        qcur = big("qcur", 10, [P, S])
        cmp_p = big("cmp_p", 11, [P, 8, 32])
        cmp_pt = big("cmp_pt", 12, [32, 2, S])
        w2t = big("w2t", 14, [P, 2, P])
        poolw = big("poolw", 15, [P, 4, P])
        w1t = [big("w1k", 16, [P, 16, P]), big("w1v", 20, [P, 16, P])]
        blk = [big("blk_k", 24, [P, 16, 2, N_CMP]), big("blk_v", 28, [P, 16, 2, N_CMP])]
        shifted = big("shifted", 36, [P, 2, 2, 16 * N_CMP])
        probs = big("probs", 16, [P, 4, S])
        pt = big("pt", 20, [P, 2, NT, S])
        poh = big("poh", 28, [P, 4, S], F32R)
        pol = big("pol", 32, [P, 4, S], F32R)
        nh = big("nh", 36, [P, 4, S], F32R)
        nl = big("nl", 40, [P, 4, S], F32R)
        mh = big("mh", 0, [P, KD, S], F32R)
        ml = big("ml", 8, [P, KD, S], F32R)
        hh = big("hh", 0, [P, KF, S], F32R)
        hl = big("hl", KF, [P, KF, S], F32R)
        cpad = big("cpad", 0, [P, 2, TAPS - 1 + S])
        conv = big("conv", 3, [P, 2, S])
        ya = big("ya", 5, [P, 2, S])
        acp = big("acp", 7, [P, 2 + S])
        lv = big("lv", 9, [P, 4, NT, P])
        lq = big("lq", 13, [P, 2, S])
        lk = big("lk", 15, [P, 2, S])
        lp = big("lp", 17, [P, 2, 2, S])
        lpt = big("lpt", 21, [P, NT, S])
        lo_ = big("lo_", 25, [P, 2, S])
        yh = big("yh", 28, [P, KD, S], F32R)
        yl = big("yl", 36, [P, KD, S], F32R)
        ca = big("ca", 36, [P, 2, S])
        cg = big("cg", 38, [P, 2, S])
        posi = big("posi", 6, [P, S], I32)
        posf = big("posf", 7, [P, S])
        ang = big("ang", 8, [P, S])
        turns = big("turns", 9, [P, S])
        red = big("red", 10, [P, S])
        posi2 = big("posi2", 11, [P, S], I32)
        posf2 = big("posf2", 12, [P, S])
        ang2 = big("ang2", 13, [P, S])
        turns2 = big("turns2", 32, [P, S])
        red2 = big("red2", 33, [P, S])

        bank = [ctx.enter_context(nc.psum_tensor(f"bank{i}", [P, S], F32)) for i in range(8)]
        G = bank[0:2]
        ROT, POOLB, TR, STAT, BC, OUT = bank[2], bank[3], bank[4], bank[5], bank[6], bank[7]

        stored = [sem(f"stored{i}") for i in range(2)]
        raw_landed = [sem(f"raw_landed{i}") for i in range(2)]
        x_landed = [sem(f"x_landed{i}") for i in range(2)]
        gains_landed = sem("gains_landed")
        par_landed = sem("par_landed")
        late_landed = sem("late_landed")
        shift_landed = sem("shift_landed")
        hi_ready = sem("hi_ready")
        lo_ready = sem("lo_ready")
        chunk_done = sem("chunk_done")
        tile_out = sem("tile_out")
        xh_ready = sem("xh_ready")
        xl_ready = sem("xl_ready")
        stat_ready = sem("stat_ready")
        root_ready = sem("root_ready")
        recip_ready = sem("recip_ready")
        bc_ready = sem("bc_ready")
        bc_read = sem("bc_read")
        sq_ready = sem("sq_ready")
        rot_in = sem("rot_in")
        rot_ready = sem("rot_ready")
        rot_read = sem("rot_read")
        tr_ready = sem("tr_ready")
        tr_read = sem("tr_read")
        sine_done = sem("sine_done")
        ready = {n: sem(n) for n in (
            "tables", "blk_ready", "hid_psum", "hid_ready", "cmp_psum", "cmp_copied", "vct_psum", "vct_ready",
            "pool_in", "pool_psum", "pool_hi", "pool_lo",
            "q_cur", "s_psum", "max_ready", "exp_ready", "p_ready", "pt_psum", "pt_ready", "pv_done", "o_psum",
            "o_hi", "o_lo", "c_psum", "c_sub", "c_exp", "c_probs", "c_tpsum", "c_tready",
            "mix_sig", "mix_sum", "mix_hi", "mix_lo",
            "conv_ready", "silu_ready", "prod_ready", "h_hi", "h_lo",
            "lam_in", "lam_psum", "lam_exp", "lam_ready", "glu_sig", "conv_done",
            "qk_ready", "head_normed", "ya_ready", "ln_sub", "ln_sq", "ln_scaled", "yc_ready", "y_hi", "y_lo",
            "zeroed", "out_ready", "par_ready")}
        R = ready
        block = ctx.enter_context(nc.Block())

        def cols(start, n):
            return slice(start, start + n) if isinstance(start, int) else bass.ds(start, n)

        def raw_slot(t):
            v = t.value()
            return raw[:, cols((v % 4) * (CB * P), CB * P)]

        t0 = Count(0)

        @block.sync
        def _(sp):
            sp.dma_start(pr1[:, :], par1).then_inc(gains_landed, 16)
            for i in range(2):
                half = slice(i * KD // 2, (i + 1) * KD // 2)
                sp.dma_start(xs[:, half, :], x[:, half, :]).then_inc(x_landed[i], 16)
            for t in range(2):
                sp.dma_start(raw[:, t * CB * P:(t + 1) * CB * P], weights[t]).then_inc(raw_landed[t], 16)
            sp.dma_start(cst[:, :], consts).then_inc(par_landed, 16)
            sp.dma_start(posi[:, :], positions.partition_broadcast(P)).then_inc(par_landed, 16)

            def load(t, source):
                sp.wait_ge(raw_landed[t % 2], 16 * (t // 2))
                if t >= 4:
                    sp.wait_ge(lo_ready, t - 3)
                sp.dma_start(raw[:, (t % 4) * CB * P:(t % 4 + 1) * CB * P], weights[source])\
                    .then_inc(raw_landed[t % 2], 16)

            load(2, 2)
            load(3, 3)
            for c in range(2):
                sp.dma_start(w1t[c][:, :, :], w1[c]).then_inc(late_landed, 16)
            sp.dma_start(posi2[:, :], positions2.partition_broadcast(P)).then_inc(late_landed, 16)
            sp.dma_start(pr2[:, :], par2).then_inc(late_landed, 16)
            sp.dma_start(msk[:, :], masks).then_inc(late_landed, 16)
            sp.dma_start(w2t[:, :, :], w2).then_inc(late_landed, 16)
            sp.dma_start(poolw[:, :, :], pool_w).then_inc(late_landed, 16)
            for t in range(4, 8):
                load(t, t)
            for c in range(2):
                sp.wait_ge(tile_out, c + 1)
                for g in range(2):
                    for half in range(2):
                        sp.dma_start(shifted[half * 64:(half + 1) * 64, c, g, :],
                                     kvraw[g * 64:(g + 1) * 64, c, 16 * half:16 * half + 16 * N_CMP])\
                            .then_inc(shift_landed, 16)
            trips = (T_ALL - 8) // 4
            with sp.Fori(0, trips) as r:
                for c in range(4):
                    t = Count(8 + c).loop(r, 4)
                    chunk, landed, split = t.value(), t.half().value(16), (t + -3).value()
                    for v in (landed, split, chunk * (P * CB * P) * 4):
                        sp.compute_val(v)
                    src = weights[bass.ds(chunk, 1), :, :].rearrange("o p c -> (o p) c")
                    sp.wait_ge(raw_landed[c % 2], landed)
                    sp.wait_ge(lo_ready, split)
                    sp.dma_start(raw[:, c * CB * P:(c + 1) * CB * P], src).then_inc(raw_landed[c % 2], 16)
            for t in range(8 + 4 * trips, T_ALL + 2):
                load(t, t if t < T_ALL else t - T_ALL)
            for m in range(KD):
                sp.wait_ge(R["out_ready"], m + 1)
                sp.dma_start(out[m], ybuf[:, m % 2, :]).then_inc(stored[m % 2], 16)
            for i in range(2):
                sp.wait_ge(stored[i], 16 * (KD // 2))

        @block.gpsimd
        def _(pool):
            def rest(t):
                v = t.value()
                two = cols((v % 2) * (CB * P), CB * P)
                pool.wait_ge(hi_ready, (t + 1).value())
                pool.tensor_tensor(wl[:, :, :].rearrange("p s n -> p (s n)")[:, two], raw_slot(t),
                                   wh[:, :, :].rearrange("p s n -> p (s n)")[:, two].bitcast(F32),
                                   ALU.subtract).then_inc(lo_ready, 1)

            with pool.Fori(0, T_ALL + 2) as t:
                rest(Count(0).loop(t, 1))

        @block.tensor
        def _(pe):
            mm = pe.matmul

            def tile(t, n, kh, kl, blocks=CB, blk0=0, first=True, last=True, count=True, feed=None, mid=None,
                     slots=None, feed_sem=None):
                feed_sem = feed_sem or xl_ready
                s, b = t.even(), G[n.even()]
                if first:
                    wait(pe, tile_out, n + -1)
                if blk0 == 0:
                    pe.wait_ge(hi_ready, (t + 1).value())
                early = blocks - 1 if feed is not None else blocks
                for k in range(early):
                    if feed is not None:
                        pe.wait_ge(feed_sem, (feed + (k + 1)).value())
                    w = wh[:, s, (blk0 + k) * P:(blk0 + k + 1) * P]
                    mm(b[:, :], w, kh(k), start=first and k == 0, stop=False)
                    mm(b[:, :], w, kl(k), start=False, stop=False)
                    if slots is not None and k == 3:
                        slots[0]()
                if mid is not None and early == blocks:
                    mid()
                if blk0 == 0:
                    pe.wait_ge(lo_ready, (t + 1).value())
                if early < blocks:
                    k = early
                    for j in range(early):
                        mm(b[:, :], wl[:, s, j * P:(j + 1) * P], kh(j), start=False, stop=False)
                    pe.wait_ge(feed_sem, (feed + blocks).value())
                    mm(b[:, :], wh[:, s, k * P:(k + 1) * P], kh(k), start=False, stop=False)
                    mm(b[:, :], wh[:, s, k * P:(k + 1) * P], kl(k), start=False, stop=False)
                    mm(b[:, :], wl[:, s, k * P:(k + 1) * P], kh(k), start=False, stop=True).then_inc(chunk_done, 1)
                    if mid is not None:
                        mid()
                    return
                for k in range(blocks):
                    i = mm(b[:, :], wl[:, s, (blk0 + k) * P:(blk0 + k + 1) * P], kh(k),
                           start=False, stop=last and k == blocks - 1)
                    if slots is not None and k == 3:
                        slots[1]()
                if count:
                    i.then_inc(chunk_done, 1)

            def xk(t, n, feed=None, mid=None, slots=None):
                tile(t, n, lambda k: xh[:, k, :], lambda k: xl[:, k, :], feed=feed, mid=mid, slots=slots)

            def stats(u, src, cols_, n=P, per=1, tiles=NT, start=lambda i: True):
                for i in range(tiles):
                    lists = src(i)
                    for a, s_ in enumerate(lists):
                        x_ = mm(STAT[0:n, per * i:per * (i + 1)], s_, cols_, start=a == 0, stop=a == len(lists) - 1)
                x_.then_inc(stat_ready, 1)

            def spread(u, src, n=P, tiles=NT, width=S):
                pe.wait_ge(recip_ready, (u + 1).value())
                wait(pe, bc_read, u)
                for i in range(tiles):
                    x_ = pe.transpose(BC[:, i * P:i * P + n], src(i), ident[0:n, 0:n])
                x_.then_inc(bc_ready, 1)

            def x_stats(u, feed):
                pe.wait_ge(xl_ready, (feed + KD).value())
                stats(u, lambda i: [sqacc[:, i * P:(i + 1) * P]], one)

            def x_spread(u):
                spread(u, lambda i: s_recip[:, i:i + 1].to_broadcast([P, P]))

            norm_of = {2: 1, 3: 2, 4: 3, 5: 4, 6: 5, 7: 6}
            rot_of = {n: i for i, n in enumerate((2, 3, 4, 5, 6, 7))}
            tr_of = {8: 0, 9: 1, 10: 2}
            pool_of = {11: 0, 12: 1, 13: 2, 14: 3}

            def head_stats(n):
                u = Count(norm_of[n])
                pe.wait_ge(sq_ready, norm_of[n])
                wait(pe, root_ready, u)
                stats(u, lambda i: [sq[:, 0, i * P:(i + 1) * P]], halves, per=2)

            def head_spread(n):
                spread(Count(norm_of[n]), lambda i: pairs[:, i * P:(i + 1) * P])

            def rotate(n):
                pe.wait_ge(rot_in, rot_of[n] + 1)
                if rot_of[n]:
                    pe.wait_ge(rot_read, rot_of[n])
                mm(ROT[:, :], rot1, tmp[:, rot_of[n] % 2, :], start=True, stop=True).then_inc(rot_ready, 1)

            def turn(n):
                pe.wait_ge(tile_out, n + 1)
                if tr_of[n]:
                    pe.wait_ge(tr_read, tr_of[n])
                for i in range(NT):
                    x_ = pe.transpose(TR[:, i * P:(i + 1) * P], ybuf[:, n % 2, i * P:(i + 1) * P], ident)
                x_.then_inc(tr_ready, 1)

            def pool_mix(i):
                pe.wait_ge(R["pool_in"], i + 1)
                if i:
                    pe.wait_ge(R["pool_lo"], i)
                else:
                    pe.wait_ge(R["hid_ready"], 2)
                mm(POOLB[:, :], poolw[:, 3 - i, :], tmp[:, i % 2, :], start=True, stop=True).then_inc(R["pool_psum"], 1)

            def compress(c):
                pe.wait_ge(R["blk_ready"], c + 1)
                if c:
                    pe.wait_ge(R["hid_ready"], c)
                for l in range(16):
                    x_ = mm(POOLB[:, 0:2 * N_CMP], w1t[c][:, l, :],
                            blk[c][:, l, :, :].rearrange("p g n -> p (g n)"), start=l == 0, stop=l == 15)
                x_.then_inc(R["hid_psum"], 1)

            def compress_out(c):
                pe.wait_ge(R["hid_ready"], c + 1)
                if c:
                    pe.wait_ge(R["cmp_copied"], c)
                mm(STAT[:, 0:2 * N_CMP], w2t[:, c, :], hid, start=True, stop=True).then_inc(R["cmp_psum"], 1)

            def after(n):
                if n == 0:
                    pe.wait_ge(par_landed, 16 * 2)
                    x_stats(Count(0), Count(0))
                if n == 1:
                    x_spread(Count(0))
                if n - 1 in norm_of:
                    head_stats(n - 1)
                if n - 2 in rot_of:
                    rotate(n - 2)
                if n - 1 in tr_of:
                    turn(n - 1)
                if n == 10:
                    pe.wait_ge(late_landed, 16 * 7)
                if n in (10, 11):
                    compress(n - 10)
                if n in (11, 12):
                    compress_out(n - 11)
                if n - 2 in pool_of:
                    pool_mix(pool_of[n - 2])
                if n == 13:
                    pe.wait_ge(sq_ready, 7)
                    pe.wait_ge(R["cmp_copied"], 2)
                    mm(STAT[0:32, 0:2], csq, halves, start=True, stop=True).then_inc(stat_ready, 1)
                if n == 14:
                    pe.wait_ge(recip_ready, 8)
                    pe.wait_ge(bc_read, 7)
                    pe.transpose(BC[:, 0:32], pairs[0:32, 0:P], ident[0:32, 0:32]).then_inc(bc_ready, 1)
                    pe.wait_ge(tr_read, 3)
                    pe.transpose(TR[0:32, 0:P], vcf, ident).then_inc(R["vct_psum"], 1)

            for n in range(N_IN):
                xk(Count(n), Count(n), feed=Count(0) if n == 0 else None, mid=lambda: after(n))
                if n - 1 in norm_of:
                    head_spread(n - 1)
            pe.wait_ge(rot_in, 7)
            pe.wait_ge(rot_read, 6)
            mm(ROT[:, 0:32], rot1, cyn, start=True, stop=True).then_inc(rot_ready, 1)
            pool_mix(2)
            pool_mix(3)
            pe.wait_ge(R["vct_ready"], 1)
            pe.wait_ge(rot_read, 7)

            SB = [G[0], G[1], ROT, POOLB]
            TB = [STAT, BC]
            pe.wait_ge(tile_out, N_IN)
            pe.wait_ge(R["pool_lo"], 4)
            with pe.Fori(0, 4) as j:
                U = Count(0).loop(j, NU)
                J = Count(0).loop(j, 1)
                B4 = Count(0).loop(j, 4)
                pe.wait_ge(R["q_cur"], (J + 1).value())
                for g in range(2):
                    s = (TR, OUT)[g]
                    mm(s[:, 0:P], identb, cmp_mask[:, g * P:(g + 1) * P], start=True, stop=False)
                    for i in range(NT):
                        x_ = mm(s[:, i * 32:(i + 1) * 32], qcur[g * 64:(g + 1) * 64, i * P:(i + 1) * P],
                                kct[g * 64:(g + 1) * 64, :], start=False, stop=i == 3)
                x_.then_inc(R["c_psum"], 1)

                def score(u):
                    g, b, i = u // 8, u // 4 % 2, u % 4
                    pe.wait_ge(R["exp_ready"], (U + (u - 3)).value()) if u >= 4 else None
                    s = SB[u % 4]
                    n = (i + 1) * P
                    mm(s[:, 0:n], qcur[g * 64:(g + 1) * 64, i * P:(i + 1) * P], kk[g * 64:(g + 1) * 64, b, 0:n],
                       start=True, stop=False)
                    mm(s[:, i * P:n], identb, causal, start=False, stop=True).then_inc(R["s_psum"], 1)

                def turn_probs(u):
                    i = u % 4
                    pe.wait_ge(R["p_ready"], (U + (u + 1)).value())
                    if u >= 2:
                        pe.wait_ge(R["pt_ready"], (U + (u - 1)).value())
                    for c in range(i + 1):
                        x_ = pe.transpose(TB[u % 2][:, c * P:(c + 1) * P], probs[:, u % 4, c * P:(c + 1) * P], ident)
                    x_.then_inc(R["pt_psum"], 1)

                def values(w):
                    g, b = w // 2, w % 2
                    pe.wait_ge(R["pt_ready"], (U + (4 * w + 4)).value())
                    for c in range(NT):
                        x_ = mm(OUT[g * 64:(g + 1) * 64, c * P:S], vt[:, b, c, g * 64:(g + 1) * 64],
                                pt[:, w % 2, c, c * P:S], start=b == 0 and c == 0, stop=False)
                    x_.then_inc(R["pv_done"], 1)

                score(0)
                score(1)
                score(2)
                for u in range(NU):
                    if u + 3 < NU:
                        score(u + 3)
                    turn_probs(u)
                    if u == 3:
                        pe.wait_ge(R["c_probs"], (J + 1).value())
                        for g in range(2):
                            for i in range(NT):
                                x_ = pe.transpose(TR[0:32, i * P:(i + 1) * P], cmp_p[:, g * NT + i, :], ident)
                            x_.then_inc(R["c_tpsum"], 1)
                            if g == 0:
                                pe.wait_ge(R["c_tready"], Count(1).loop(j, 2).value())
                    if u % 4 == 0 and u:
                        values(u // 4 - 1)
                        if u == 8:
                            pe.wait_ge(R["c_tready"], Count(2).loop(j, 2).value())
                            mm(OUT[0:64, :], vct[:, 0:64], cmp_pt[:, 0, :], start=False, stop=True)
                values(3)
                mm(OUT[64:P, :], vct[:, 64:P], cmp_pt[:, 1, :], start=False, stop=True).then_inc(R["o_psum"], 1)
                pe.wait_ge(R["o_lo"], (J + 1).value())

            tb, nb = Count(T_IN), Count(N_IN)
            with pe.Fori(0, KD // 2) as r:
                for m in range(2):
                    t, n = (tb + 3 * m).loop(r, 6), (nb + 4 * m).loop(r, 8)
                    xk(t, n)
                    xk(t + 1, n + 1)
                    tile(t + 2, n + 2, lambda k: poh[:, k, :], lambda k: pol[:, k, :], blocks=4, count=False)
                    tile(t + 2, n + 3, lambda k: nh[:, k, :], lambda k: nl[:, k, :], blocks=4, blk0=4)

            def out_and_ffn(tb, nb, ysrc, y_ready, u, feed):
                with pe.Fori(0, KD // 2) as r:
                    for m in range(2):
                        tile((tb + m).loop(r, 2), (nb + m).loop(r, 2), lambda k: ysrc[0][:, k, :],
                             lambda k: ysrc[1][:, k, :], feed=y_ready[1] if m == 0 else None, feed_sem=y_ready[0])
                tb, nb = tb + T_OUT, nb + KD
                xk(tb, nb, feed=feed, mid=lambda: x_stats(u, feed))
                xk(tb + 1, nb + 1, mid=lambda: x_spread(u))
                with pe.Fori(0, KF - 1) as r:
                    xk((tb + 2).loop(r, 2), (nb + 2).loop(r, 2))
                    xk((tb + 3).loop(r, 2), (nb + 3).loop(r, 2))
                tb, nb = tb + T_UP, nb + T_UP
                return tb, nb

            def down(tb, nb, h_lo):
                with pe.Fori(0, KD // 2) as r:
                    for m in range(2):
                        for c in range(DOWN_CHUNKS):
                            k0 = CB * c
                            if m == 0:
                                pe.wait_ge(R["h_lo"], (h_lo + (min(k0 + CB, KF) - KF)).value())
                            tile((tb + (DOWN_CHUNKS * m + c)).loop(r, 2 * DOWN_CHUNKS), (nb + m).loop(r, 2),
                                 lambda k: hh[:, k0 + k, :], lambda k: hl[:, k0 + k, :],
                                 blocks=min(CB, KF - k0), first=c == 0, last=c == DOWN_CHUNKS - 1)

            tb, nb = out_and_ffn(Count(T_IN + T_MIX), Count(N_IN + N_MIX), (mh, ml), (R["mix_lo"], Count(0)),
                                 Count(8), Count(KD))
            down(tb, nb, Count(KF))

            with pe.Fori(0, LAYERS) as l:
                T = Count(T_BLOCK1).loop(l, T_LAYER)
                N = Count(N_BLOCK1).loop(l, N_LAYER)
                U0 = Count(U_BLOCK1).loop(l, U_LAYER)
                feed = Count(2 * KD).loop(l, 2 * KD)
                L1 = Count(1).loop(l, 1)

                def lam_sum():
                    pe.wait_ge(R["lam_in"], L1.value())
                    mm(POOLB[:, 0:2], ones, lamp, start=True, stop=True).then_inc(R["lam_psum"], 1)

                RO = Count(7).loop(l, 8)
                SS = Count(4 * NU).loop(l, 32)
                TT = Count(4 * NU).loop(l, 16)
                OO = Count(4).loop(l, 4)
                SC = (POOLB, TR)

                def turn_v(h):
                    pe.wait_ge(tile_out, (N + (HEAD0 + 3 * h)).value())
                    pe.wait_ge(rot_read, (RO + (2 * h + 2)).value())
                    for c in range(NT):
                        x_ = pe.transpose(ROT[:, c * P:(c + 1) * P], ybuf[:, (HEAD0 - 1 + 3 * h) % 2,
                                                                          c * P:(c + 1) * P], ident)
                    x_.then_inc(tr_ready, 1)

                def rotate_l(i):
                    n = 4 + 3 * (i // 2) + i % 2
                    pe.wait_ge(tile_out, (N + (n + 1)).value())
                    if i % 2:
                        pe.wait_ge(rot_read, (RO + i).value())
                    else:
                        pe.wait_ge(tr_read, Count(3 + i // 2).loop(l, 4).value())
                    mm(ROT[:, :], rot2, ybuf[:, n % 2, :], start=True, stop=True).then_inc(rot_ready, 1)

                def score_l(h, i):
                    n = (i + 1) * P
                    if i == 0:
                        pe.wait_ge(R["qk_ready"], Count(2 * h + 2).loop(l, 8).value())
                        if h == 0:
                            pe.wait_ge(R["lam_exp"], L1.value())
                    for m in range(2):
                        u = 8 * h + 2 * i + m
                        if i or h:
                            pe.wait_ge(R["exp_ready"], (SS + (u - 1)).value())
                        mm(SC[m][:, 0:n], lq[m * 64:(m + 1) * 64, h % 2, i * P:n], lk[m * 64:(m + 1) * 64, h % 2, 0:n],
                           start=True, stop=False)
                        mm(SC[m][:, i * P:n], identb, causal, start=False, stop=True).then_inc(R["s_psum"], 1)

                def turn_l(h, i):
                    pe.wait_ge(R["p_ready"], (TT + (4 * h + i + 1)).value())
                    if i:
                        pe.wait_ge(R["pt_ready"], (TT + (4 * h + i)).value())
                    elif h:
                        pe.wait_ge(R["o_hi"], (OO + h).value())
                    for c in range(i + 1):
                        x_ = pe.transpose(OUT[:, c * P:(c + 1) * P], lp[:, i % 2, 0, c * P:(c + 1) * P], ident)
                    x_.then_inc(R["pt_psum"], 1)

                def values_l(h):
                    pe.wait_ge(R["pt_ready"], (TT + (4 * h + 4)).value())
                    pe.wait_ge(tr_read, Count(4 + h).loop(l, 4).value())
                    for c in range(NT):
                        x_ = mm(OUT[:, c * P:S], lv[:, h, c, :], lpt[:, c, c * P:S], start=c == 0, stop=c == 3)
                    x_.then_inc(R["o_psum"], 1)

                def head_step(h, step):
                    if step < 4:
                        score_l(h, step)
                    if 2 <= step < 6:
                        turn_l(h, step - 2)
                    if step == 6:
                        values_l(h)
                    if step == 7:
                        pe.wait_ge(sq_ready, Count(8 + h).loop(l, 4).value())
                        stats(U0 + (1 + h), lambda i: [sq[:, 0, i * P:(i + 1) * P]], one)
                    if step == 8:
                        spread(U0 + (1 + h), lambda i: s_recip[:, i:i + 1].to_broadcast([P, P]))

                def ln_stats(u, src):
                    stats(u, lambda i: [src[:, c, i * P:(i + 1) * P] for c in range(2)], one)

                def slot(n, half):
                    s, steps = list(layer_slots(n))[half]
                    if half == 0:
                        if n == 1:
                            x_spread(U0)
                            lam_sum()
                        if 5 <= n < 16:
                            h, what = (n - 5) // 3, (n - 5) % 3
                            if what < 2:
                                rotate_l(2 * h + what)
                        if HEAD0 <= n < 17 and (n - HEAD0) % 3 == 0:
                            turn_v((n - HEAD0) // 3)
                    for h, step in steps:
                        head_step(h, step)
                    if s == 26:
                        pe.wait_ge(R["conv_done"], L1.value())
                        ln_stats(U0 + 5, conv)
                    if s == 27:
                        spread(U0 + 5, lambda i: s_recip[:, i:i + 1].to_broadcast([P, P]))
                    if s == 28:
                        pe.wait_ge(R["ln_sq"], L1.value())
                        ln_stats(U0 + 6, sq)
                    if s == 29:
                        spread(U0 + 6, lambda i: s_recip[:, i:i + 1].to_broadcast([P, P]))

                for n in range(T_LIN):
                    if n == 0:
                        xk(T, N, feed=feed, mid=lambda: x_stats(U0, feed))
                    else:
                        xk(T + n, N + n, slots=[lambda: slot(n, 0), lambda: slot(n, 1)])

                tb, nb = out_and_ffn(T + T_LIN, N + T_LIN, (yh, yl), (R["y_lo"], Count(0).loop(l, KD)), U0 + 7,
                                     Count(3 * KD).loop(l, 2 * KD))
                down(tb, nb, Count(2 * KF).loop(l, KF))

            x_stats(Count(U_BLOCK1 + LAYERS * U_LAYER), Count((2 + 2 * LAYERS) * KD))
            x_spread(Count(U_BLOCK1 + LAYERS * U_LAYER))

        @block.scalar
        def _(act):
            def copy(o, i, scale=1.0):
                return act.activation(o, i, ACT.Copy, scale=scale)

            def head(t):
                s = t.even()
                act.wait_ge(raw_landed[s], (t.half() + 1).value(16))
                wait(act, chunk_done, t + -1)
                copy(wh[:, s, :], raw_slot(t)).then_inc(hi_ready, 1)

            def root(u, n, parts=P, scale=1.0, eps=EPS, plain=False):
                act.wait_ge(stat_ready, (u + 1).value())
                wait(act, recip_ready, u)
                o, i = s_root[0:parts, 0:n], STAT[0:parts, 0:n]
                if plain:
                    copy(o, i, scale=scale).then_inc(root_ready, 1)
                else:
                    act.activation(o, i, ACT.Sqrt, scale=scale, bias=eps_ap(eps)[0:parts, :]).then_inc(root_ready, 1)

            def eps_ap(e):
                return small[:, 188:189] if e == EPS else small[:, 189:190]

            def flat(a):
                return a[:, :, :].rearrange("p k n -> p (k n)")

            def feed(m, k, g, n):
                if n is not None:
                    act.wait_ge(tile_out, (n + 1).value())
                wait(act, xl_ready, k + -1)
                copy(flat(xh)[:, cols(m * S, S)], flat(xs)[:, cols(m * S, S)], scale=g)
                act.activation(sq[:, k.even(), :], flat(xs)[:, cols(m * S, S)], ACT.Square).then_inc(xh_ready, 1)

            act.wait_ge(R["zeroed"], 1)
            act.wait_ge(gains_landed, 16)
            for m in range(KD):
                if m % (KD // 2) == 0:
                    act.wait_ge(x_landed[m // (KD // 2)], 16)
                feed(m, Count(m), c1("mix_g", m), None)
                if m in (1, 3):
                    head(Count(m // 2))
            root(Count(0), NT, scale=1.0 / D)

            def sine(i):
                o, a = ((sin, red), (cos, red), (sin2, red2), (cos2, red2))[i]
                act.wait_ge(R["tables"], i + 1)
                act.activation(o[:, :], a[:, :], ACT.Sin).then_inc(sine_done, 1)

            def pool_head(i):
                g = 3 - i
                act.wait_ge(R["pool_psum"], i + 1)
                copy(poh[:, g, :], POOLB[:, :], scale=c1("pool_scale", g)).then_inc(R["pool_hi"], 1)

            def hidden_cmp(c):
                act.wait_ge(R["hid_psum"], c + 1)
                if c:
                    act.wait_ge(R["cmp_psum"], c)
                act.activation(hid, POOLB[:, 0:2 * N_CMP], ACT.Silu).then_inc(R["hid_ready"], 1)

            for n in range(N_IN):
                act.wait_ge(chunk_done, n + 1)
                head(Count(n + 2))
                act.wait_ge(tile_out, n + 1)
                if 2 <= n < 8:
                    act.activation(sq[:, 0, :], ybuf[:, n % 2, :], ACT.Square).then_inc(sq_ready, 1)
                    root(Count(n - 1), 8, scale=1.0 / 64)
                if 8 <= n < 10:
                    act.wait_ge(tr_ready, n - 7)
                    copy(vt[:, n - 8, :, :].rearrange("p i d -> p (i d)"), TR[:, :]).then_inc(tr_read, 1)
                if n == 10:
                    act.wait_ge(tr_ready, 3)
                    act.activation(gates_t, TR[:, :].rearrange("p (i c) -> p i c", i=NT)[:, :, 0:24],
                                   ACT.Sigmoid).then_inc(tr_read, 1)
                if n in (0, 1):
                    sine(n)
                if n in (10, 11):
                    hidden_cmp(n - 10)
                if n in (9, 10):
                    sine(n - 7)
                if n == 12:
                    act.wait_ge(R["cmp_copied"], 1)
                    act.activation(csq, kcf, ACT.Square).then_inc(sq_ready, 1)
                if n == 13:
                    root(Count(7), 2, parts=32, scale=1.0 / 64)
                if n >= 13:
                    pool_head(n - 13)
            act.wait_ge(R["vct_psum"], 1)
            copy(vct, TR[0:32, 0:P]).then_inc(R["vct_ready"], 1)
            pool_head(2)
            pool_head(3)

            TB = [STAT, BC]
            SB = [G[0], G[1], ROT, POOLB]
            with act.Fori(0, 4) as j:
                U = Count(0).loop(j, NU)
                J = Count(0).loop(j, 1)

                def exps(u):
                    n = (u % 4 + 1) * P
                    act.wait_ge(R["max_ready"], (U + (u + 1)).value())
                    if u >= 4:
                        act.wait_ge(R["pt_psum"], (U + (u - 3)).value())
                    act.activation(probs[:, u % 4, 0:n], SB[u % 4][:, 0:n], ACT.Exp, bias=negmx[:, u:u + 1],
                                   accum_out=rows[:, u:u + 1]).then_inc(R["exp_ready"], 1)

                def put(u):
                    i, w = u % 4, u // 4
                    act.wait_ge(R["pt_psum"], (U + (u + 1)).value())
                    if w >= 2 and i == 0:
                        act.wait_ge(R["pv_done"], Count(w - 1).loop(j, 4).value())
                    copy(pt[:, w % 2, 0:i + 1, i * P:(i + 1) * P],
                         TB[u % 2][:, 0:(i + 1) * P].rearrange("p (c q) -> p c q", q=P)).then_inc(R["pt_ready"], 1)

                for u in range(NU + 2):
                    if u < NU:
                        exps(u)
                    if u == 1:
                        act.wait_ge(R["c_sub"], (J + 1).value())
                        act.activation(cmp_p[:, :, :], cmp_p[:, :, :], ACT.Exp).then_inc(R["c_exp"], 1)
                    if u >= 2:
                        put(u - 2)
                    if u == 5:
                        for g in range(2):
                            act.wait_ge(R["c_tpsum"], Count(g + 1).loop(j, 2).value())
                            copy(cmp_pt[:, g, :], TR[0:32, :]).then_inc(R["c_tready"], 1)
                act.wait_ge(R["o_psum"], (J + 1).value())
                copy(nh[:, :, :].rearrange("p k n -> p (k n)")[:, bass.ds(j * S, S)], OUT[:, :])\
                    .then_inc(R["o_hi"], 1)

            with act.Fori(0, KD // 2) as r:
                for m in range(2):
                    t = Count(T_IN + 3 * m).loop(r, 6)
                    K = Count(m).loop(r, 2)
                    for c in range(3):
                        act.wait_ge(chunk_done, (t + (c + 1)).value())
                        head(t + (c + 2))
                        if c < 2:
                            act.wait_ge(tile_out, Count(N_IN + 4 * m + c + 1).loop(r, 8).value())
                            act.activation(ybuf[:, c, :], ybuf[:, c, :], ACT.Sigmoid).then_inc(R["mix_sig"], 1)
                    act.wait_ge(R["mix_sum"], (K + 1).value())
                    copy(mh[:, :, :].rearrange("p k n -> p (k n)")[:, bass.ds(K.value() * S, S)], tmp2[:, 0:S])\
                        .then_inc(R["mix_hi"], 1)

            def out_and_ffn(t, n, u, feed0, gain, h0, first_block):
                with act.Fori(0, KD // 2) as r:
                    for m in range(2):
                        tt = (t + m).loop(r, 2)
                        act.wait_ge(chunk_done, (tt + 1).value())
                        head(tt + 2)
                    for m in range(2):
                        feed(r * 2 + m, (feed0 + m).loop(r, 2), gain("ffn_g", r, m), (n + m).loop(r, 2))
                t, n = t + T_OUT, n + KD
                act.wait_ge(chunk_done, (t + 1).value())
                root(u, NT, scale=1.0 / D)
                head(t + 2)
                act.wait_ge(chunk_done, (t + 2).value())
                head(t + 3)

                hidden(n, h0, 0, first_block)
                with act.Fori(1, KF) as r:
                    for c in range(2):
                        act.wait_ge(chunk_done, (t + (c + 1)).loop(r, 2).value())
                        head((t + (c + 2)).loop(r, 2))
                    hidden(n.loop(r, 2), h0.loop(r, 1), r, first_block)
                return t + T_UP, n + T_UP

            def hidden(n, k, j, first_block):
                if first_block:
                    act.wait_ge(R["conv_ready"], (k + 1).value())
                else:
                    act.wait_ge(tile_out, (n + 1).value())
                act.activation(tmp[:, 0, :], tmp[:, 0, :], ACT.Silu).then_inc(R["silu_ready"], 1)
                act.wait_ge(R["prod_ready"], (k + 1).value())
                copy(flat(hh)[:, cols(j * S, S)], tmp[:, 1, :]).then_inc(R["h_hi"], 1)

            def down(t, n, feed0, gain):
                with act.Fori(0, KD // 2) as r:
                    for c in range(2 * DOWN_CHUNKS):
                        tt = (t + c).loop(r, 2 * DOWN_CHUNKS)
                        act.wait_ge(chunk_done, (tt + 1).value())
                        head(tt + 2)
                        if c == DOWN_CHUNKS:
                            feed(r * 2, feed0.loop(r, 2), gain("next_g", r, 0), n.loop(r, 2))
                    feed(r * 2 + 1, (feed0 + 1).loop(r, 2), gain("next_g", r, 1), (n + 1).loop(r, 2))

            def gain1(name, r, m):
                return pr1[:, bass.ds(r * 2 + (P1[name] + m), 1)]

            def gain2(name, r, m):
                return par[:, bass.ds(r * 2 + (P2[name] + m), 1)]

            t, n = out_and_ffn(Count(T_IN + T_MIX), Count(N_IN + N_MIX), Count(8), Count(KD), gain1, Count(0), True)
            down(t, n, Count(2 * KD), gain1)

            with act.Fori(0, LAYERS) as l:
                T = Count(T_BLOCK1).loop(l, T_LAYER)
                N = Count(N_BLOCK1).loop(l, N_LAYER)
                U0 = Count(U_BLOCK1).loop(l, U_LAYER)
                L1 = Count(1).loop(l, 1)
                act.wait_ge(R["par_ready"], L1.value())
                SS = Count(4 * NU).loop(l, 32)
                TT = Count(4 * NU).loop(l, 16)
                SC = (POOLB, TR)
                Y = Count(0).loop(l, KD)

                def exps(h, i):
                    n = (i + 1) * P
                    for m in range(2):
                        u = 2 * i + m
                        act.wait_ge(R["max_ready"], (SS + (8 * h + u + 1)).value())
                        act.activation(lp[:, i % 2, m, 0:n], SC[m][:, 0:n], ACT.Exp, bias=negmx2[:, u:u + 1],
                                       accum_out=rows2[:, u:u + 1]).then_inc(R["exp_ready"], 1)

                def put(h, i):
                    act.wait_ge(R["pt_psum"], (TT + (4 * h + i + 1)).value())
                    copy(lpt[:, 0:i + 1, i * P:(i + 1) * P],
                         OUT[:, 0:(i + 1) * P].rearrange("p (c q) -> p c q", q=P)).then_inc(R["pt_ready"], 1)

                def y_head(name, src):
                    copy(yh[:, Y_ORDER.index(name), :], src).then_inc(R["y_hi"], 1)

                def head_step(h, step):
                    if 2 <= step < 6:
                        put(h, step - 2)
                    if step < 4:
                        exps(h, step)
                    if step == 6:
                        act.wait_ge(R["o_psum"], Count(5 + h).loop(l, 4).value())
                        copy(lo_[:, h % 2, :], OUT[:, :]).then_inc(R["o_hi"], 1)
                        act.activation(sq[:, 0, :], OUT[:, :], ACT.Square).then_inc(sq_ready, 1)
                    if step == 7:
                        root(U0 + (1 + h), NT, scale=1.0 / P)
                    if step == 9:
                        act.wait_ge(R["head_normed"], Count(h + 1).loop(l, 4).value())
                        y_head(f"head{h}", lo_[:, h % 2, :])

                for n in range(T_LIN):
                    for s, steps in layer_slots(n):
                        if n == 1 and s % 2 == 0:
                            act.wait_ge(R["lam_psum"], L1.value())
                            act.activation(lame, POOLB[:, 0:2], ACT.Exp).then_inc(R["lam_exp"], 1)
                        if HEAD0 <= n < 17 and (n - HEAD0) % 3 == 0 and s % 2 == 0:
                            h = (n - HEAD0) // 3
                            act.wait_ge(tr_ready, Count(4 + h).loop(l, 4).value())
                            copy(lv[:, h, :, :].rearrange("p c d -> p (c d)"), ROT[:, :]).then_inc(tr_read, 1)
                        for h, step in steps:
                            head_step(h, step)
                        if s == 24:
                            act.wait_ge(R["ya_ready"], Count(1).loop(l, 2).value())
                            y_head("ya0", ya[:, 0, :])
                        if s == 26:
                            root(U0 + 5, NT, scale=1.0 / 256, plain=True)
                        if s == 28:
                            act.wait_ge(R["ln_sub"], L1.value())
                            act.activation(sq[:, :, :], conv[:, :, :], ACT.Square).then_inc(R["ln_sq"], 1)
                            root(U0 + 6, NT, scale=1.0 / 256, eps=LN_EPS)
                    act.wait_ge(chunk_done, (T + (n + 1)).value())
                    if n == 0:
                        root(U0, NT, scale=1.0 / D)
                    head(T + (n + 2))
                    if n in (2, 3):
                        act.wait_ge(tile_out, (N + (n + 1)).value())
                        act.activation(cg[:, n - 2, :], cg[:, n - 2, :], ACT.Sigmoid, bias=c2("glu_b", n))\
                            .then_inc(R["glu_sig"], 1)
                act.wait_ge(R["ya_ready"], Count(2).loop(l, 2).value())
                y_head("ya1", ya[:, 1, :])
                for c in range(2):
                    act.wait_ge(R["ln_scaled"], Count(c + 1).loop(l, 2).value())
                    act.activation(conv[:, c, :], conv[:, c, :], ACT.Silu, bias=c2("ln_b", c)).then_inc(R["yc_ready"], 1)
                    act.wait_ge(R["yc_ready"], Count(c + 1).loop(l, 2).value())
                    y_head(f"conv{c}", conv[:, c, :])
                t, n = out_and_ffn(T + T_LIN, N + T_LIN, U0 + 7, Count(3 * KD).loop(l, 2 * KD), gain2,
                                   Count(KF).loop(l, KF), False)
                down(t, n, Count(4 * KD).loop(l, 2 * KD), gain2)
            root(Count(U_BLOCK1 + LAYERS * U_LAYER), NT, scale=1.0 / D)

        @block.vector
        def _(dve):
            tt, ts, stt = dve.tensor_tensor, dve.tensor_scalar, dve.scalar_tensor_tensor

            def fma(o, a, s, b):
                return stt(out=o, in0=a, scalar=s, in1=b, op0=ALU.mult, op1=ALU.add)

            def mul3(o, a, s, b):
                return stt(out=o, in0=a, scalar=s, in1=b, op0=ALU.mult, op1=ALU.mult)

            flat = lambda a: a[:, :, :].rearrange("p k n -> p (k n)")

            def tile_of(a, m):
                return a[:, m, :] if isinstance(m, int) else flat(a)[:, bass.ds(m * S, S)]

            def feed(m, k, g):
                dve.wait_ge(xh_ready, (k + 1).value())
                stt(out=tile_of(xl, m), in0=tile_of(xs, m), scalar=g, in1=tile_of(xh, m).bitcast(F32),
                    op0=ALU.mult, op1=ALU.subtract)
                tt(sqacc[:, :], sqacc[:, :], sq[:, k.even(), :], ALU.add).then_inc(xl_ready, 1)

            def recips(u, n, parts=P, plain=False):
                dve.wait_ge(root_ready, (u + 1).value())
                o, i = s_recip[0:parts, 0:n], s_root[0:parts, 0:n]
                (dve.tensor_copy(o, i) if plain else dve.reciprocal(o, i)).then_inc(recip_ready, 1)

            def pair_recips(u, n, parts=P):
                dve.wait_ge(root_ready, (u + 1).value())
                dve.reciprocal(s_recip[0:parts, 0:n], s_root[0:parts, 0:n])
                dve.drain()
                dve.tensor_copy(pairs[0:parts, 0:64 * n].rearrange("p (u d) -> p u d", d=64),
                                s_recip[0:parts, 0:n].unsqueeze(2).to_broadcast([parts, n, 64])).then_inc(recip_ready, 1)

            def x_norm(u):
                recips(u, NT)
                dve.wait_ge(bc_ready, (u + 1).value())
                dve.tensor_copy(rstd[:, :], BC[:, :]).then_inc(bc_read, 1)
                dve.memset(sqacc[:, :], 0.0)
                dve.drain()

            def take(t, n, o, scale=None):
                dve.wait_ge(chunk_done, (t + 1).value())
                b = G[n.even()]
                if scale is None:
                    return tt(o, b[:, :], rstd[:, :], ALU.mult).then_inc(tile_out, 1)
                return mul3(o, b[:, :], scale, rstd[:, :]).then_inc(tile_out, 1)

            def tables(src, pf, an, tu, rd, inv, first):
                two_pi = 2.0 * np.pi
                c1_ = 6.28125
                c2_ = float(np.float32(np.round((two_pi - c1_) * 2 ** 18) / 2 ** 18))
                c3_ = float(two_pi - c1_ - c2_)
                magic = 1.5 * 2 ** 23
                lim = 3.1415925
                for c in range(2):
                    if c == 0:
                        dve.tensor_copy(pf[:, :], src[:, :])
                        dve.drain()
                        ts(an[:, :], pf[:, :], inv, None, ALU.mult)
                    else:
                        yield
                    dve.drain()
                    ts(tu[:, :], an[:, :], 1.0 / two_pi, 0.25 * c, ALU.mult, ALU.add)
                    dve.drain()
                    ts(tu[:, :], tu[:, :], magic, magic, ALU.add, ALU.subtract)
                    if c:
                        dve.wait_ge(sine_done, first + 1)
                    dve.drain()
                    fma(rd[:, :], tu[:, :], -c1_, an[:, :])
                    dve.drain()
                    fma(rd[:, :], tu[:, :], -c2_, rd[:, :])
                    dve.drain()
                    fma(rd[:, :], tu[:, :], -c3_, rd[:, :])
                    dve.drain()
                    ts(rd[:, :], rd[:, :], float(np.pi / 2) * c, lim, ALU.add, ALU.min)
                    dve.drain()
                    ts(rd[:, :], rd[:, :], -lim, None, ALU.max).then_inc(R["tables"], 1)
                yield

            dve.memset(small[:, :], 0.0)
            dve.memset(small2[:, :], 0.0)
            dve.memset(sqacc[:, :], 0.0)
            dve.drain()
            dve.memset(small[:, 188:189], EPS)
            dve.memset(small[:, 189:190], LN_EPS)
            dve.drain()
            dve.memset(tmp2[:, :], 0.0).then_inc(R["zeroed"], 1)
            dve.wait_ge(gains_landed, 16)
            for m in range(KD):
                if m % (KD // 2) == 0:
                    dve.wait_ge(x_landed[m // (KD // 2)], 16)
                dve.drain()
                feed(m, Count(m), c1("mix_g", m))
            ts(q_g8, c1("q_g"), 0.125, None, ALU.mult)
            x_norm(Count(0))
            dve.wait_ge(par_landed, 32)
            tables1 = tables(posi, posf, ang, turns, red, cst[:, C["inv1"]:C["inv1"] + 1], 0)
            tables2 = tables(posi2, posf2, ang2, turns2, red2, cst[:, C["inv2"]:C["inv2"] + 1], 2)

            def normed(n, gain):
                i = n - 2
                dve.wait_ge(bc_ready, n)
                mul3(tmp[:, i % 2, :], ybuf[:, n % 2, :], gain, BC[:, :]).then_inc(bc_read, 1)
                dve.drain()
                tt(tmp3[:, 0:S], tmp[:, i % 2, :], cos[:, :], ALU.mult).then_inc(rot_in, 1)

            def rotated(i, dst):
                dve.wait_ge(rot_ready, i + 1)
                tt(tmp2[:, 0:S], ROT[:, :], sin[:, :], ALU.mult).then_inc(rot_read, 1)
                dve.drain()
                tt(dst, tmp2[:, 0:S], tmp3[:, 0:S], ALU.add)

            dsts = [kk[:, 0, :], kk[:, 1, :]] + [qall[:, c, :] for c in range(4)]
            gains = [c1("sel_g"), c1("win_g")] + [q_g8] * 4

            def pooled(i):
                g = 3 - i
                w = 2 << g
                y = ybuf[:, (11 + i) % 2, :]
                dve.memset(tmp2[:, 0:16], 0.0)
                dve.memset(tmp3[:, 0:16], 0.0)
                dve.tensor_copy(tmp2[:, 16:528], y)
                a, b, w_ = tmp2, tmp3, 1
                while w_ < w:
                    dve.drain()
                    tt(b[:, 16:528], a[:, 16:528], a[:, 16 - w_:528 - w_], ALU.add)
                    a, b, w_ = b, a, 2 * w_
                dve.drain()
                if i >= 2:
                    dve.wait_ge(R["pool_psum"], i - 1)
                stt(out=tmp[:, i % 2, :], in0=a[:, 16:528], scalar=1.0 / w, in1=y, op0=ALU.mult, op1=ALU.subtract)
                tt(small2[:, 480:496], a[:, 16:32], cst[:, C["rcount"] + 16 * g:C["rcount"] + 16 * g + 16], ALU.mult)
                dve.drain()
                tt(tmp[:, i % 2, 0:16], small2[:, 480:496], y[:, 0:16], ALU.subtract).then_inc(R["pool_in"], 1)

            def pool_rest(i):
                g = 3 - i
                dve.wait_ge(R["pool_hi"], i + 1)
                stt(out=pol[:, g, :], in0=POOLB[:, :], scalar=c1("pool_scale", g), in1=poh[:, g, :].bitcast(F32),
                    op0=ALU.mult, op1=ALU.subtract).then_inc(R["pool_lo"], 1)

            def blocks(c, pe_name):
                e = pr1[:, P1[pe_name]:P1[pe_name] + 16].unsqueeze(2).to_broadcast([P, 16, N_CMP])
                for g in range(2):
                    x_ = tt(blk[c][:, :, g, :], shifted[:, c, g, :].rearrange("p (b l) -> p l b", l=16), e, ALU.add)
                x_.then_inc(R["blk_ready"], 1)

            def key_cmp():
                dve.wait_ge(bc_ready, 8)
                mul3(cyn[:, 0:32], kcf, c1("cmp_g"), BC[:, 0:32]).then_inc(bc_read, 1)
                dve.drain()
                ends = lambda a: a[:, 16:S].rearrange("p (b l) -> p b l", l=16)[:, :, 15]
                tt(ctm[:, 0:31], cyn[:, 0:31], ends(cos), ALU.mult).then_inc(rot_in, 1)
                dve.wait_ge(rot_ready, 7)
                tt(csq[:, 0:31], ROT[:, 0:31], ends(sin), ALU.mult)
                dve.drain()
                tt(kct[:, 0:31], csq[:, 0:31], ctm[:, 0:31], ALU.add).then_inc(rot_read, 1)

            def copy_cmp(c):
                dve.wait_ge(R["cmp_psum"], c + 1)
                for g in range(2):
                    x_ = dve.tensor_copy((kcf, vcf)[c][g * 64:(g + 1) * 64, 0:31],
                                         STAT[g * 64:(g + 1) * 64, g * 31:g * 31 + 31])
                x_.then_inc(R["cmp_copied"], 1)

            for n in range(N_IN):
                if 2 <= n - 1 < 8:
                    pair_recips(Count(n - 2), 8)
                take(Count(n), Count(n), kvraw[:, n, :] if n < 2 else ybuf[:, n % 2, :])
                if 2 <= n - 2 < 8:
                    rotated(n - 4, dsts[n - 4])
                if 2 <= n - 1 < 8:
                    normed(n - 1, gains[n - 3])
                if n < 2:
                    next(tables1)
                if n == 2:
                    dve.wait_ge(sine_done, 2)
                if n == 9:
                    dve.wait_ge(shift_landed, 8 * 16)
                    blocks(0, "pe_k")
                    blocks(1, "pe_v")
                if n in (9, 10):
                    dve.wait_ge(late_landed, 16 * 7)
                    next(tables2)
                if n == 14:
                    key_cmp()
                if n >= 11:
                    dve.drain()
                    pooled(n - 11)
                if n in (11, 12):
                    copy_cmp(n - 11)
                if n >= 13:
                    pool_rest(n - 13)
                if n == 13:
                    pair_recips(Count(7), 2, parts=32)
            pool_rest(2)
            pool_rest(3)
            dve.wait_ge(sine_done, 4)
            dve.drain()

            SB = [G[0], G[1], ROT, POOLB]
            with dve.Fori(0, 4) as j:
                U = Count(0).loop(j, NU)
                J = Count(0).loop(j, 1)
                dve.tensor_copy(qcur[:, :], flat(qall)[:, bass.ds(j * S, S)]).then_inc(R["q_cur"], 1)
                dve.wait_ge(R["c_psum"], (J + 1).value())
                sc = [b[:, 0:P].rearrange("p (u n) -> p u n", n=32) for b in (TR, OUT)]
                for g in range(2):
                    dve.tensor_reduce(mx8[:, 4 * g:4 * g + 4], sc[g], AX.X, ALU.max)
                dve.drain()
                ts(mx8, mx8, MASKED / 1e5, None, ALU.max)
                dve.drain()
                for g in range(2):
                    x_ = tt(cmp_p[:, 4 * g:4 * g + 4, :], sc[g],
                            mx8[:, 4 * g:4 * g + 4].unsqueeze(2).to_broadcast([P, 4, 32]), ALU.subtract)
                x_.then_inc(R["c_sub"], 1)

                def top(u):
                    dve.wait_ge(R["s_psum"], (U + (u + 1)).value())
                    dve.tensor_reduce(negmx[:, u:u + 1], SB[u % 4][:, 0:(u % 4 + 1) * P], AX.X, ALU.max, negate=True)\
                        .then_inc(R["max_ready"], 1)

                def scale(u):
                    g, b, i = u // 8, u // 4 % 2, u % 4
                    n = (i + 1) * P
                    dve.wait_ge(R["exp_ready"], (U + (u + 1)).value())
                    dve.reciprocal(rinv[:, u:u + 1], rows[:, u:u + 1])
                    dve.drain()
                    ts(probs[:, u % 4, 0:n], probs[:, u % 4, 0:n], rinv[:, u:u + 1],
                       small2[:, bass.ds(j * 6 + (24 * i + 3 * g + 1 + b), 1)], ALU.mult, ALU.mult)\
                        .then_inc(R["p_ready"], 1)

                for u in range(NU + 2):
                    if u < NU:
                        top(u)
                    if u >= 2:
                        scale(u - 2)
                    if u == 2:
                        dve.wait_ge(R["c_exp"], (J + 1).value())
                        dve.tensor_reduce(sum8, cmp_p[:, :, :], AX.X, ALU.add)
                        dve.drain()
                        ts(sum8, sum8, 1e-30, None, ALU.max)
                        dve.drain()
                        dve.reciprocal(fac8, sum8)
                        dve.drain()
                        for g in range(2):
                            for i in range(NT):
                                x_ = ts(cmp_p[:, g * NT + i, :], cmp_p[:, g * NT + i, :],
                                   fac8[:, g * NT + i:g * NT + i + 1],
                                   small2[:, bass.ds(j * 6 + (24 * i + 3 * g), 1)], ALU.mult, ALU.mult)
                        x_.then_inc(R["c_probs"], 1)
                dve.wait_ge(R["o_hi"], (J + 1).value())
                tt(flat(nl)[:, bass.ds(j * S, S)], OUT[:, :], flat(nh)[:, bass.ds(j * S, S)].bitcast(F32),
                   ALU.subtract).then_inc(R["o_lo"], 1)

            with dve.Fori(0, KD // 2) as r:
                for m in range(2):
                    t, n = Count(T_IN + 3 * m).loop(r, 6), Count(N_IN + 4 * m).loop(r, 8)
                    K = Count(m).loop(r, 2)
                    for c in range(2):
                        take(t + c, n + c, ybuf[:, c, :])
                    for c in range(2):
                        dve.wait_ge(R["mix_sig"], Count(2 * m + c + 1).loop(r, 4).value())
                        dve.wait_ge(chunk_done, (t + 3).value())
                        tt(tmp[:, c, :], ybuf[:, c, :], G[(n + (2 + c)).even()][:, :], ALU.mult).then_inc(tile_out, 1)
                    dve.drain()
                    tt(tmp2[:, 0:S], tmp[:, 0, :], tmp[:, 1, :], ALU.add).then_inc(R["mix_sum"], 1)
                    dve.wait_ge(R["mix_hi"], (K + 1).value())
                    tt(flat(ml)[:, bass.ds(K.value() * S, S)], tmp2[:, 0:S],
                       flat(mh)[:, bass.ds(K.value() * S, S)].bitcast(F32), ALU.subtract).then_inc(R["mix_lo"], 1)

            def add_to_x(t, n, m):
                dve.wait_ge(chunk_done, (t + 1).value())
                tt(tile_of(xs, m), tile_of(xs, m), G[n.even()][:, :], ALU.add).then_inc(tile_out, 1)

            def out_and_ffn(t, n, u, feed0, gain, h0, first_block):
                with dve.Fori(0, KD // 2) as r:
                    for m in range(2):
                        add_to_x((t + m).loop(r, 2), (n + m).loop(r, 2), r * 2 + m)
                    for m in range(2):
                        dve.drain()
                        feed(r * 2 + m, (feed0 + m).loop(r, 2), gain("ffn_g", r, m))
                t, n = t + T_OUT, n + KD
                x_norm(u)
                hidden(t, n, h0, 0, first_block)
                with dve.Fori(1, KF) as r:
                    hidden(t.loop(r, 2), n.loop(r, 2), h0.loop(r, 1), r, first_block)
                return t + T_UP, n + T_UP

            def hidden(t, n, k, j, first_block):
                if first_block:
                    take(t, n, tmp2[:, 2:2 + S])
                    w = (lambda c: pr1[:, P1["conv_w"] + c:P1["conv_w"] + c + 1]) if isinstance(j, int) else \
                        (lambda c: pr1[:, bass.ds(j * 3 + (P1["conv_w"] + c), 1)])
                    b = c1("conv_b") if isinstance(j, int) else pr1[:, bass.ds(j + P1["conv_b"], 1)]
                    if isinstance(j, int):
                        dve.memset(tmp2[:, 0:2], 0.0)
                    dve.drain()
                    ts(tmp3[:, 0:S], tmp2[:, 2:2 + S], w(2), b, ALU.mult, ALU.add)
                    dve.drain()
                    fma(tmp3[:, 0:S], tmp2[:, 1:1 + S], w(1), tmp3[:, 0:S])
                    dve.drain()
                    fma(tmp[:, 0, :], tmp2[:, 0:S], w(0), tmp3[:, 0:S]).then_inc(R["conv_ready"], 1)
                else:
                    take(t, n, tmp[:, 0, :])
                take(t + 1, n + 1, ybuf[:, 0, :])
                dve.drain()
                dve.wait_ge(R["silu_ready"], (k + 1).value())
                tt(tmp[:, 1, :], tmp[:, 0, :], ybuf[:, 0, :], ALU.mult).then_inc(R["prod_ready"], 1)
                dve.wait_ge(R["h_hi"], (k + 1).value())
                tt(flat(hl)[:, cols(j * S, S)], tmp[:, 1, :], flat(hh)[:, cols(j * S, S)].bitcast(F32),
                   ALU.subtract).then_inc(R["h_lo"], 1)

            def down(t, n, feed0, gain):
                with dve.Fori(0, KD // 2) as r:
                    for m in range(2):
                        add_to_x((t + (DOWN_CHUNKS * (m + 1) - 1)).loop(r, 2 * DOWN_CHUNKS), (n + m).loop(r, 2), r * 2 + m)
                        dve.drain()
                        feed(r * 2 + m, (feed0 + m).loop(r, 2), gain("next_g", r, m))
                dve.drain()

            def gain1(name, r, m):
                return pr1[:, bass.ds(r * 2 + (P1[name] + m), 1)]

            def gain2(name, r, m):
                return par[:, bass.ds(r * 2 + (P2[name] + m), 1)]

            t, n = out_and_ffn(Count(T_IN + T_MIX), Count(N_IN + N_MIX), Count(8), Count(KD), gain1, Count(0), True)
            down(t, n, Count(2 * KD), gain1)

            with dve.Fori(0, LAYERS) as l:
                T = Count(T_BLOCK1).loop(l, T_LAYER)
                N = Count(N_BLOCK1).loop(l, N_LAYER)
                U0 = Count(U_BLOCK1).loop(l, U_LAYER)
                L1 = Count(1).loop(l, 1)
                dve.tensor_copy(par[:, :], pr2[:, bass.ds(l * NP2, NP2)]).then_inc(R["par_ready"], 1)
                dve.memset(cpad[:, :, 0:TAPS - 1], 0.0)
                dve.memset(acp[:, 0:2], 0.0)
                dve.drain()
                for c in range(2):
                    x_ = tt(lamp[:, c:c + 1], c2("lam", 2 * c), c2("lam", 2 * c + 1), ALU.mult)
                x_.then_inc(R["lam_in"], 1)
                ts(sub_gain, c2("sub_g"), c2("lam_init", 1), None, ALU.mult)
                x_norm(U0)
                dve.wait_ge(R["lam_exp"], L1.value())
                tt(neglam, lame[:, 1:2], lame[:, 0:1], ALU.subtract)
                dve.drain()
                tt(neglam, neglam, c2("lam_init", 0), ALU.subtract)

                SS = Count(4 * NU).loop(l, 32)
                SC = (POOLB, TR)

                def rot_end(i):
                    dve.wait_ge(rot_ready, Count(8 + i).loop(l, 8).value())
                    tt(tmp2[:, 0:S], ROT[:, :], sin2[:, :], ALU.mult).then_inc(rot_read, 1)
                    dve.drain()
                    tt((lq, lk)[i % 2][:, i // 2 % 2, :], tmp2[:, 0:S], tmp3[:, 0:S], ALU.add)\
                        .then_inc(R["qk_ready"], 1)

                tap = [0]

                def taps(n):
                    for k in range(tap[0], min(tap[0] + n, TAPS)):
                        dve.drain()
                        for c in range(2):
                            w = c2("dw_w", c * TAPS + k)
                            if k == 0:
                                ts(conv[:, c, :], cpad[:, c, 0:S], w, c2("dw_b", c), ALU.mult, ALU.add)
                            else:
                                x_ = fma(conv[:, c, :], cpad[:, c, k:k + S], w, conv[:, c, :])
                        if k == TAPS - 1:
                            x_.then_inc(R["conv_done"], 1)
                    tap[0] += n

                def glu(c):
                    dve.wait_ge(R["glu_sig"], Count(c + 1).loop(l, 2).value())
                    stt(out=cpad[:, c, TAPS - 1:TAPS - 1 + S], in0=ca[:, c, :], scalar=c2("glu_b", c),
                        in1=cg[:, c, :], op0=ALU.add, op1=ALU.mult)

                def peak(h, i):
                    for m in range(2):
                        u = 2 * i + m
                        dve.wait_ge(R["s_psum"], (SS + (8 * h + u + 1)).value())
                        dve.tensor_reduce(negmx2[:, u:u + 1], SC[m][:, 0:(i + 1) * P], AX.X, ALU.max,
                                          negate=True).then_inc(R["max_ready"], 1)

                def combine(h, i):
                    n = (i + 1) * P
                    dve.wait_ge(R["exp_ready"], (SS + (8 * h + 2 * i + 2)).value())
                    dve.reciprocal(rinv2[:, 2 * i:2 * i + 2], rows2[:, 2 * i:2 * i + 2])
                    dve.drain()
                    ts(lp[:, i % 2, 1, 0:n], lp[:, i % 2, 1, 0:n], rinv2[:, 2 * i + 1:2 * i + 2], neglam,
                       ALU.mult, ALU.mult)
                    dve.drain()
                    fma(lp[:, i % 2, 0, 0:n], lp[:, i % 2, 0, 0:n], rinv2[:, 2 * i:2 * i + 1],
                        lp[:, i % 2, 1, 0:n]).then_inc(R["p_ready"], 1)

                def y_rest(name, src):
                    k = Y_ORDER.index(name)
                    dve.wait_ge(R["y_hi"], Count(k + 1).loop(l, KD).value())
                    tt(yl[:, k, :], src, yh[:, k, :].bitcast(F32), ALU.subtract).then_inc(R["y_lo"], 1)

                def head_step(h, step):
                    if 1 <= step < 5:
                        combine(h, step - 1)
                    if step < 4:
                        peak(h, step)
                    if step == 7:
                        recips(U0 + (1 + h), NT)
                    if step == 9:
                        dve.wait_ge(bc_ready, (U0 + (2 + h)).value())
                        mul3(lo_[:, h % 2, :], lo_[:, h % 2, :], sub_gain, BC[:, :]).then_inc(bc_read, 1)
                        dve.drain()
                        dve.sem_inc(R["head_normed"], 1)
                    if step == 10:
                        y_rest(f"head{h}", lo_[:, h % 2, :])

                TAP_PLAN = {4: (2, 1), 5: (1, 1), 6: (2, 1), 19: (2, 2)}
                for n in range(T_LIN):
                    for half, (s, steps) in enumerate(layer_slots(n)):
                        if half == 1 and 5 <= n < 16 and (n - 5) % 3 < 2:
                            rot_end(2 * ((n - 5) // 3) + (n - 5) % 3)
                        for h, step in steps:
                            head_step(h, step)
                        if n >= 4:
                            taps(TAP_PLAN.get(n, (1, 1))[half])
                        if s == 24:
                            y_rest("ya0", ya[:, 0, :])
                        if s == 26:
                            recips(U0 + 5, NT, plain=True)
                        if s == 27:
                            dve.wait_ge(bc_ready, (U0 + 6).value())
                            for c in range(2):
                                x_ = tt(conv[:, c, :], conv[:, c, :], BC[:, :], ALU.subtract)
                            x_.then_inc(bc_read, 1)
                            dve.drain()
                            dve.sem_inc(R["ln_sub"], 1)
                        if s == 28:
                            recips(U0 + 6, NT)
                    tl, nl_ = T + n, N + n
                    if n < 2:
                        take(tl, nl_, ca[:, n, :])
                    elif n < 4:
                        take(tl, nl_, cg[:, n - 2, :])
                        glu(n - 2)
                    elif n < 16:
                        what = (n - 4) % 3
                        take(tl, nl_, ybuf[:, n % 2, :], scale=0.125 if what == 0 else None)
                        if what < 2:
                            dve.drain()
                            tt(tmp3[:, 0:S], ybuf[:, n % 2, :], cos2[:, :], ALU.mult)
                    else:
                        c, what = (n - 16) // 3, (n - 16) % 3
                        if what == 0:
                            take(tl, nl_, tmp3[:, 0:S])
                        elif what == 1:
                            take(tl, nl_, tmp2[:, 0:S])
                            dve.drain()
                            tt(acp[:, 2:2 + S], tmp3[:, 0:S], tmp2[:, 0:S], ALU.mult)
                            dve.drain()
                            ts(ya[:, c, :], acp[:, 2:2 + S], c2("short_w", 3 * c + 2), None, ALU.mult)
                            dve.drain()
                            fma(ya[:, c, :], acp[:, 1:1 + S], c2("short_w", 3 * c + 1), ya[:, c, :])
                            dve.drain()
                            fma(ya[:, c, :], acp[:, 0:S], c2("short_w", 3 * c), ya[:, c, :])
                        else:
                            take(tl, nl_, tmp3[:, 0:S])
                            dve.drain()
                            tt(ya[:, c, :], ya[:, c, :], tmp3[:, 0:S], ALU.mult).then_inc(R["ya_ready"], 1)
                assert tap[0] >= TAPS
                dve.wait_ge(bc_ready, (U0 + 7).value())
                for c in range(2):
                    x_ = mul3(conv[:, c, :], conv[:, c, :], c2("ln_g", c), BC[:, :]).then_inc(R["ln_scaled"], 1)
                dve.drain()
                dve.sem_inc(bc_read, 1)
                y_rest("ya1", ya[:, 1, :])
                for c in range(2):
                    y_rest(f"conv{c}", conv[:, c, :])
                t, n = out_and_ffn(T + T_LIN, N + T_LIN, U0 + 7, Count(3 * KD).loop(l, 2 * KD), gain2,
                                   Count(KF).loop(l, KF), False)
                down(t, n, Count(4 * KD).loop(l, 2 * KD), gain2)

            x_norm(Count(U_BLOCK1 + LAYERS * U_LAYER))
            for m in range(KD):
                if m >= 2:
                    dve.wait_ge(stored[m % 2], 16 * (m // 2))
                mul3(ybuf[:, m % 2, :], xs[:, m, :], c2("next_g", m), rstd[:, :]).then_inc(R["out_ready"], 1)


def kernel(**inputs):
    import ml_dtypes
    import concourse.bacc as bacc
    from concourse.bass_utils import run_bass_kernel_spmd

    g = {k: np.ascontiguousarray(v) for k, v in inputs.items()}

    def blocks(w):
        k, m = w.shape
        return w.reshape(k // P, P, m // P, P).transpose(2, 0, 1, 3)

    def chunks(b):
        m, k = b.shape[:2]
        n = -(-k // CB)
        full = np.zeros((m, n * CB, P, P), np.float32)
        full[:, :k] = b
        return full.reshape(m * n, CB, P, P).transpose(0, 2, 1, 3).reshape(m * n, P, CB * P)

    def columns(v):
        return v.reshape(-1, P).T

    def pair(v):
        return np.concatenate([v, v])[:, None]

    w_in = g["w_in"][0]
    kv = w_in[:, 1024:1792].reshape(D, 6, P)
    q = w_in[:, 512:1024].reshape(D, 2, 4, 64).transpose(0, 2, 1, 3).reshape(D, 4, P)
    gates = np.zeros((D, P), np.float32)
    gates[:, :24] = w_in[:, 1792:1816].reshape(D, 2, 4, 3).transpose(0, 2, 1, 3).reshape(D, 24)
    tiles = [kv[:, i] for i in (0, 1, 2, 4)] + [q[:, j] for j in range(4)] + [kv[:, 3], kv[:, 5], gates]
    tiles += [w_in[:, g * P:(g + 1) * P] for g in (3, 2, 1, 0)]
    stream = [chunks(blocks(np.concatenate(tiles, 1)))]
    merge = blocks(w_in[:, 1816:])
    nsa_rows = g["w_nsa_out"][0].reshape(2, 4, 64, D).transpose(1, 0, 2, 3).reshape(512, D)
    both = np.concatenate([blocks(g["w_pool_out"][0]), blocks(nsa_rows)], 1)
    mix = np.stack([merge[:KD], merge[KD:], both], 1).reshape(3 * KD, CB, P, P)
    stream.append(chunks(mix))

    def ffn(gate, value, down):
        up = np.stack([blocks(gate), blocks(value)], 1).reshape(2 * KF, KD, P, P)
        return [chunks(up), chunks(blocks(down))]

    stream.append(chunks(blocks(g["w_out"][0])))
    stream += ffn(g["w_up"][0][:, :FF], g["w_up"][0][:, FF:], g["w_down"][0])
    y_rows = [("ya0", "ya1", "head0", "head1", "head2", "head3", "conv0", "conv1").index(y) for y in Y_ORDER]
    for l in range(LAYERS):
        w = g["w_in_2"][l]
        a_b, a_c, a_x = w[:, 0:256], w[:, 256:512], w[:, 512:768]
        ql, kl = (w[:, o:o + 512].reshape(D, 2, 4, 64).transpose(0, 2, 1, 3).reshape(D, 4, P) for o in (768, 1280))
        parts = [w[:, 2304:2816]]
        for h in range(4):
            parts += [ql[:, h], kl[:, h], w[:, 1792 + h * P:1920 + h * P]]
        for c in range(2):
            parts += [a[:, c * P:(c + 1) * P] for a in (a_c, a_x, a_b)]
        stream.append(chunks(blocks(np.concatenate(parts, 1))))
        stream.append(chunks(blocks(g["w_out_2"][l].reshape(KD, P, D)[y_rows].reshape(D, D))))
        stream += ffn(g["w_gate_2"][l], g["w_up_2"][l], g["w_down_2"][l])
    weights = np.concatenate(stream)
    assert len(weights) == T_ALL

    par1 = np.zeros((P, NP1), np.float32)

    def put1(name, v):
        par1[:, P1[name]:P1[name] + v.shape[1]] = v

    put1("mix_g", columns(g["mix_norm_g"][0]))
    put1("q_g", pair(g["q_norm_g"][0]))
    for i, name in enumerate(("cmp_g", "sel_g", "win_g")):
        put1(name, pair(g["k_norm_g"][0, i]))
    put1("pool_scale", columns(g["pool_scale"][0]))
    put1("ffn_g", columns(g["ffn_norm_g"][0]))
    put1("conv_w", g["conv_w"][0].reshape(3, KF, P).transpose(2, 1, 0).reshape(P, 3 * KF))
    put1("conv_b", columns(g["conv_b"][0]))
    put1("next_g", columns(g["mix_norm_g_2"][0]))
    for i, name in enumerate(("pe_k", "pe_v")):
        put1(name, g["cmp_pe"][0, i].reshape(2, 16, 64).transpose(0, 2, 1).reshape(P, 16))

    par2 = np.zeros((P, LAYERS * NP2), np.float32)
    for l in range(LAYERS):
        def put2(name, v, at=0):
            o = l * NP2 + P2[name] + at
            par2[:v.shape[0], o:o + v.shape[1]] = v

        put2("short_w", g["short_conv_w_2"][l].reshape(3, 2, P).transpose(2, 1, 0).reshape(P, 6))
        put2("glu_b", columns(g["glu_b_2"][l]))
        put2("dw_w", g["conf_dw_w_2"][l].reshape(TAPS, 2, P).transpose(2, 1, 0).reshape(P, 2 * TAPS))
        put2("dw_b", columns(g["conf_dw_b_2"][l]))
        put2("ln_g", columns(g["conf_ln_g_2"][l]))
        put2("ln_b", columns(g["conf_ln_b_2"][l]))
        put2("sub_g", columns(g["diff_subln_g_2"][l]))
        put2("ffn_g", columns(g["ffn_norm_g_2"][l]))
        put2("next_g", columns(g["mix_norm_g_2"][l + 1] if l + 1 < LAYERS else g["final_norm_g_2"]))
        for i, name in enumerate(("lam_q1_2", "lam_k1_2", "lam_q2_2", "lam_k2_2")):
            put2("lam", g[name][l][:, None], i)
        init = 0.8 - 0.6 * np.exp(-0.3 * l)
        put2("lam_init", np.tile(np.float32([[init, 1.0 - init]]), (P, 1)))

    consts = np.zeros((P, NC), np.float32)
    consts[:, C["ident"]:C["ident"] + P] = np.eye(P)
    for name, dim, half in (("rot1", 16, 8), ("rot2", 64, 32)):
        for h in (0, 64):
            for i in range(half):
                consts[h + half + i, C[name] + h + i] = -1.0
                consts[h + i, C[name] + h + half + i] = 1.0
    consts[:, C["ones"]:C["ones"] + P] = 1.0
    consts[:64, C["halves"]] = 1.0
    consts[64:, C["halves"] + 1] = 1.0
    p = np.arange(P) % 64
    inv1 = (500000.0 ** (-(np.arange(8) * 2.0 / 16))).astype(np.float32)
    consts[:, C["inv1"]] = np.where(p < 16, inv1[p % 8], 0.0)
    inv2 = np.float32(1) / (np.float32(10000) ** (np.arange(0, 64, 2, dtype=np.float32) / np.float32(64)))
    consts[:, C["inv2"]] = inv2[p % 32]
    for i in range(4):
        consts[:, C["rcount"] + 16 * i:C["rcount"] + 16 * i + 16] = 1.0 / np.minimum(np.arange(16) + 1, 2 << i)
    masks = np.zeros((P, 2 * P + 256), np.float32)
    masks[:, 0:P] = np.eye(P)
    t = np.arange(P)
    masks[:, P:2 * P] = np.where(t[None, :] <= t[:, None], 0.0, MASKED)
    for i in range(NT):
        seen = (16 * np.arange(32) + 31)[None, :] <= (i * P + t)[:, None]
        for u in (i, NT + i):
            masks[:, 2 * P + 32 * u:2 * P + 32 * u + 32] = np.where(seen & (np.arange(32) < N_CMP), 0.0, MASKED)
    masks = masks.astype(ml_dtypes.bfloat16)

    w1 = g["cmp_w1"][0].reshape(2, 2, 16, 64, P).transpose(0, 1, 3, 2, 4).reshape(2, P, 16, P)
    w2 = np.stack([np.concatenate([w, w], 1) for w in g["cmp_w2"][0]], 1)
    pool_w = g["pool_w"][0].transpose(1, 0, 2)
    xt = g["x"][0].T.reshape(KD, P, S).transpose(1, 0, 2)
    arrays = {
        "x": xt, "positions": g["positions"][0], "positions2": g["positions_2"][0], "weights": weights, "par1": par1,
        "par2": par2, "consts": consts, "masks": masks, "w1": w1, "w2": w2, "pool_w": pool_w,
    }
    arrays = {k: np.ascontiguousarray(v) for k, v in arrays.items()}
    nc = bacc.Bacc("TRN2", target_bir_lowering=False, num_devices=1)
    args = [nc.dram_tensor(f"in_{k}", v.shape, mybir.dt.from_np(v.dtype), kind="ExternalInput").ap()
            for k, v in arrays.items()]
    out = nc.dram_tensor("out_t", (KD, P, S), F32, kind="ExternalOutput").ap()
    build(nc, *args, out)
    r = run_bass_kernel_spmd(nc, [{f"in_{k}": v for k, v in arrays.items()}], core_ids=[0])
    return r.results[0]["out_t"].reshape(D, S).T.reshape(1, S, D)
```

```python
from contextlib import ExitStack

import numpy as np

import concourse.bass as bass
from concourse import mybir

ALU = mybir.AluOpType
ACT = mybir.ActivationFunctionType
AX = mybir.AxisListType
F32 = mybir.dt.float32
F32R = mybir.dt.float32r
BF16 = mybir.dt.bfloat16
I32 = mybir.dt.int32

P = 128
S = 512
NT = S // P
D = 1024
KD = D // P
FF = 2816
KF = FF // P
CB = 8
DOWN_CHUNKS = -(-KF // CB)
N_CMP = (S - 32) // 16 + 1
LAYERS = 2
EPS = 1e-6
LN_EPS = 1e-5
TAPS = 31
MASKED = -1e30

P1 = {}
_at = 0
for _name, _n in (("mix_g", KD), ("q_g", 1), ("cmp_g", 1), ("sel_g", 1), ("win_g", 1), ("pool_scale", 4),
                  ("ffn_g", KD), ("conv_w", 3 * KF), ("conv_b", KF), ("next_g", KD), ("pe_k", 16), ("pe_v", 16)):
    P1[_name] = _at
    _at += _n
NP1 = _at
P2 = {}
_at = 0
for _name, _n in (("short_w", 6), ("glu_b", 4), ("dw_w", 2 * TAPS), ("dw_b", 2), ("ln_g", 2), ("ln_b", 2),
                  ("sub_g", 1), ("ffn_g", KD), ("next_g", KD), ("lam", 4), ("lam_init", 2)):
    P2[_name] = _at
    _at += _n
NP2 = _at
C = {}
_at = 0
for _name, _n in (("ident", P), ("rot1", P), ("rot2", P), ("ones", P), ("halves", 2), ("inv1", 1), ("inv2", 1),
                  ("rcount", 64)):
    C[_name] = _at
    _at += _n
NC = _at

T_IN, N_IN = 15, 15
T_MIX, N_MIX = 3 * KD, 4 * KD
T_OUT = KD
T_UP = 2 * KF
T_DOWN = DOWN_CHUNKS * KD
T_BLOCK1 = T_IN + T_MIX + T_OUT + T_UP + T_DOWN
N_BLOCK1 = N_IN + N_MIX + T_OUT + T_UP + KD
T_LIN = 22
T_LAYER = T_LIN + T_OUT + T_UP + T_DOWN
N_LAYER = T_LIN + T_OUT + T_UP + KD
T_ALL = T_BLOCK1 + LAYERS * T_LAYER
assert T_LAYER % 2 == 0 and N_LAYER % 2 == 0
U_BLOCK1, U_LAYER = 9, 8
HEAD0 = 7
Y_ORDER = ("head0", "head1", "head2", "ya0", "head3", "ya1", "conv0", "conv1")
NU = 16


class Count:

    def __init__(self, const, terms=()):
        self.const, self.terms = const, tuple(terms)

    def __add__(self, n):
        return Count(self.const + n, self.terms)

    def loop(self, reg, step):
        return Count(self.const, self.terms + ((reg, step),))

    def half(self):
        assert all(s % 2 == 0 for _, s in self.terms)
        return Count(self.const // 2, [(r, s // 2) for r, s in self.terms])

    def even(self):
        assert all(s % 2 == 0 for _, s in self.terms)
        return self.const % 2

    def value(self, times=1):
        v = self.const * times
        for r, s in self.terms:
            v = r * (s * times) + v
        return v

    def low(self):
        return self.const


def layer_slots(n):
    for half in range(2):
        s = 2 * (n - HEAD0) + half
        yield s, [(h, s - 6 * h) for h in (3, 2, 1, 0) if 0 <= s - 6 * h <= 10]


def wait(eng, sem, count, times=1):
    if count.low() > 0:
        eng.wait_ge(sem, count.value(times))


def build(nc, x, positions, positions2, weights, par1, par2, consts, masks, w1, w2, pool_w, out):
    ctx = ExitStack()
    with ctx:
        base = -(-nc.sbuf_base // 64) * 64
        top = [base]

        def at(name, shape, dt, offset):
            return nc.alloc_sbuf_tensor_at(name, list(shape), dt, offset=offset)

        def sb(name, shape, dt=F32):
            size = int(np.prod(shape[1:])) * (2 if dt == BF16 else 4)
            t = at(name, shape, dt, top[0])
            top[0] += -(-size // 64) * 64
            return t

        def sem(name):
            return ctx.enter_context(nc.semaphore(name))

        xs = sb("xs", [P, KD, S])
        xh = sb("xh", [P, KD, S], F32R)
        xl = sb("xl", [P, KD, S], F32R)
        raw = sb("raw", [P, 4 * CB * P])
        wh = sb("wh", [P, 2, CB * P], F32R)
        wl = sb("wl", [P, 2, CB * P], F32R)
        cst = sb("cst", [P, NC])
        msk = sb("msk", [P, 2 * P + 256], BF16)
        pr1 = sb("pr1", [P, NP1])
        pr2 = sb("pr2", [P, LAYERS * NP2])
        par = sb("par", [P, NP2])
        cos = sb("cos", [P, S])
        sin = sb("sin", [P, S])
        cos2 = sb("cos2", [P, S])
        sin2 = sb("sin2", [P, S])
        rstd = sb("rstd", [P, S])
        sqacc = sb("sqacc", [P, S])
        small = sb("small", [P, 192])
        ybuf = sb("ybuf", [P, 2, S])
        BIG = top[0]
        UNIT = 4 * S

        def big(name, unit, shape, dt=F32):
            size = int(np.prod(shape[1:])) * 4
            assert unit * UNIT + size <= 48 * UNIT, name
            return at(name, shape, dt, BIG + unit * UNIT)

        top[0] = BIG + 44 * UNIT
        sq = sb("sq", [P, 2, S])
        tmp = sb("tmp", [P, 2, S])
        tmp2 = sb("tmp2", [P, 528])
        tmp3 = sb("tmp3", [P, 528])
        small2 = sb("small2", [P, 512])
        pairs = sb("pairs", [P, S])
        assert top[0] <= nc.sbuf_usable_end, (top[0], nc.sbuf_usable_end)

        ident = cst[:, C["ident"]:C["ident"] + P]
        rot1 = cst[:, C["rot1"]:C["rot1"] + P]
        rot2 = cst[:, C["rot2"]:C["rot2"] + P]
        ones = cst[:, C["ones"]:C["ones"] + P]
        one = cst[:, C["ones"]:C["ones"] + 1]
        halves = cst[:, C["halves"]:C["halves"] + 2]
        identb = msk[:, 0:P]
        causal = msk[:, P:2 * P]
        cmp_mask = msk[:, 2 * P:2 * P + 256]

        def c1(name, i=0):
            return pr1[:, P1[name] + i:P1[name] + i + 1]

        def c2(name, i=0):
            return par[:, P2[name] + i:P2[name] + i + 1]

        s_root = small[:, 0:8]
        s_recip = small[:, 8:16]
        q_g8 = small[:, 16:17]
        mx8 = small[:, 24:32]
        sum8 = small[:, 32:40]
        fac8 = small[:, 40:48]
        negmx = small[:, 48:64]
        rows = small[:, 64:80]
        rinv = small[:, 80:96]
        lamp = small[:, 96:98]
        lame = small[:, 98:100]
        neglam = small[:, 100:101]
        negmx2 = small[:, 104:112]
        rows2 = small[:, 112:120]
        rinv2 = small[:, 120:128]
        sub_gain = small[:, 128:129]
        gates_t = small2[:, 0:96].rearrange("p (i c) -> p i c", i=NT)
        vct = small2[0:32, 96:224]
        kcf = small2[:, 224:256]
        vcf = small2[:, 256:288]
        kct = small2[:, 288:320]
        csq = small2[:, 320:352]
        cyn = small2[:, 352:384]
        ctm = small2[:, 384:416]
        hid = small2[:, 416:478]

        kvraw = big("kvraw", 0, [P, 2, S])
        pm = big("pm", 0, [P, KD, S])
        w2t = big("w2t", 2, [P, 2, P])
        poolw = big("poolw", 3, [P, 4, P])
        kk = big("kk", 8, [P, 2, S])
        vt = big("vt", 10, [P, 2, NT, P])
        qall = big("qall", 12, [P, 4, S])
        qcur = big("qcur", 46, [P, S])
        cmp_p = big("cmp_p", 47, [P, 8, 32])
        cmp_pt = big("cmp_pt", 44, [32, 2, S])
        w1t = [big("w1k", 16, [P, 16, P]), big("w1v", 20, [P, 16, P])]
        blk = [big("blk_k", 24, [P, 16, 2, N_CMP]), big("blk_v", 28, [P, 16, 2, N_CMP])]
        shifted = big("shifted", 36, [P, 2, 2, 16 * N_CMP])
        probs = big("probs", 16, [P, 4, S])
        pt = big("pt", 20, [P, 2, NT, S])
        poh = big("poh", 28, [P, 4, S], F32R)
        pol = big("pol", 32, [P, 4, S], F32R)
        nh = big("nh", 36, [P, 4, S], F32R)
        nl = big("nl", 40, [P, 4, S], F32R)
        mh = big("mh", 0, [P, KD, S], F32R)
        ml = big("ml", 8, [P, KD, S], F32R)
        hh = big("hh", 0, [P, KF, S], F32R)
        hl = big("hl", KF, [P, KF, S], F32R)
        cpad = big("cpad", 0, [P, 2, TAPS - 1 + S])
        conv = big("conv", 3, [P, 2, S])
        ya = big("ya", 5, [P, 2, S])
        acp = big("acp", 7, [P, 2 + S])
        lv = big("lv", 9, [P, 4, NT, P])
        lq = big("lq", 13, [P, 2, S])
        lk = big("lk", 15, [P, 2, S])
        lp = big("lp", 17, [P, 2, 2, S])
        lpt = big("lpt", 21, [P, NT, S])
        lo_ = big("lo_", 25, [P, 2, S])
        yh = big("yh", 28, [P, KD, S], F32R)
        yl = big("yl", 36, [P, KD, S], F32R)
        ca = big("ca", 36, [P, 2, S])
        cg = big("cg", 38, [P, 2, S])
        posi = big("posi", 6, [P, S], I32)
        posf = big("posf", 7, [P, S])
        ang = big("ang", 8, [P, S])
        turns = big("turns", 9, [P, S])
        red = big("red", 10, [P, S])
        posi2 = big("posi2", 4, [P, S], I32)
        posf2 = big("posf2", 5, [P, S])
        ang2 = big("ang2", 6, [P, S])
        turns2 = big("turns2", 7, [P, S])
        red2 = big("red2", 40, [P, S])

        qcurs = [qcur, tmp2[:, 0:S]]

        bank = [ctx.enter_context(nc.psum_tensor(f"bank{i}", [P, S], F32)) for i in range(8)]
        G = bank[0:2]
        ROT, POOLB, TR, STAT, BC, OUT = bank[2], bank[3], bank[4], bank[5], bank[6], bank[7]

        stored = sem("stored")
        raw_landed = [sem(f"raw_landed{i}") for i in range(2)]
        x_landed = [sem(f"x_landed{i}") for i in range(2)]
        gains_landed = sem("gains_landed")
        par_landed = sem("par_landed")
        late_landed = sem("late_landed")
        shift_landed = sem("shift_landed")
        hi_ready = sem("hi_ready")
        lo_ready = sem("lo_ready")
        chunk_done = sem("chunk_done")
        half_done = sem("half_done")
        tile_out = sem("tile_out")
        xh_ready = sem("xh_ready")
        xl_ready = sem("xl_ready")
        stat_ready = sem("stat_ready")
        root_ready = sem("root_ready")
        recip_ready = sem("recip_ready")
        bc_ready = sem("bc_ready")
        bc_read = sem("bc_read")
        sq_ready = sem("sq_ready")
        rot_in = sem("rot_in")
        rot_ready = sem("rot_ready")
        rot_read = sem("rot_read")
        tr_ready = sem("tr_ready")
        tr_read = sem("tr_read")
        sine_done = sem("sine_done")
        ready = {n: sem(n) for n in (
            "tables", "blk_ready", "hid_psum", "hid_ready", "cmp_psum", "cmp_copied", "vct_psum", "vct_ready",
            "pool_in", "pool_psum", "pool_hi", "pool_lo",
            "q_cur", "s_psum", "max_ready", "exp_ready", "p_ready", "pt_psum", "pt_ready", "pv_done", "o_psum",
            "o_hi", "o_lo", "c_psum", "c_sub", "c_exp", "c_probs", "c_tpsum", "c_tready",
            "mix_sig", "mix_sum", "mix_hi", "mix_lo",
            "conv_ready", "silu_ready", "prod_ready", "h_hi", "h_lo",
            "lam_in", "lam_psum", "lam_exp", "glu_sig", "conv_done",
            "qk_ready", "head_normed", "ya_ready", "ln_sub", "ln_sq", "ln_scaled", "yc_ready", "y_hi", "y_lo",
            "zeroed", "out_ready", "par_ready")}
        R = ready
        block = ctx.enter_context(nc.Block())

        def cols(start, n):
            return slice(start, start + n) if isinstance(start, int) else bass.ds(start, n)

        def raw_slot(t):
            v = t.value()
            return raw[:, cols((v % 4) * (CB * P), CB * P)]

        t0 = Count(0)

        @block.sync
        def _(sp):
            sp.dma_start(pr1[:, :], par1).then_inc(gains_landed, 16)
            for i in range(2):
                half = slice(i * KD // 2, (i + 1) * KD // 2)
                sp.dma_start(xs[:, half, :], x[:, half, :]).then_inc(x_landed[i], 16)
            for t in range(2):
                sp.dma_start(raw[:, t * CB * P:(t + 1) * CB * P], weights[t]).then_inc(raw_landed[t], 16)
            sp.dma_start(cst[:, :], consts).then_inc(par_landed, 16)
            sp.dma_start(posi[:, :], positions.partition_broadcast(P)).then_inc(par_landed, 16)

            def load(t, source):
                sp.wait_ge(raw_landed[t % 2], 16 * (t // 2))
                if t >= 4:
                    sp.wait_ge(lo_ready, t - 3)
                sp.dma_start(raw[:, (t % 4) * CB * P:(t % 4 + 1) * CB * P], weights[source])\
                    .then_inc(raw_landed[t % 2], 16)

            load(2, 2)
            load(3, 3)
            for c in range(2):
                sp.dma_start(w1t[c][:, :, :], w1[c]).then_inc(late_landed, 16)
            sp.dma_start(posi2[:, :], positions2.partition_broadcast(P)).then_inc(late_landed, 16)
            sp.dma_start(pr2[:, :], par2).then_inc(late_landed, 16)
            sp.dma_start(msk[:, :], masks).then_inc(late_landed, 16)
            sp.dma_start(w2t[:, :, :], w2).then_inc(late_landed, 16)
            sp.dma_start(poolw[:, :, :], pool_w).then_inc(late_landed, 16)
            for t in range(4, 8):
                load(t, t)
            for c in range(2):
                sp.wait_ge(tile_out, c + 1)
                for g in range(2):
                    for half in range(2):
                        sp.dma_start(shifted[half * 64:(half + 1) * 64, c, g, :],
                                     kvraw[g * 64:(g + 1) * 64, c, 16 * half:16 * half + 16 * N_CMP])\
                            .then_inc(shift_landed, 16)
            trips = (T_ALL - 8) // 4
            with sp.Fori(0, trips) as r:
                for c in range(4):
                    t = Count(8 + c).loop(r, 4)
                    chunk, landed, split = t.value(), t.half().value(16), (t + -3).value()
                    for v in (landed, split, chunk * (P * CB * P) * 4):
                        sp.compute_val(v)
                    src = weights[bass.ds(chunk, 1), :, :].rearrange("o p c -> (o p) c")
                    sp.wait_ge(raw_landed[c % 2], landed)
                    sp.wait_ge(lo_ready, split)
                    sp.dma_start(raw[:, c * CB * P:(c + 1) * CB * P], src).then_inc(raw_landed[c % 2], 16)
            for t in range(8 + 4 * trips, T_ALL + 2):
                load(t, t if t < T_ALL else t - T_ALL)
            for m in range(KD):
                sp.wait_ge(R["out_ready"], m + 1)
                sp.dma_start(out[m], xs[:, m, :]).then_inc(stored, 16)
            sp.wait_ge(stored, 16 * KD)

        @block.gpsimd
        def _(pool):
            def rest(t):
                v = t.value()
                two = cols((v % 2) * (CB * P), CB * P)
                pool.wait_ge(hi_ready, (t + 1).value())
                pool.tensor_tensor(wl[:, :, :].rearrange("p s n -> p (s n)")[:, two], raw_slot(t),
                                   wh[:, :, :].rearrange("p s n -> p (s n)")[:, two].bitcast(F32),
                                   ALU.subtract).then_inc(lo_ready, 1)

            with pool.Fori(0, T_ALL + 2) as t:
                rest(Count(0).loop(t, 1))

        @block.tensor
        def _(pe):
            mm = pe.matmul

            def tile(t, n, kh, kl, blocks=CB, blk0=0, first=True, last=True, count=True, feed=None, mid=None,
                     slots=None, feed_sem=None):
                feed_sem = feed_sem or xl_ready
                s, b = t.even(), G[n.even()]
                if first:
                    wait(pe, tile_out, n + -1)
                if blk0 == 0:
                    pe.wait_ge(hi_ready, (t + 1).value())
                early = blocks - 1 if feed is not None else blocks
                for k in range(early):
                    if feed is not None:
                        pe.wait_ge(feed_sem, (feed + (k + 1)).value())
                    w = wh[:, s, (blk0 + k) * P:(blk0 + k + 1) * P]
                    mm(b[:, :], w, kh(k), start=first and k == 0, stop=False)
                    mm(b[:, :], w, kl(k), start=False, stop=False)
                    if slots is not None and k == 3:
                        slots[0]()
                if mid is not None and early == blocks:
                    mid()
                if blk0 == 0:
                    pe.wait_ge(lo_ready, (t + 1).value())
                if early < blocks:
                    k = early
                    for j in range(early):
                        mm(b[:, :], wl[:, s, j * P:(j + 1) * P], kh(j), start=False, stop=False)
                    pe.wait_ge(feed_sem, (feed + blocks).value())
                    mm(b[:, :], wh[:, s, k * P:(k + 1) * P], kh(k), start=False, stop=False)
                    mm(b[:, :], wh[:, s, k * P:(k + 1) * P], kl(k), start=False, stop=False)
                    mm(b[:, :], wl[:, s, k * P:(k + 1) * P], kh(k), start=False, stop=True).then_inc(chunk_done, 1)
                    if mid is not None:
                        mid()
                    return
                for k in range(blocks):
                    i = mm(b[:, :], wl[:, s, (blk0 + k) * P:(blk0 + k + 1) * P], kh(k),
                           start=False, stop=last and k == blocks - 1)
                    if slots is not None and k == 3:
                        slots[1]()
                i.then_inc(chunk_done if count else half_done, 1)

            def products(t, n, kh, kl, blocks=CB, blk0=0, count=True):
                s, b = t.even(), G[n.even()]
                pe.wait_ge(tile_out, (n + -1).value())
                if blk0 == 0:
                    pe.wait_ge(hi_ready, (t + 1).value())
                for k in range(blocks):
                    w = wh[:, s, (blk0 + k) * P:(blk0 + k + 1) * P]
                    mm(b[:, :], w, kh(k), start=k == 0, stop=False)
                    mm(b[:, :], w, kl(k), start=False, stop=False)
                    yield
                if blk0 == 0:
                    pe.wait_ge(lo_ready, (t + 1).value())
                for k in range(blocks):
                    i = mm(b[:, :], wl[:, s, (blk0 + k) * P:(blk0 + k + 1) * P], kh(k),
                           start=False, stop=k == blocks - 1)
                    if k == blocks - 1:
                        i.then_inc(chunk_done if count else half_done, 1)
                    if k % 2:
                        yield

            def xk(t, n, feed=None, mid=None, slots=None):
                tile(t, n, lambda k: xh[:, k, :], lambda k: xl[:, k, :], feed=feed, mid=mid, slots=slots)

            def stats(u, src, cols_, n=P, per=1, tiles=NT, start=lambda i: True):
                for i in range(tiles):
                    lists = src(i)
                    for a, s_ in enumerate(lists):
                        x_ = mm(STAT[0:n, per * i:per * (i + 1)], s_, cols_, start=a == 0, stop=a == len(lists) - 1)
                x_.then_inc(stat_ready, 1)

            def spread(u, src, n=P, tiles=NT, width=S):
                pe.wait_ge(recip_ready, (u + 1).value())
                wait(pe, bc_read, u)
                for i in range(tiles):
                    x_ = pe.transpose(BC[:, i * P:i * P + n], src(i), ident[0:n, 0:n])
                x_.then_inc(bc_ready, 1)

            def x_stats(u, feed):
                pe.wait_ge(xl_ready, (feed + KD).value())
                stats(u, lambda i: [sqacc[:, i * P:(i + 1) * P]], one)

            def x_spread(u):
                spread(u, lambda i: s_recip[:, i:i + 1].to_broadcast([P, P]))

            norm_of = {2: 1, 3: 2, 4: 3, 5: 4, 6: 5, 7: 6}
            rot_of = {n: i for i, n in enumerate((2, 3, 4, 5, 6, 7))}
            tr_of = {12: 0, 13: 1, 14: 2}
            pool_of = {8: 0, 9: 1, 10: 2, 11: 3}

            def head_stats(n):
                u = Count(norm_of[n])
                pe.wait_ge(sq_ready, norm_of[n])
                wait(pe, root_ready, u)
                stats(u, lambda i: [sq[:, 0, i * P:(i + 1) * P]], halves, per=2)

            def head_spread(n):
                spread(Count(norm_of[n]), lambda i: pairs[:, i * P:(i + 1) * P])

            def rotate(n):
                pe.wait_ge(rot_in, rot_of[n] + 1)
                if rot_of[n]:
                    pe.wait_ge(rot_read, rot_of[n])
                mm(ROT[:, :], rot1, tmp[:, rot_of[n] % 2, :], start=True, stop=True).then_inc(rot_ready, 1)

            def turn(n):
                pe.wait_ge(tile_out, n + 1)
                if tr_of[n]:
                    pe.wait_ge(tr_read, tr_of[n])
                else:
                    pe.wait_ge(R["vct_ready"], 1)
                for i in range(NT):
                    x_ = pe.transpose(TR[:, i * P:(i + 1) * P], ybuf[:, n % 2, i * P:(i + 1) * P], ident)
                x_.then_inc(tr_ready, 1)

            def pool_mix(i):
                pe.wait_ge(R["pool_in"], i + 1)
                if i:
                    pe.wait_ge(R["pool_lo"], i)
                else:
                    pe.wait_ge(R["hid_ready"], 2)
                mm(POOLB[:, :], poolw[:, 3 - i, :], tmp[:, i % 2, :], start=True, stop=True).then_inc(R["pool_psum"], 1)

            def compress(c):
                pe.wait_ge(R["blk_ready"], c + 1)
                if c:
                    pe.wait_ge(R["hid_ready"], c)
                for l in range(16):
                    x_ = mm(POOLB[:, 0:2 * N_CMP], w1t[c][:, l, :],
                            blk[c][:, l, :, :].rearrange("p g n -> p (g n)"), start=l == 0, stop=l == 15)
                x_.then_inc(R["hid_psum"], 1)

            def compress_out(c):
                pe.wait_ge(R["hid_ready"], c + 1)
                if c:
                    pe.wait_ge(R["cmp_copied"], c)
                mm(STAT[:, 0:2 * N_CMP], w2t[:, c, :], hid, start=True, stop=True).then_inc(R["cmp_psum"], 1)

            def after(n):
                if n == 0:
                    pe.wait_ge(par_landed, 16 * 2)
                    x_stats(Count(0), Count(0))
                if n == 1:
                    x_spread(Count(0))
                if n - 1 in norm_of:
                    head_stats(n - 1)
                if n - 2 in rot_of:
                    rotate(n - 2)
                if n - 1 in tr_of:
                    turn(n - 1)
                if n == 9:
                    pe.wait_ge(late_landed, 16 * 7)
                if n in (9, 10):
                    compress(n - 9)
                if n in (10, 11):
                    compress_out(n - 10)
                if n - 3 in pool_of:
                    pool_mix(pool_of[n - 3])
                if n == 12:
                    pe.wait_ge(sq_ready, 7)
                    pe.wait_ge(R["cmp_copied"], 2)
                    mm(STAT[0:32, 0:2], csq, halves, start=True, stop=True).then_inc(stat_ready, 1)
                    pe.transpose(TR[0:32, 0:P], vcf, ident).then_inc(R["vct_psum"], 1)
                if n == 13:
                    pe.wait_ge(recip_ready, 8)
                    pe.wait_ge(bc_read, 7)
                    pe.transpose(BC[:, 0:32], pairs[0:32, 0:P], ident[0:32, 0:32]).then_inc(bc_ready, 1)
                if n == 14:
                    pe.wait_ge(rot_in, 7)
                    pe.wait_ge(rot_read, 6)
                    mm(ROT[:, 0:32], rot1, cyn, start=True, stop=True).then_inc(rot_ready, 1)

            for n in range(N_IN):
                xk(Count(n), Count(n), feed=Count(0) if n == 0 else None, mid=lambda: after(n))
                if n - 1 in norm_of:
                    head_spread(n - 1)
            turn(14)
            pe.wait_ge(rot_read, 7)

            SB = [ROT, POOLB]
            TB = [STAT, BC]
            pe.wait_ge(R["pool_lo"], 4)
            pe.wait_ge(tr_read, 3)

            def pool_branch(t, n):
                for m in range(2):
                    yield from products(t + m, n + m, lambda k: xh[:, k, :], lambda k: xl[:, k, :])
                for m in range(2):
                    yield from products(t + 2, n + (2 + m), lambda k: poh[:, k, :], lambda k: pol[:, k, :], blocks=4,
                                        blk0=4 * m, count=m == 1)

            def attention(trip, odd):
                U, J = trip(0, NU), trip(0, 1)
                filler = pool_branch(trip(T_IN, 3), trip(N_IN, 4))

                def fill(n):
                    for _ in range(n):
                        next(filler)

                pe.wait_ge(R["q_cur"], (J + 1).value())
                qcur = qcurs[odd]
                def score(u):
                    g, b, i = u // 8, u // 4 % 2, u % 4
                    if u >= 2:
                        pe.wait_ge(R["exp_ready"], (U + (u - 1)).value())
                    s = SB[u % 2]
                    n = (i + 1) * P
                    mm(s[:, 0:n], qcur[g * 64:(g + 1) * 64, i * P:(i + 1) * P], kk[g * 64:(g + 1) * 64, b, 0:n],
                       start=True, stop=False)
                    mm(s[:, i * P:n], identb, causal, start=False, stop=True).then_inc(R["s_psum"], 1)

                def turn_probs(u):
                    i = u % 4
                    pe.wait_ge(R["p_ready"], (U + (u + 1)).value())
                    if u >= 2:
                        pe.wait_ge(R["pt_ready"], (U + (u - 1)).value())
                    for c in range(i + 1):
                        x_ = pe.transpose(TB[u % 2][:, c * P:(c + 1) * P], probs[:, u % 4, c * P:(c + 1) * P], ident)
                    x_.then_inc(R["pt_psum"], 1)

                def values(w):
                    g, b = w // 2, w % 2
                    pe.wait_ge(R["pt_ready"], (U + (4 * w + 4)).value())
                    for c in range(NT):
                        x_ = mm(OUT[g * 64:(g + 1) * 64, c * P:S], vt[:, b, c, g * 64:(g + 1) * 64],
                                pt[:, w % 2, c, c * P:S], start=b == 0 and c == 0, stop=False)
                    x_.then_inc(R["pv_done"], 1)

                score(0)
                score(1)
                for g in range(2):
                    s = (TR, BC)[g]
                    mm(s[:, 0:P], identb, cmp_mask[:, g * P:(g + 1) * P], start=True, stop=False)
                    for qt in range(NT):
                        x_ = mm(s[:, qt * 32:(qt + 1) * 32], qcur[g * 64:(g + 1) * 64, qt * P:(qt + 1) * P],
                                kct[g * 64:(g + 1) * 64, :], start=False, stop=qt == 3)
                x_.then_inc(R["c_psum"], 1)
                fill(4)
                for u in range(NU):
                    if u + 2 < NU:
                        score(u + 2)
                    if u < NU - 2:
                        fill(2)
                    turn_probs(u)
                    if u in (3, 5):
                        g = u // 2 - 1
                        pe.wait_ge(R["c_probs"], (J + 1).value())
                        if g:
                            pe.wait_ge(R["c_tready"], trip(1, 2).value())
                        for i in range(NT):
                            x_ = pe.transpose(TR[0:32, i * P:(i + 1) * P], cmp_p[:, g * NT + i, :], ident)
                        x_.then_inc(R["c_tpsum"], 1)
                    if u % 4 == 0 and u:
                        values(u // 4 - 1)
                        if u == 8:
                            pe.wait_ge(R["c_tready"], trip(2, 2).value())
                            mm(OUT[0:64, :], vct[:, 0:64], cmp_pt[:, 0, :], start=False, stop=True)
                fill(4)
                values(3)
                mm(OUT[64:P, :], vct[:, 64:P], cmp_pt[:, 1, :], start=False, stop=True).then_inc(R["o_psum"], 1)
            with pe.Fori(0, 2) as r:
                for i in range(2):
                    attention(lambda const, step: Count(const + i * step).loop(r, 2 * step), i)

            pe.wait_ge(R["o_lo"], 4)
            with pe.Fori(0, 2) as r:
                for i in range(2):
                    t, n = Count(T_IN + 12 + 3 * i).loop(r, 6), Count(N_IN + 16 + 4 * i).loop(r, 8)
                    for m in range(2):
                        xk(t + m, n + m)
                    for m in range(2):
                        tile(t + 2, n + (2 + m), lambda k: nh[:, k, :], lambda k: nl[:, k, :], blocks=4, blk0=4 * m,
                             count=m == 1)

            def out_and_ffn(tb, nb, ysrc, y_ready, u, feed):
                with pe.Fori(0, KD // 2) as r:
                    for m in range(2):
                        tile((tb + m).loop(r, 2), (nb + m).loop(r, 2), lambda k: ysrc[0][:, k, :],
                             lambda k: ysrc[1][:, k, :], feed=y_ready[1] if m == 0 else None, feed_sem=y_ready[0])
                tb, nb = tb + T_OUT, nb + KD
                xk(tb, nb, feed=feed, mid=lambda: x_stats(u, feed))
                xk(tb + 1, nb + 1, mid=lambda: x_spread(u))
                with pe.Fori(0, KF - 1) as r:
                    xk((tb + 2).loop(r, 2), (nb + 2).loop(r, 2))
                    xk((tb + 3).loop(r, 2), (nb + 3).loop(r, 2))
                tb, nb = tb + T_UP, nb + T_UP
                return tb, nb

            def down(tb, nb, h_lo):
                with pe.Fori(0, KD // 2) as r:
                    for m in range(2):
                        for c in range(DOWN_CHUNKS):
                            k0 = CB * c
                            if m == 0:
                                pe.wait_ge(R["h_lo"], (h_lo + (min(k0 + CB, KF) - KF)).value())
                            tile((tb + (DOWN_CHUNKS * m + c)).loop(r, 2 * DOWN_CHUNKS), (nb + m).loop(r, 2),
                                 lambda k: hh[:, k0 + k, :], lambda k: hl[:, k0 + k, :],
                                 blocks=min(CB, KF - k0), first=c == 0, last=c == DOWN_CHUNKS - 1)

            tb, nb = out_and_ffn(Count(T_IN + T_MIX), Count(N_IN + N_MIX), (mh, ml), (R["mix_lo"], Count(0)),
                                 Count(8), Count(KD))
            down(tb, nb, Count(KF))

            with pe.Fori(0, LAYERS) as l:
                T = Count(T_BLOCK1).loop(l, T_LAYER)
                N = Count(N_BLOCK1).loop(l, N_LAYER)
                U0 = Count(U_BLOCK1).loop(l, U_LAYER)
                feed = Count(2 * KD).loop(l, 2 * KD)
                L1 = Count(1).loop(l, 1)

                def lam_sum():
                    pe.wait_ge(R["lam_in"], L1.value())
                    mm(POOLB[:, 0:2], ones, lamp, start=True, stop=True).then_inc(R["lam_psum"], 1)

                RO = Count(7).loop(l, 8)
                SS = Count(4 * NU).loop(l, 32)
                TT = Count(4 * NU).loop(l, 16)
                OO = Count(4).loop(l, 4)
                SC = (POOLB, TR)

                def turn_v(h):
                    pe.wait_ge(tile_out, (N + (HEAD0 + 3 * h)).value())
                    pe.wait_ge(rot_read, (RO + (2 * h + 2)).value())
                    for c in range(NT):
                        x_ = pe.transpose(ROT[:, c * P:(c + 1) * P], ybuf[:, (HEAD0 - 1 + 3 * h) % 2,
                                                                          c * P:(c + 1) * P], ident)
                    x_.then_inc(tr_ready, 1)

                def rotate_l(i):
                    n = 4 + 3 * (i // 2) + i % 2
                    pe.wait_ge(tile_out, (N + (n + 1)).value())
                    if i % 2:
                        pe.wait_ge(rot_read, (RO + i).value())
                    else:
                        pe.wait_ge(tr_read, Count(3 + i // 2).loop(l, 4).value())
                    mm(ROT[:, :], rot2, ybuf[:, n % 2, :], start=True, stop=True).then_inc(rot_ready, 1)

                def score_l(h, i):
                    n = (i + 1) * P
                    if i == 0:
                        pe.wait_ge(R["qk_ready"], Count(2 * h + 2).loop(l, 8).value())
                        if h == 0:
                            pe.wait_ge(R["lam_exp"], L1.value())
                    for m in range(2):
                        u = 8 * h + 2 * i + m
                        if i or h:
                            pe.wait_ge(R["exp_ready"], (SS + (u - 1)).value())
                        mm(SC[m][:, 0:n], lq[m * 64:(m + 1) * 64, h % 2, i * P:n], lk[m * 64:(m + 1) * 64, h % 2, 0:n],
                           start=True, stop=False)
                        mm(SC[m][:, i * P:n], identb, causal, start=False, stop=True).then_inc(R["s_psum"], 1)

                def turn_l(h, i):
                    pe.wait_ge(R["p_ready"], (TT + (4 * h + i + 1)).value())
                    if i:
                        pe.wait_ge(R["pt_ready"], (TT + (4 * h + i)).value())
                    elif h:
                        pe.wait_ge(R["o_hi"], (OO + h).value())
                    for c in range(i + 1):
                        x_ = pe.transpose(OUT[:, c * P:(c + 1) * P], lp[:, i % 2, 0, c * P:(c + 1) * P], ident)
                    x_.then_inc(R["pt_psum"], 1)

                def values_l(h):
                    pe.wait_ge(R["pt_ready"], (TT + (4 * h + 4)).value())
                    pe.wait_ge(tr_read, Count(4 + h).loop(l, 4).value())
                    for c in range(NT):
                        x_ = mm(OUT[:, c * P:S], lv[:, h, c, :], lpt[:, c, c * P:S], start=c == 0, stop=c == 3)
                    x_.then_inc(R["o_psum"], 1)

                def head_step(h, step):
                    if step < 4:
                        score_l(h, step)
                    if 2 <= step < 6:
                        turn_l(h, step - 2)
                    if step == 6:
                        values_l(h)
                    if step == 7:
                        pe.wait_ge(sq_ready, Count(8 + h).loop(l, 4).value())
                        stats(U0 + (1 + h), lambda i: [sq[:, 0, i * P:(i + 1) * P]], one)
                    if step == 8:
                        spread(U0 + (1 + h), lambda i: s_recip[:, i:i + 1].to_broadcast([P, P]))

                def ln_stats(u, src):
                    stats(u, lambda i: [src[:, c, i * P:(i + 1) * P] for c in range(2)], one)

                def slot(n, half):
                    s, steps = list(layer_slots(n))[half]
                    if half == 0:
                        if n == 1:
                            x_spread(U0)
                            lam_sum()
                    for h, step in steps:
                        head_step(h, step)
                    if half == 0:
                        if 5 <= n < 16:
                            h, what = (n - 5) // 3, (n - 5) % 3
                            if what < 2:
                                rotate_l(2 * h + what)
                        if HEAD0 <= n < 17 and (n - HEAD0) % 3 == 0:
                            turn_v((n - HEAD0) // 3)
                    if s == 26:
                        pe.wait_ge(R["conv_done"], L1.value())
                        ln_stats(U0 + 5, conv)
                    if s == 27:
                        spread(U0 + 5, lambda i: s_recip[:, i:i + 1].to_broadcast([P, P]))
                    if s == 28:
                        pe.wait_ge(R["ln_sq"], L1.value())
                        ln_stats(U0 + 6, sq)
                    if s == 29:
                        spread(U0 + 6, lambda i: s_recip[:, i:i + 1].to_broadcast([P, P]))

                for n in range(T_LIN):
                    if n == 0:
                        xk(T, N, feed=feed, mid=lambda: x_stats(U0, feed))
                    else:
                        xk(T + n, N + n, slots=[lambda: slot(n, 0), lambda: slot(n, 1)])

                tb, nb = out_and_ffn(T + T_LIN, N + T_LIN, (yh, yl), (R["y_lo"], Count(0).loop(l, KD)), U0 + 7,
                                     Count(3 * KD).loop(l, 2 * KD))
                down(tb, nb, Count(2 * KF).loop(l, KF))

            x_stats(Count(U_BLOCK1 + LAYERS * U_LAYER), Count((2 + 2 * LAYERS) * KD))
            x_spread(Count(U_BLOCK1 + LAYERS * U_LAYER))

        @block.scalar
        def _(act):
            def copy(o, i, scale=1.0):
                return act.activation(o, i, ACT.Copy, scale=scale)

            def head(t):
                s = t.even()
                act.wait_ge(raw_landed[s], (t.half() + 1).value(16))
                wait(act, chunk_done, t + -1)
                copy(wh[:, s, :], raw_slot(t)).then_inc(hi_ready, 1)

            def root(u, n, parts=P, scale=1.0, eps=EPS, plain=False):
                act.wait_ge(stat_ready, (u + 1).value())
                wait(act, recip_ready, u)
                o, i = s_root[0:parts, 0:n], STAT[0:parts, 0:n]
                if plain:
                    copy(o, i, scale=scale).then_inc(root_ready, 1)
                else:
                    act.activation(o, i, ACT.Sqrt, scale=scale, bias=eps_ap(eps)[0:parts, :]).then_inc(root_ready, 1)

            def eps_ap(e):
                return small[:, 188:189] if e == EPS else small[:, 189:190]

            def flat(a):
                return a[:, :, :].rearrange("p k n -> p (k n)")

            def feed(m, k, g, n):
                if n is not None:
                    act.wait_ge(tile_out, (n + 1).value())
                wait(act, xl_ready, k + -1)
                copy(flat(xh)[:, cols(m * S, S)], flat(xs)[:, cols(m * S, S)], scale=g)
                act.activation(sq[:, k.even(), :], flat(xs)[:, cols(m * S, S)], ACT.Square).then_inc(xh_ready, 1)

            act.wait_ge(R["zeroed"], 1)
            act.wait_ge(gains_landed, 16)
            for m in range(KD):
                if m % (KD // 2) == 0:
                    act.wait_ge(x_landed[m // (KD // 2)], 16)
                feed(m, Count(m), c1("mix_g", m), None)
                if m in (1, 3):
                    head(Count(m // 2))
            root(Count(0), NT, scale=1.0 / D)

            def sine(i):
                o, a = ((sin, red), (cos, red), (sin2, red2), (cos2, red2))[i]
                act.wait_ge(R["tables"], i + 1)
                act.activation(o[:, :], a[:, :], ACT.Sin).then_inc(sine_done, 1)

            def pool_head(i):
                g = 3 - i
                act.wait_ge(R["pool_psum"], i + 1)
                copy(poh[:, g, :], POOLB[:, :], scale=c1("pool_scale", g)).then_inc(R["pool_hi"], 1)

            def hidden_cmp(c):
                act.wait_ge(R["hid_psum"], c + 1)
                if c:
                    act.wait_ge(R["cmp_psum"], c)
                act.activation(hid, POOLB[:, 0:2 * N_CMP], ACT.Silu).then_inc(R["hid_ready"], 1)

            for n in range(N_IN):
                act.wait_ge(chunk_done, n + 1)
                head(Count(n + 2))
                act.wait_ge(tile_out, n + 1)
                if 2 <= n < 8:
                    act.activation(sq[:, 0, :], ybuf[:, n % 2, :], ACT.Square).then_inc(sq_ready, 1)
                    root(Count(n - 1), 8, scale=1.0 / 64)
                if 12 <= n < 14:
                    act.wait_ge(tr_ready, n - 11)
                    copy(vt[:, n - 12, :, :].rearrange("p i d -> p (i d)"), TR[:, :]).then_inc(tr_read, 1)
                if n in (0, 1):
                    sine(n)
                if n in (9, 10):
                    hidden_cmp(n - 9)
                if n == 11:
                    act.wait_ge(R["cmp_copied"], 1)
                    act.activation(csq, kcf, ACT.Square).then_inc(sq_ready, 1)
                    act.wait_ge(R["vct_psum"], 1)
                    copy(vct, TR[0:32, 0:P]).then_inc(R["vct_ready"], 1)
                    root(Count(7), 2, parts=32, scale=1.0 / 64)
                if 10 <= n < 14:
                    pool_head(n - 10)
            act.wait_ge(tr_ready, 3)
            act.activation(gates_t, TR[:, :].rearrange("p (i c) -> p i c", i=NT)[:, :, 0:24],
                           ACT.Sigmoid).then_inc(tr_read, 1)
            sine(2)
            sine(3)

            TB = [STAT, BC]
            SB = [ROT, POOLB]

            def gate(n):
                for c in range(2):
                    act.wait_ge(tile_out, (n + (c + 1)).value())
                    act.activation(ybuf[:, c, :], ybuf[:, c, :], ACT.Sigmoid).then_inc(R["mix_sig"], 1)

            def attention(trip, j):
                U, J = trip(0, NU), trip(0, 1)
                t, n = trip(T_IN, 3), trip(N_IN, 4)

                def exps(u):
                    n = (u % 4 + 1) * P
                    act.wait_ge(R["max_ready"], (U + (u + 1)).value())
                    if u >= 4:
                        act.wait_ge(R["pt_psum"], (U + (u - 3)).value())
                    act.activation(probs[:, u % 4, 0:n], SB[u % 2][:, 0:n], ACT.Exp, bias=negmx[:, u:u + 1],
                                   accum_out=rows[:, u:u + 1]).then_inc(R["exp_ready"], 1)

                def put(u):
                    i, w = u % 4, u // 4
                    act.wait_ge(R["pt_psum"], (U + (u + 1)).value())
                    if w >= 2 and i == 0:
                        act.wait_ge(R["pv_done"], trip(w - 1, 4).value())
                    copy(pt[:, w % 2, 0:i + 1, i * P:(i + 1) * P],
                         TB[u % 2][:, 0:(i + 1) * P].rearrange("p (c q) -> p c q", q=P)).then_inc(R["pt_ready"], 1)

                for u in range(NU + 2):
                    if u < NU:
                        exps(u)
                    if u == 1:
                        act.wait_ge(R["c_sub"], (J + 1).value())
                        act.activation(cmp_p[:, :, :], cmp_p[:, :, :], ACT.Exp).then_inc(R["c_exp"], 1)
                    if u >= 2:
                        put(u - 2)
                    if u in (4, 6):
                        g = u // 2 - 2
                        act.wait_ge(R["c_tpsum"], trip(g + 1, 2).value())
                        copy(cmp_pt[:, g, :], TR[0:32, :]).then_inc(R["c_tready"], 1)
                    if u == 6:
                        act.wait_ge(chunk_done, (t + 1).value())
                        head(t + 2)
                    if u == 12:
                        act.wait_ge(chunk_done, (t + 2).value())
                        head(t + 3)
                        gate(n)
                act.wait_ge(R["o_psum"], (J + 1).value())
                copy(flat(nh)[:, bass.ds(j * S, S)], OUT[:, :]).then_inc(R["o_hi"], 1)
                act.wait_ge(chunk_done, (t + 3).value())
                head(t + 4)

            with act.Fori(0, 2) as r:
                for i in range(2):
                    attention(lambda const, step: Count(const + i * step).loop(r, 2 * step), r * 2 + i)

            with act.Fori(0, 2) as r:
                for i in range(2):
                    t, n = Count(T_IN + 12 + 3 * i).loop(r, 6), Count(N_IN + 16 + 4 * i).loop(r, 8)
                    for c in range(2):
                        act.wait_ge(chunk_done, (t + (c + 1)).value())
                        head(t + (c + 2))
                    gate(n)
                    act.wait_ge(chunk_done, (t + 3).value())
                    head(t + 4)
                    for c in range(2):
                        K = Count(2 * i + c).loop(r, 4)
                        act.wait_ge(R["mix_sum"], (K + 1).value())
                        copy(flat(mh)[:, bass.ds(K.value() * S, S)], (tmp2, tmp3)[c][:, 0:S]).then_inc(R["mix_hi"], 1)

            def out_and_ffn(t, n, u, feed0, gain, h0, first_block):
                with act.Fori(0, KD // 2) as r:
                    for m in range(2):
                        tt = (t + m).loop(r, 2)
                        act.wait_ge(chunk_done, (tt + 1).value())
                        head(tt + 2)
                    for m in range(2):
                        feed(r * 2 + m, (feed0 + m).loop(r, 2), gain("ffn_g", r, m), (n + m).loop(r, 2))
                t, n = t + T_OUT, n + KD
                act.wait_ge(chunk_done, (t + 1).value())
                root(u, NT, scale=1.0 / D)
                head(t + 2)
                act.wait_ge(chunk_done, (t + 2).value())
                head(t + 3)

                hidden(n, h0, 0, first_block)
                with act.Fori(1, KF) as r:
                    for c in range(2):
                        act.wait_ge(chunk_done, (t + (c + 1)).loop(r, 2).value())
                        head((t + (c + 2)).loop(r, 2))
                    hidden(n.loop(r, 2), h0.loop(r, 1), r, first_block)
                return t + T_UP, n + T_UP

            def hidden(n, k, j, first_block):
                if first_block:
                    act.wait_ge(R["conv_ready"], (k + 1).value())
                else:
                    act.wait_ge(tile_out, (n + 1).value())
                act.activation(tmp[:, 0, :], tmp[:, 0, :], ACT.Silu).then_inc(R["silu_ready"], 1)
                act.wait_ge(R["prod_ready"], (k + 1).value())
                copy(flat(hh)[:, cols(j * S, S)], tmp[:, 1, :]).then_inc(R["h_hi"], 1)

            def down(t, n, feed0, gain):
                with act.Fori(0, KD // 2) as r:
                    for c in range(2 * DOWN_CHUNKS):
                        tt = (t + c).loop(r, 2 * DOWN_CHUNKS)
                        act.wait_ge(chunk_done, (tt + 1).value())
                        head(tt + 2)
                        if c == DOWN_CHUNKS:
                            feed(r * 2, feed0.loop(r, 2), gain("next_g", r, 0), n.loop(r, 2))
                    feed(r * 2 + 1, (feed0 + 1).loop(r, 2), gain("next_g", r, 1), (n + 1).loop(r, 2))

            def gain1(name, r, m):
                return pr1[:, bass.ds(r * 2 + (P1[name] + m), 1)]

            def gain2(name, r, m):
                return par[:, bass.ds(r * 2 + (P2[name] + m), 1)]

            t, n = out_and_ffn(Count(T_IN + T_MIX), Count(N_IN + N_MIX), Count(8), Count(KD), gain1, Count(0), True)
            down(t, n, Count(2 * KD), gain1)

            with act.Fori(0, LAYERS) as l:
                T = Count(T_BLOCK1).loop(l, T_LAYER)
                N = Count(N_BLOCK1).loop(l, N_LAYER)
                U0 = Count(U_BLOCK1).loop(l, U_LAYER)
                L1 = Count(1).loop(l, 1)
                act.wait_ge(R["par_ready"], L1.value())
                SS = Count(4 * NU).loop(l, 32)
                TT = Count(4 * NU).loop(l, 16)
                SC = (POOLB, TR)
                Y = Count(0).loop(l, KD)

                def exps(h, i):
                    n = (i + 1) * P
                    for m in range(2):
                        u = 2 * i + m
                        act.wait_ge(R["max_ready"], (SS + (8 * h + u + 1)).value())
                        act.activation(lp[:, i % 2, m, 0:n], SC[m][:, 0:n], ACT.Exp, bias=negmx2[:, u:u + 1],
                                       accum_out=rows2[:, u:u + 1]).then_inc(R["exp_ready"], 1)

                def put(h, i):
                    act.wait_ge(R["pt_psum"], (TT + (4 * h + i + 1)).value())
                    copy(lpt[:, 0:i + 1, i * P:(i + 1) * P],
                         OUT[:, 0:(i + 1) * P].rearrange("p (c q) -> p c q", q=P)).then_inc(R["pt_ready"], 1)

                def y_head(name, src):
                    copy(yh[:, Y_ORDER.index(name), :], src).then_inc(R["y_hi"], 1)

                def head_step(h, step):
                    if 2 <= step < 6:
                        put(h, step - 2)
                    if step < 4:
                        exps(h, step)
                    if step == 6:
                        act.wait_ge(R["o_psum"], Count(5 + h).loop(l, 4).value())
                        copy(lo_[:, h % 2, :], OUT[:, :]).then_inc(R["o_hi"], 1)
                        act.activation(sq[:, 0, :], OUT[:, :], ACT.Square).then_inc(sq_ready, 1)
                    if step == 7:
                        root(U0 + (1 + h), NT, scale=1.0 / P)
                    if step == 9:
                        act.wait_ge(R["head_normed"], Count(h + 1).loop(l, 4).value())
                        y_head(f"head{h}", lo_[:, h % 2, :])

                for n in range(T_LIN):
                    for s, steps in layer_slots(n):
                        if n == 1 and s % 2 == 0:
                            act.wait_ge(R["lam_psum"], L1.value())
                            act.activation(lame, POOLB[:, 0:2], ACT.Exp).then_inc(R["lam_exp"], 1)
                        for h, step in steps:
                            head_step(h, step)
                        if HEAD0 <= n < 17 and (n - HEAD0) % 3 == 0 and s % 2 == 0:
                            h = (n - HEAD0) // 3
                            act.wait_ge(tr_ready, Count(4 + h).loop(l, 4).value())
                            copy(lv[:, h, :, :].rearrange("p c d -> p (c d)"), ROT[:, :]).then_inc(tr_read, 1)
                        if s == 24:
                            act.wait_ge(R["ya_ready"], Count(1).loop(l, 2).value())
                            y_head("ya0", ya[:, 0, :])
                        if s == 26:
                            root(U0 + 5, NT, scale=1.0 / 256, plain=True)
                        if s == 28:
                            act.wait_ge(R["ln_sub"], L1.value())
                            act.activation(sq[:, :, :], conv[:, :, :], ACT.Square).then_inc(R["ln_sq"], 1)
                            root(U0 + 6, NT, scale=1.0 / 256, eps=LN_EPS)
                    act.wait_ge(chunk_done, (T + (n + 1)).value())
                    if n == 0:
                        root(U0, NT, scale=1.0 / D)
                    head(T + (n + 2))
                    if n in (2, 3):
                        act.wait_ge(tile_out, (N + (n + 1)).value())
                        act.activation(cg[:, n - 2, :], cg[:, n - 2, :], ACT.Sigmoid, bias=c2("glu_b", n))\
                            .then_inc(R["glu_sig"], 1)
                act.wait_ge(R["ya_ready"], Count(2).loop(l, 2).value())
                y_head("ya1", ya[:, 1, :])
                for c in range(2):
                    act.wait_ge(R["ln_scaled"], Count(c + 1).loop(l, 2).value())
                    act.activation(conv[:, c, :], conv[:, c, :], ACT.Silu, bias=c2("ln_b", c)).then_inc(R["yc_ready"], 1)
                    act.wait_ge(R["yc_ready"], Count(c + 1).loop(l, 2).value())
                    y_head(f"conv{c}", conv[:, c, :])
                t, n = out_and_ffn(T + T_LIN, N + T_LIN, U0 + 7, Count(3 * KD).loop(l, 2 * KD), gain2,
                                   Count(KF).loop(l, KF), False)
                down(t, n, Count(4 * KD).loop(l, 2 * KD), gain2)
            root(Count(U_BLOCK1 + LAYERS * U_LAYER), NT, scale=1.0 / D)

        @block.vector
        def _(dve):
            tt, ts, stt = dve.tensor_tensor, dve.tensor_scalar, dve.scalar_tensor_tensor

            def fma(o, a, s, b):
                return stt(out=o, in0=a, scalar=s, in1=b, op0=ALU.mult, op1=ALU.add)

            def mul3(o, a, s, b):
                return stt(out=o, in0=a, scalar=s, in1=b, op0=ALU.mult, op1=ALU.mult)

            flat = lambda a: a[:, :, :].rearrange("p k n -> p (k n)")

            def tile_of(a, m):
                return a[:, m, :] if isinstance(m, int) else flat(a)[:, bass.ds(m * S, S)]

            def feed(m, k, g):
                dve.wait_ge(xh_ready, (k + 1).value())
                stt(out=tile_of(xl, m), in0=tile_of(xs, m), scalar=g, in1=tile_of(xh, m).bitcast(F32),
                    op0=ALU.mult, op1=ALU.subtract)
                tt(sqacc[:, :], sqacc[:, :], sq[:, k.even(), :], ALU.add).then_inc(xl_ready, 1)

            def recips(u, n, parts=P, plain=False):
                dve.wait_ge(root_ready, (u + 1).value())
                o, i = s_recip[0:parts, 0:n], s_root[0:parts, 0:n]
                (dve.tensor_copy(o, i) if plain else dve.reciprocal(o, i)).then_inc(recip_ready, 1)

            def pair_recips(u, n, parts=P):
                dve.wait_ge(root_ready, (u + 1).value())
                dve.reciprocal(s_recip[0:parts, 0:n], s_root[0:parts, 0:n])
                dve.drain()
                dve.tensor_copy(pairs[0:parts, 0:64 * n].rearrange("p (u d) -> p u d", d=64),
                                s_recip[0:parts, 0:n].unsqueeze(2).to_broadcast([parts, n, 64])).then_inc(recip_ready, 1)

            def x_norm(u):
                recips(u, NT)
                dve.wait_ge(bc_ready, (u + 1).value())
                dve.tensor_copy(rstd[:, :], BC[:, :]).then_inc(bc_read, 1)
                dve.memset(sqacc[:, :], 0.0)
                dve.drain()

            def take(t, n, o, scale=None):
                dve.wait_ge(chunk_done, (t + 1).value())
                b = G[n.even()]
                if scale is None:
                    return tt(o, b[:, :], rstd[:, :], ALU.mult).then_inc(tile_out, 1)
                return mul3(o, b[:, :], scale, rstd[:, :]).then_inc(tile_out, 1)

            def tables(src, pf, an, tu, rd, inv, first):
                two_pi = 2.0 * np.pi
                c1_ = 6.28125
                c2_ = float(np.float32(np.round((two_pi - c1_) * 2 ** 18) / 2 ** 18))
                c3_ = float(two_pi - c1_ - c2_)
                magic = 1.5 * 2 ** 23
                lim = 3.1415925
                for c in range(2):
                    if c == 0:
                        dve.tensor_copy(pf[:, :], src[:, :])
                        dve.drain()
                        ts(an[:, :], pf[:, :], inv, None, ALU.mult)
                    else:
                        yield
                    dve.drain()
                    ts(tu[:, :], an[:, :], 1.0 / two_pi, 0.25 * c, ALU.mult, ALU.add)
                    dve.drain()
                    ts(tu[:, :], tu[:, :], magic, magic, ALU.add, ALU.subtract)
                    if c:
                        dve.wait_ge(sine_done, first + 1)
                    dve.drain()
                    fma(rd[:, :], tu[:, :], -c1_, an[:, :])
                    dve.drain()
                    fma(rd[:, :], tu[:, :], -c2_, rd[:, :])
                    dve.drain()
                    fma(rd[:, :], tu[:, :], -c3_, rd[:, :])
                    dve.drain()
                    ts(rd[:, :], rd[:, :], float(np.pi / 2) * c, lim, ALU.add, ALU.min)
                    dve.drain()
                    ts(rd[:, :], rd[:, :], -lim, None, ALU.max).then_inc(R["tables"], 1)
                yield

            dve.memset(small[:, :], 0.0)
            dve.memset(small2[:, :], 0.0)
            dve.memset(sqacc[:, :], 0.0)
            dve.drain()
            dve.memset(small[:, 188:189], EPS)
            dve.memset(small[:, 189:190], LN_EPS)
            dve.drain()
            dve.memset(tmp2[:, :], 0.0).then_inc(R["zeroed"], 1)
            dve.wait_ge(gains_landed, 16)
            for m in range(KD):
                if m % (KD // 2) == 0:
                    dve.wait_ge(x_landed[m // (KD // 2)], 16)
                dve.drain()
                feed(m, Count(m), c1("mix_g", m))
            ts(q_g8, c1("q_g"), 0.125, None, ALU.mult)
            x_norm(Count(0))
            dve.wait_ge(par_landed, 32)
            tables1 = tables(posi, posf, ang, turns, red, cst[:, C["inv1"]:C["inv1"] + 1], 0)
            tables2 = tables(posi2, posf2, ang2, turns2, red2, cst[:, C["inv2"]:C["inv2"] + 1], 2)

            def normed(n, gain):
                i = n - 2
                dve.wait_ge(bc_ready, n)
                mul3(tmp[:, i % 2, :], ybuf[:, n % 2, :], gain, BC[:, :]).then_inc(bc_read, 1)
                dve.drain()
                tt(tmp3[:, 0:S], tmp[:, i % 2, :], cos[:, :], ALU.mult).then_inc(rot_in, 1)

            def rotated(i, dst):
                dve.wait_ge(rot_ready, i + 1)
                tt(tmp2[:, 0:S], ROT[:, :], sin[:, :], ALU.mult).then_inc(rot_read, 1)
                dve.drain()
                tt(dst, tmp2[:, 0:S], tmp3[:, 0:S], ALU.add)

            dsts = [kk[:, 0, :], kk[:, 1, :]] + [qall[:, c, :] for c in range(4)]
            gains = [c1("sel_g"), c1("win_g")] + [q_g8] * 4

            def pooled(i):
                g = 3 - i
                w = 2 << g
                y = ybuf[:, (8 + i) % 2, :]
                dve.memset(tmp2[:, 0:16], 0.0)
                dve.memset(tmp3[:, 0:16], 0.0)
                dve.tensor_copy(tmp2[:, 16:528], y)
                a, b, w_ = tmp2, tmp3, 1
                while w_ < w:
                    dve.drain()
                    tt(b[:, 16:528], a[:, 16:528], a[:, 16 - w_:528 - w_], ALU.add)
                    a, b, w_ = b, a, 2 * w_
                dve.drain()
                if i >= 2:
                    dve.wait_ge(R["pool_psum"], i - 1)
                stt(out=tmp[:, i % 2, :], in0=a[:, 16:528], scalar=1.0 / w, in1=y, op0=ALU.mult, op1=ALU.subtract)
                tt(small2[:, 480:496], a[:, 16:32], cst[:, C["rcount"] + 16 * g:C["rcount"] + 16 * g + 16], ALU.mult)
                dve.drain()
                tt(tmp[:, i % 2, 0:16], small2[:, 480:496], y[:, 0:16], ALU.subtract).then_inc(R["pool_in"], 1)

            def pool_rest(i):
                g = 3 - i
                dve.wait_ge(R["pool_hi"], i + 1)
                stt(out=pol[:, g, :], in0=POOLB[:, :], scalar=c1("pool_scale", g), in1=poh[:, g, :].bitcast(F32),
                    op0=ALU.mult, op1=ALU.subtract).then_inc(R["pool_lo"], 1)

            def blocks(c, pe_name):
                e = pr1[:, P1[pe_name]:P1[pe_name] + 16].unsqueeze(2).to_broadcast([P, 16, N_CMP])
                for g in range(2):
                    x_ = tt(blk[c][:, :, g, :], shifted[:, c, g, :].rearrange("p (b l) -> p l b", l=16), e, ALU.add)
                x_.then_inc(R["blk_ready"], 1)

            def key_norm():
                dve.wait_ge(bc_ready, 8)
                mul3(cyn[:, 0:32], kcf, c1("cmp_g"), BC[:, 0:32]).then_inc(bc_read, 1)
                dve.drain()
                tt(ctm[:, 0:31], cyn[:, 0:31], ends(cos), ALU.mult).then_inc(rot_in, 1)

            def ends(a):
                return a[:, 16:S].rearrange("p (b l) -> p b l", l=16)[:, :, 15]

            def key_end():
                dve.wait_ge(rot_ready, 7)
                tt(csq[:, 0:31], ROT[:, 0:31], ends(sin), ALU.mult)
                dve.drain()
                tt(kct[:, 0:31], csq[:, 0:31], ctm[:, 0:31], ALU.add).then_inc(rot_read, 1)

            def copy_cmp(c):
                dve.wait_ge(R["cmp_psum"], c + 1)
                for g in range(2):
                    x_ = dve.tensor_copy((kcf, vcf)[c][g * 64:(g + 1) * 64, 0:31],
                                         STAT[g * 64:(g + 1) * 64, g * 31:g * 31 + 31])
                x_.then_inc(R["cmp_copied"], 1)

            for n in range(N_IN):
                if 2 <= n - 1 < 8:
                    pair_recips(Count(n - 2), 8)
                take(Count(n), Count(n), kvraw[:, n, :] if n < 2 else ybuf[:, n % 2, :])
                if 2 <= n - 2 < 8:
                    rotated(n - 4, dsts[n - 4])
                if 2 <= n - 1 < 8:
                    normed(n - 1, gains[n - 3])
                if n < 2:
                    next(tables1)
                if n == 2:
                    dve.wait_ge(sine_done, 2)
                if n in (4, 6):
                    dve.wait_ge(shift_landed, 8 * 16)
                    blocks(n // 2 - 2, ("pe_k", "pe_v")[n // 2 - 2])
                if n in (10, 11):
                    copy_cmp(n - 10)
                if n == 12:
                    pair_recips(Count(7), 2, parts=32)
                if n == 13:
                    key_norm()
                if 9 <= n < 13:
                    dve.drain()
                    pooled(n - 9)
                    dve.drain()
                if 11 <= n:
                    pool_rest(n - 11)
            key_end()
            dve.tensor_copy(qcurs[0][:, :], qall[:, 0, :]).then_inc(R["q_cur"], 1)
            dve.wait_ge(late_landed, 16 * 7)
            next(tables2)
            next(tables2)
            dve.wait_ge(sine_done, 4)
            dve.drain()

            SB = [ROT, POOLB]

            def gated(t, m, n, sig, half, o):
                dve.wait_ge(R["mix_sig"], (sig + (m + 1)).value())
                if m:
                    dve.wait_ge(chunk_done, (t + 3).value())
                else:
                    dve.wait_ge(half_done, (half + 1).value())
                return tt(o, ybuf[:, m, :], G[n.even()][:, :], ALU.mult).then_inc(tile_out, 1)

            def attention(trip, j, odd):
                U, J = trip(0, NU), trip(0, 1)
                t, n = trip(T_IN, 3), trip(N_IN, 4)

                def pool_gated(m):
                    gated(t, m, n + (2 + m), trip(0, 2), J, flat(pm)[:, bass.ds(j * (2 * S) + m * S, S)])

                def compressed():
                    dve.wait_ge(R["c_psum"], (J + 1).value())
                    sc = [b[:, 0:P].rearrange("p (u n) -> p u n", n=32) for b in (TR, BC)]
                    for g in range(2):
                        dve.tensor_reduce(mx8[:, 4 * g:4 * g + 4], sc[g], AX.X, ALU.max)
                    dve.drain()
                    ts(mx8, mx8, MASKED / 1e5, None, ALU.max)
                    dve.drain()
                    for g in range(2):
                        x_ = tt(cmp_p[:, 4 * g:4 * g + 4, :], sc[g],
                                mx8[:, 4 * g:4 * g + 4].unsqueeze(2).to_broadcast([P, 4, 32]), ALU.subtract)
                    x_.then_inc(R["c_sub"], 1)

                def top(u):
                    dve.wait_ge(R["s_psum"], (U + (u + 1)).value())
                    dve.tensor_reduce(negmx[:, u:u + 1], SB[u % 2][:, 0:(u % 4 + 1) * P], AX.X, ALU.max, negate=True)\
                        .then_inc(R["max_ready"], 1)

                def scale(u):
                    g, b, i = u // 8, u // 4 % 2, u % 4
                    n = (i + 1) * P
                    dve.wait_ge(R["exp_ready"], (U + (u + 1)).value())
                    dve.reciprocal(rinv[:, u:u + 1], rows[:, u:u + 1])
                    dve.drain()
                    ts(probs[:, u % 4, 0:n], probs[:, u % 4, 0:n], rinv[:, u:u + 1],
                       small2[:, bass.ds(j * 6 + (24 * i + 3 * g + 1 + b), 1)], ALU.mult, ALU.mult)\
                        .then_inc(R["p_ready"], 1)

                for u in range(NU + 1):
                    if u < NU:
                        top(u)
                    if u == 0:
                        compressed()
                    if u >= 1:
                        scale(u - 1)
                    if u == 13:
                        dve.tensor_copy(qcurs[1 - odd][:, :], flat(qall)[:, bass.ds(((j + 1) % 4) * S, S)])\
                            .then_inc(R["q_cur"], 1)
                    if u == 6:
                        take(t, n, ybuf[:, 0, :])
                    if u == 12:
                        take(t + 1, n + 1, ybuf[:, 1, :])
                    if u == 15:
                        pool_gated(0)
                    if u == 2:
                        dve.wait_ge(R["c_exp"], (J + 1).value())
                        dve.tensor_reduce(sum8, cmp_p[:, :, :], AX.X, ALU.add)
                        dve.drain()
                        ts(sum8, sum8, 1e-30, None, ALU.max)
                        dve.drain()
                        dve.reciprocal(fac8, sum8)
                        dve.drain()
                        for g in range(2):
                            for i in range(NT):
                                x_ = ts(cmp_p[:, g * NT + i, :], cmp_p[:, g * NT + i, :],
                                   fac8[:, g * NT + i:g * NT + i + 1],
                                   small2[:, bass.ds(j * 6 + (24 * i + 3 * g), 1)], ALU.mult, ALU.mult)
                        x_.then_inc(R["c_probs"], 1)
                dve.wait_ge(R["o_hi"], (J + 1).value())
                tt(flat(nl)[:, bass.ds(j * S, S)], OUT[:, :], flat(nh)[:, bass.ds(j * S, S)].bitcast(F32),
                   ALU.subtract).then_inc(R["o_lo"], 1)
                pool_gated(1)

            with dve.Fori(0, 2) as r:
                for i in range(2):
                    attention(lambda const, step: Count(const + i * step).loop(r, 2 * step), r * 2 + i, i)

            with dve.Fori(0, 2) as r:
                for i in range(2):
                    t, n = Count(T_IN + 12 + 3 * i).loop(r, 6), Count(N_IN + 16 + 4 * i).loop(r, 8)
                    for c in range(2):
                        take(t + c, n + c, ybuf[:, c, :])
                    for c in range(2):
                        gated(t, c, n + (2 + c), Count(8 + 2 * i).loop(r, 4), Count(4 + i).loop(r, 2), tmp[:, c, :])
                        dve.drain()
                        tt((tmp2, tmp3)[c][:, 0:S], tmp[:, c, :], flat(pm)[:, bass.ds(r * (4 * S) + (2 * i + c) * S, S)],
                           ALU.add).then_inc(R["mix_sum"], 1)
                    for c in range(2):
                        K = Count(2 * i + c).loop(r, 4)
                        dve.wait_ge(R["mix_hi"], (K + 1).value())
                        tt(flat(ml)[:, bass.ds(K.value() * S, S)], (tmp2, tmp3)[c][:, 0:S],
                           flat(mh)[:, bass.ds(K.value() * S, S)].bitcast(F32), ALU.subtract).then_inc(R["mix_lo"], 1)

            def add_to_x(t, n, m):
                dve.wait_ge(chunk_done, (t + 1).value())
                tt(tile_of(xs, m), tile_of(xs, m), G[n.even()][:, :], ALU.add).then_inc(tile_out, 1)

            def out_and_ffn(t, n, u, feed0, gain, h0, first_block):
                with dve.Fori(0, KD // 2) as r:
                    for m in range(2):
                        add_to_x((t + m).loop(r, 2), (n + m).loop(r, 2), r * 2 + m)
                    for m in range(2):
                        dve.drain()
                        feed(r * 2 + m, (feed0 + m).loop(r, 2), gain("ffn_g", r, m))
                t, n = t + T_OUT, n + KD
                x_norm(u)
                hidden(t, n, h0, 0, first_block)
                with dve.Fori(1, KF) as r:
                    hidden(t.loop(r, 2), n.loop(r, 2), h0.loop(r, 1), r, first_block)
                return t + T_UP, n + T_UP

            def hidden(t, n, k, j, first_block):
                if first_block:
                    take(t, n, tmp2[:, 2:2 + S])
                    w = (lambda c: pr1[:, P1["conv_w"] + c:P1["conv_w"] + c + 1]) if isinstance(j, int) else \
                        (lambda c: pr1[:, bass.ds(j * 3 + (P1["conv_w"] + c), 1)])
                    b = c1("conv_b") if isinstance(j, int) else pr1[:, bass.ds(j + P1["conv_b"], 1)]
                    if isinstance(j, int):
                        dve.memset(tmp2[:, 0:2], 0.0)
                    dve.drain()
                    ts(tmp3[:, 0:S], tmp2[:, 2:2 + S], w(2), b, ALU.mult, ALU.add)
                    dve.drain()
                    fma(tmp3[:, 0:S], tmp2[:, 1:1 + S], w(1), tmp3[:, 0:S])
                    dve.drain()
                    fma(tmp[:, 0, :], tmp2[:, 0:S], w(0), tmp3[:, 0:S]).then_inc(R["conv_ready"], 1)
                else:
                    take(t, n, tmp[:, 0, :])
                take(t + 1, n + 1, ybuf[:, 0, :])
                dve.drain()
                dve.wait_ge(R["silu_ready"], (k + 1).value())
                tt(tmp[:, 1, :], tmp[:, 0, :], ybuf[:, 0, :], ALU.mult).then_inc(R["prod_ready"], 1)
                dve.wait_ge(R["h_hi"], (k + 1).value())
                tt(flat(hl)[:, cols(j * S, S)], tmp[:, 1, :], flat(hh)[:, cols(j * S, S)].bitcast(F32),
                   ALU.subtract).then_inc(R["h_lo"], 1)

            def down(t, n, feed0, gain):
                with dve.Fori(0, KD // 2) as r:
                    for m in range(2):
                        add_to_x((t + (DOWN_CHUNKS * (m + 1) - 1)).loop(r, 2 * DOWN_CHUNKS), (n + m).loop(r, 2), r * 2 + m)
                        dve.drain()
                        feed(r * 2 + m, (feed0 + m).loop(r, 2), gain("next_g", r, m))
                dve.drain()

            def gain1(name, r, m):
                return pr1[:, bass.ds(r * 2 + (P1[name] + m), 1)]

            def gain2(name, r, m):
                return par[:, bass.ds(r * 2 + (P2[name] + m), 1)]

            t, n = out_and_ffn(Count(T_IN + T_MIX), Count(N_IN + N_MIX), Count(8), Count(KD), gain1, Count(0), True)
            down(t, n, Count(2 * KD), gain1)

            with dve.Fori(0, LAYERS) as l:
                T = Count(T_BLOCK1).loop(l, T_LAYER)
                N = Count(N_BLOCK1).loop(l, N_LAYER)
                U0 = Count(U_BLOCK1).loop(l, U_LAYER)
                L1 = Count(1).loop(l, 1)
                dve.tensor_copy(par[:, :], pr2[:, bass.ds(l * NP2, NP2)]).then_inc(R["par_ready"], 1)
                dve.memset(cpad[:, :, 0:TAPS - 1], 0.0)
                dve.memset(acp[:, 0:2], 0.0)
                dve.drain()
                for c in range(2):
                    x_ = tt(lamp[:, c:c + 1], c2("lam", 2 * c), c2("lam", 2 * c + 1), ALU.mult)
                x_.then_inc(R["lam_in"], 1)
                ts(sub_gain, c2("sub_g"), c2("lam_init", 1), None, ALU.mult)
                x_norm(U0)
                dve.wait_ge(R["lam_exp"], L1.value())
                tt(neglam, lame[:, 1:2], lame[:, 0:1], ALU.subtract)
                dve.drain()
                tt(neglam, neglam, c2("lam_init", 0), ALU.subtract)

                SS = Count(4 * NU).loop(l, 32)
                SC = (POOLB, TR)

                def rot_end(i):
                    dve.wait_ge(rot_ready, Count(8 + i).loop(l, 8).value())
                    tt(tmp2[:, 0:S], ROT[:, :], sin2[:, :], ALU.mult).then_inc(rot_read, 1)
                    dve.drain()
                    tt((lq, lk)[i % 2][:, i // 2 % 2, :], tmp2[:, 0:S], tmp3[:, 0:S], ALU.add)\
                        .then_inc(R["qk_ready"], 1)

                tap = [0]

                def taps(n):
                    for k in range(tap[0], min(tap[0] + n, TAPS)):
                        dve.drain()
                        for c in range(2):
                            w = c2("dw_w", c * TAPS + k)
                            if k == 0:
                                ts(conv[:, c, :], cpad[:, c, 0:S], w, c2("dw_b", c), ALU.mult, ALU.add)
                            else:
                                x_ = fma(conv[:, c, :], cpad[:, c, k:k + S], w, conv[:, c, :])
                        if k == TAPS - 1:
                            x_.then_inc(R["conv_done"], 1)
                    tap[0] += n

                def glu(c):
                    dve.wait_ge(R["glu_sig"], Count(c + 1).loop(l, 2).value())
                    stt(out=cpad[:, c, TAPS - 1:TAPS - 1 + S], in0=ca[:, c, :], scalar=c2("glu_b", c),
                        in1=cg[:, c, :], op0=ALU.add, op1=ALU.mult)

                def peak(h, i):
                    for m in range(2):
                        u = 2 * i + m
                        dve.wait_ge(R["s_psum"], (SS + (8 * h + u + 1)).value())
                        dve.tensor_reduce(negmx2[:, u:u + 1], SC[m][:, 0:(i + 1) * P], AX.X, ALU.max,
                                          negate=True).then_inc(R["max_ready"], 1)

                def combine(h, i):
                    n = (i + 1) * P
                    dve.wait_ge(R["exp_ready"], (SS + (8 * h + 2 * i + 2)).value())
                    dve.reciprocal(rinv2[:, 2 * i:2 * i + 2], rows2[:, 2 * i:2 * i + 2])
                    dve.drain()
                    ts(lp[:, i % 2, 1, 0:n], lp[:, i % 2, 1, 0:n], rinv2[:, 2 * i + 1:2 * i + 2], neglam,
                       ALU.mult, ALU.mult)
                    dve.drain()
                    fma(lp[:, i % 2, 0, 0:n], lp[:, i % 2, 0, 0:n], rinv2[:, 2 * i:2 * i + 1],
                        lp[:, i % 2, 1, 0:n]).then_inc(R["p_ready"], 1)

                def y_rest(name, src):
                    k = Y_ORDER.index(name)
                    dve.wait_ge(R["y_hi"], Count(k + 1).loop(l, KD).value())
                    tt(yl[:, k, :], src, yh[:, k, :].bitcast(F32), ALU.subtract).then_inc(R["y_lo"], 1)

                def head_step(h, step):
                    if 1 <= step < 5:
                        combine(h, step - 1)
                    if step < 4:
                        peak(h, step)
                    if step == 7:
                        recips(U0 + (1 + h), NT)
                    if step == 9:
                        dve.wait_ge(bc_ready, (U0 + (2 + h)).value())
                        mul3(lo_[:, h % 2, :], lo_[:, h % 2, :], sub_gain, BC[:, :]).then_inc(bc_read, 1)
                        dve.drain()
                        dve.sem_inc(R["head_normed"], 1)
                    if step == 10:
                        y_rest(f"head{h}", lo_[:, h % 2, :])

                TAP_PLAN = {4: (2, 1), 5: (1, 1), 6: (2, 1), 19: (2, 2)}
                for n in range(T_LIN):
                    for half, (s, steps) in enumerate(layer_slots(n)):
                        if half == 1 and 5 <= n < 16 and (n - 5) % 3 < 2:
                            rot_end(2 * ((n - 5) // 3) + (n - 5) % 3)
                        for h, step in steps:
                            head_step(h, step)
                        if n >= 4:
                            taps(TAP_PLAN.get(n, (1, 1))[half])
                        if s == 24:
                            y_rest("ya0", ya[:, 0, :])
                        if s == 26:
                            recips(U0 + 5, NT, plain=True)
                        if s == 27:
                            dve.wait_ge(bc_ready, (U0 + 6).value())
                            for c in range(2):
                                x_ = tt(conv[:, c, :], conv[:, c, :], BC[:, :], ALU.subtract)
                            x_.then_inc(bc_read, 1)
                            dve.drain()
                            dve.sem_inc(R["ln_sub"], 1)
                        if s == 28:
                            recips(U0 + 6, NT)
                    tl, nl_ = T + n, N + n
                    if n < 2:
                        take(tl, nl_, ca[:, n, :])
                    elif n < 4:
                        take(tl, nl_, cg[:, n - 2, :])
                        glu(n - 2)
                    elif n < 16:
                        what = (n - 4) % 3
                        take(tl, nl_, ybuf[:, n % 2, :], scale=0.125 if what == 0 else None)
                        if what < 2:
                            dve.drain()
                            tt(tmp3[:, 0:S], ybuf[:, n % 2, :], cos2[:, :], ALU.mult)
                    else:
                        c, what = (n - 16) // 3, (n - 16) % 3
                        if what == 0:
                            take(tl, nl_, tmp3[:, 0:S])
                        elif what == 1:
                            take(tl, nl_, tmp2[:, 0:S])
                            dve.drain()
                            tt(acp[:, 2:2 + S], tmp3[:, 0:S], tmp2[:, 0:S], ALU.mult)
                            dve.drain()
                            ts(ya[:, c, :], acp[:, 2:2 + S], c2("short_w", 3 * c + 2), None, ALU.mult)
                            dve.drain()
                            fma(ya[:, c, :], acp[:, 1:1 + S], c2("short_w", 3 * c + 1), ya[:, c, :])
                            dve.drain()
                            fma(ya[:, c, :], acp[:, 0:S], c2("short_w", 3 * c), ya[:, c, :])
                        else:
                            take(tl, nl_, tmp3[:, 0:S])
                            dve.drain()
                            tt(ya[:, c, :], ya[:, c, :], tmp3[:, 0:S], ALU.mult).then_inc(R["ya_ready"], 1)
                assert tap[0] >= TAPS
                dve.wait_ge(bc_ready, (U0 + 7).value())
                for c in range(2):
                    x_ = mul3(conv[:, c, :], conv[:, c, :], c2("ln_g", c), BC[:, :]).then_inc(R["ln_scaled"], 1)
                dve.drain()
                dve.sem_inc(bc_read, 1)
                y_rest("ya1", ya[:, 1, :])
                for c in range(2):
                    y_rest(f"conv{c}", conv[:, c, :])
                t, n = out_and_ffn(T + T_LIN, N + T_LIN, U0 + 7, Count(3 * KD).loop(l, 2 * KD), gain2,
                                   Count(KF).loop(l, KF), False)
                down(t, n, Count(4 * KD).loop(l, 2 * KD), gain2)

            x_norm(Count(U_BLOCK1 + LAYERS * U_LAYER))
            for m in range(KD):
                mul3(xs[:, m, :], xs[:, m, :], c2("next_g", m), rstd[:, :]).then_inc(R["out_ready"], 1)


def kernel(**inputs):
    import ml_dtypes
    import concourse.bacc as bacc
    from concourse.bass_utils import run_bass_kernel_spmd

    g = {k: np.ascontiguousarray(v) for k, v in inputs.items()}

    def blocks(w):
        k, m = w.shape
        return w.reshape(k // P, P, m // P, P).transpose(2, 0, 1, 3)

    def chunks(b):
        m, k = b.shape[:2]
        n = -(-k // CB)
        full = np.zeros((m, n * CB, P, P), np.float32)
        full[:, :k] = b
        return full.reshape(m * n, CB, P, P).transpose(0, 2, 1, 3).reshape(m * n, P, CB * P)

    def columns(v):
        return v.reshape(-1, P).T

    def pair(v):
        return np.concatenate([v, v])[:, None]

    w_in = g["w_in"][0]
    kv = w_in[:, 1024:1792].reshape(D, 6, P)
    q = w_in[:, 512:1024].reshape(D, 2, 4, 64).transpose(0, 2, 1, 3).reshape(D, 4, P)
    gates = np.zeros((D, P), np.float32)
    gates[:, :24] = w_in[:, 1792:1816].reshape(D, 2, 4, 3).transpose(0, 2, 1, 3).reshape(D, 24)
    tiles = [kv[:, i] for i in (0, 1, 2, 4)] + [q[:, j] for j in range(4)]
    tiles += [w_in[:, g * P:(g + 1) * P] for g in (3, 2, 1, 0)] + [kv[:, 3], kv[:, 5], gates]
    stream = [chunks(blocks(np.concatenate(tiles, 1)))]
    merge = blocks(w_in[:, 1816:])
    nsa_rows = g["w_nsa_out"][0].reshape(2, 4, 64, D).transpose(1, 0, 2, 3).reshape(512, D)
    for gate, outputs in ((merge[:KD], blocks(g["w_pool_out"][0])), (merge[KD:], blocks(nsa_rows))):
        pairs = [gate.reshape(KD // 2, 2, CB, P, P), outputs.reshape(KD // 2, 1, CB, P, P)]
        stream.append(chunks(np.concatenate(pairs, 1).reshape(3 * KD // 2, CB, P, P)))

    def ffn(gate, value, down):
        up = np.stack([blocks(gate), blocks(value)], 1).reshape(2 * KF, KD, P, P)
        return [chunks(up), chunks(blocks(down))]

    stream.append(chunks(blocks(g["w_out"][0])))
    stream += ffn(g["w_up"][0][:, :FF], g["w_up"][0][:, FF:], g["w_down"][0])
    y_rows = [("ya0", "ya1", "head0", "head1", "head2", "head3", "conv0", "conv1").index(y) for y in Y_ORDER]
    for l in range(LAYERS):
        w = g["w_in_2"][l]
        a_b, a_c, a_x = w[:, 0:256], w[:, 256:512], w[:, 512:768]
        ql, kl = (w[:, o:o + 512].reshape(D, 2, 4, 64).transpose(0, 2, 1, 3).reshape(D, 4, P) for o in (768, 1280))
        parts = [w[:, 2304:2816]]
        for h in range(4):
            parts += [ql[:, h], kl[:, h], w[:, 1792 + h * P:1920 + h * P]]
        for c in range(2):
            parts += [a[:, c * P:(c + 1) * P] for a in (a_c, a_x, a_b)]
        stream.append(chunks(blocks(np.concatenate(parts, 1))))
        stream.append(chunks(blocks(g["w_out_2"][l].reshape(KD, P, D)[y_rows].reshape(D, D))))
        stream += ffn(g["w_gate_2"][l], g["w_up_2"][l], g["w_down_2"][l])
    weights = np.concatenate(stream)
    assert len(weights) == T_ALL

    par1 = np.zeros((P, NP1), np.float32)

    def put1(name, v):
        par1[:, P1[name]:P1[name] + v.shape[1]] = v

    put1("mix_g", columns(g["mix_norm_g"][0]))
    put1("q_g", pair(g["q_norm_g"][0]))
    for i, name in enumerate(("cmp_g", "sel_g", "win_g")):
        put1(name, pair(g["k_norm_g"][0, i]))
    put1("pool_scale", columns(g["pool_scale"][0]))
    put1("ffn_g", columns(g["ffn_norm_g"][0]))
    put1("conv_w", g["conv_w"][0].reshape(3, KF, P).transpose(2, 1, 0).reshape(P, 3 * KF))
    put1("conv_b", columns(g["conv_b"][0]))
    put1("next_g", columns(g["mix_norm_g_2"][0]))
    for i, name in enumerate(("pe_k", "pe_v")):
        put1(name, g["cmp_pe"][0, i].reshape(2, 16, 64).transpose(0, 2, 1).reshape(P, 16))

    par2 = np.zeros((P, LAYERS * NP2), np.float32)
    for l in range(LAYERS):
        def put2(name, v, at=0):
            o = l * NP2 + P2[name] + at
            par2[:v.shape[0], o:o + v.shape[1]] = v

        put2("short_w", g["short_conv_w_2"][l].reshape(3, 2, P).transpose(2, 1, 0).reshape(P, 6))
        put2("glu_b", columns(g["glu_b_2"][l]))
        put2("dw_w", g["conf_dw_w_2"][l].reshape(TAPS, 2, P).transpose(2, 1, 0).reshape(P, 2 * TAPS))
        put2("dw_b", columns(g["conf_dw_b_2"][l]))
        put2("ln_g", columns(g["conf_ln_g_2"][l]))
        put2("ln_b", columns(g["conf_ln_b_2"][l]))
        put2("sub_g", columns(g["diff_subln_g_2"][l]))
        put2("ffn_g", columns(g["ffn_norm_g_2"][l]))
        put2("next_g", columns(g["mix_norm_g_2"][l + 1] if l + 1 < LAYERS else g["final_norm_g_2"]))
        for i, name in enumerate(("lam_q1_2", "lam_k1_2", "lam_q2_2", "lam_k2_2")):
            put2("lam", g[name][l][:, None], i)
        init = 0.8 - 0.6 * np.exp(-0.3 * l)
        put2("lam_init", np.tile(np.float32([[init, 1.0 - init]]), (P, 1)))

    consts = np.zeros((P, NC), np.float32)
    consts[:, C["ident"]:C["ident"] + P] = np.eye(P)
    for name, dim, half in (("rot1", 16, 8), ("rot2", 64, 32)):
        for h in (0, 64):
            for i in range(half):
                consts[h + half + i, C[name] + h + i] = -1.0
                consts[h + i, C[name] + h + half + i] = 1.0
    consts[:, C["ones"]:C["ones"] + P] = 1.0
    consts[:64, C["halves"]] = 1.0
    consts[64:, C["halves"] + 1] = 1.0
    p = np.arange(P) % 64
    inv1 = (500000.0 ** (-(np.arange(8) * 2.0 / 16))).astype(np.float32)
    consts[:, C["inv1"]] = np.where(p < 16, inv1[p % 8], 0.0)
    inv2 = np.float32(1) / (np.float32(10000) ** (np.arange(0, 64, 2, dtype=np.float32) / np.float32(64)))
    consts[:, C["inv2"]] = inv2[p % 32]
    for i in range(4):
        consts[:, C["rcount"] + 16 * i:C["rcount"] + 16 * i + 16] = 1.0 / np.minimum(np.arange(16) + 1, 2 << i)
    masks = np.zeros((P, 2 * P + 256), np.float32)
    masks[:, 0:P] = np.eye(P)
    t = np.arange(P)
    masks[:, P:2 * P] = np.where(t[None, :] <= t[:, None], 0.0, MASKED)
    for i in range(NT):
        seen = (16 * np.arange(32) + 31)[None, :] <= (i * P + t)[:, None]
        for u in (i, NT + i):
            masks[:, 2 * P + 32 * u:2 * P + 32 * u + 32] = np.where(seen & (np.arange(32) < N_CMP), 0.0, MASKED)
    masks = masks.astype(ml_dtypes.bfloat16)

    w1 = g["cmp_w1"][0].reshape(2, 2, 16, 64, P).transpose(0, 1, 3, 2, 4).reshape(2, P, 16, P)
    w2 = np.stack([np.concatenate([w, w], 1) for w in g["cmp_w2"][0]], 1)
    pool_w = g["pool_w"][0].transpose(1, 0, 2)
    xt = g["x"][0].T.reshape(KD, P, S).transpose(1, 0, 2)
    arrays = {
        "x": xt, "positions": g["positions"][0], "positions2": g["positions_2"][0], "weights": weights, "par1": par1,
        "par2": par2, "consts": consts, "masks": masks, "w1": w1, "w2": w2, "pool_w": pool_w,
    }
    arrays = {k: np.ascontiguousarray(v) for k, v in arrays.items()}
    nc = bacc.Bacc("TRN2", target_bir_lowering=False, num_devices=1)
    args = [nc.dram_tensor(f"in_{k}", v.shape, mybir.dt.from_np(v.dtype), kind="ExternalInput").ap()
            for k, v in arrays.items()]
    out = nc.dram_tensor("out_t", (KD, P, S), F32, kind="ExternalOutput").ap()
    build(nc, *args, out)
    r = run_bass_kernel_spmd(nc, [{f"in_{k}": v for k, v in arrays.items()}], core_ids=[0])
    return r.results[0]["out_t"].reshape(D, S).T.reshape(1, S, D)
```
